# Optimizing a Trainium2 kernel written in Bass

```python
import math
import jax, jax.numpy as jnp
from jax import lax
import numpy as np
import jax
import jax.numpy as jnp

D_MODEL = 1024
BATCH = 1
SEQ = 256
DEPTH = 2

N_A_LAYERS = DEPTH // 2
N_B_LAYERS = DEPTH - N_A_LAYERS
PLE_DIM = 256
DN_ALPHA = (2.0 * DEPTH) ** 0.25
DN_BETA = (8.0 * DEPTH) ** -0.25
NORM_EPS = 1e-5

ML_HEADS = 8
ML_QK_DIM = D_MODEL // (2 * ML_HEADS)
ML_V_DIM = D_MODEL // ML_HEADS
ML_CHUNK = 64
ML_Q_END = ML_HEADS * ML_QK_DIM
ML_K_END = 2 * ML_HEADS * ML_QK_DIM
ML_V_END = ML_K_END + ML_HEADS * ML_V_DIM
ML_I_END = ML_V_END + ML_HEADS
ML_F_END = ML_I_END + ML_HEADS
ML_IN_COLS = ML_F_END + D_MODEL

MLA_HEADS = 8
MLA_NOPE_DIM = 128
MLA_ROPE_DIM = 64
MLA_V_DIM = 128
MLA_KV_RANK = 256
MLA_Q_RANK = 384
ROPE_THETA = 10000.0
ATTN_BLOCK = 128

PEER_HEADS = 8
PEER_N_KEYS = 128
PEER_N_EXPERTS = PEER_N_KEYS * PEER_N_KEYS
PEER_KEY_DIM = 256
PEER_HALF = PEER_KEY_DIM // 2
PEER_TOPK = 16
PEER_BLOCK = 128


def layer_norm(x, g, b):
    xf = x.astype(jnp.float32)
    mu = jnp.mean(xf, -1, keepdims=True)
    var = jnp.mean(jnp.square(xf - mu), -1, keepdims=True)
    y = (xf - mu) * lax.rsqrt(var + NORM_EPS)
    return (y * g.astype(jnp.float32) + b.astype(jnp.float32)).astype(x.dtype)

def rms_norm(x, g):
    xf = x.astype(jnp.float32)
    y = xf * lax.rsqrt(jnp.mean(jnp.square(xf), -1, keepdims=True) + NORM_EPS)
    return (y * g.astype(jnp.float32)).astype(x.dtype)

def rope_angles(positions, dim):
    inv_freq = ROPE_THETA ** (-jnp.arange(0, dim, 2, dtype=jnp.float32) / dim)
    ang = positions.astype(jnp.float32)[..., None] * inv_freq
    return jnp.cos(ang), jnp.sin(ang)

def apply_rope(x, cos, sin):
    xf = x.astype(jnp.float32)
    x1, x2 = jnp.split(xf, 2, axis=-1)
    return jnp.concatenate([x1 * cos - x2 * sin, x1 * sin + x2 * cos], -1).astype(x.dtype)

def mlstm_chunk_step(carry, inp):
    C, n, m = carry
    q, k, v, ig, lf = inp
    L = q.shape[2]
    b = jnp.cumsum(lf, axis=-1)
    causal = jnp.tril(jnp.ones((L, L), dtype=bool))
    log_w = jnp.where(causal, b[..., :, None] - b[..., None, :] + ig[..., None, :], -jnp.inf)
    log_inter = b + m[..., None]
    m_t = jnp.maximum(log_inter, jnp.max(log_w, -1))
    w = jnp.exp(log_w - m_t[..., None])
    s_inter = jnp.exp(log_inter - m_t)
    qk = jnp.einsum('bhtd,bhsd->bhts', q, k) * w
    num = jnp.einsum('bhts,bhsv->bhtv', qk, v) + s_inter[..., None] * jnp.einsum('bhtd,bhdv->bhtv', q, C)
    den = jnp.sum(qk, -1) + s_inter * jnp.einsum('bhtd,bhd->bht', q, n)
    h = num / jnp.maximum(jnp.abs(den), jnp.exp(-m_t))[..., None]
    b_last = b[..., -1]
    log_src = b_last[..., None] - b + ig
    m_new = jnp.maximum(b_last + m, jnp.max(log_src, -1))
    w_src = jnp.exp(log_src - m_new[..., None])
    s_old = jnp.exp(b_last + m - m_new)
    C_new = s_old[..., None, None] * C + jnp.einsum('bhs,bhsd,bhsv->bhdv', w_src, k, v)
    n_new = s_old[..., None] * n + jnp.einsum('bhs,bhsd->bhd', w_src, k)
    return (C_new, n_new, m_new), h

def mlstm_mixer(x, w_in, b_if, hn_g, w_out):
    B, S, _ = x.shape
    H, L = ML_HEADS, ML_CHUNK
    nc = S // L
    proj = x @ w_in
    q, k, v = proj[..., :ML_Q_END], proj[..., ML_Q_END:ML_K_END], proj[..., ML_K_END:ML_V_END]
    gi, gf, og = proj[..., ML_V_END:ML_I_END], proj[..., ML_I_END:ML_F_END], proj[..., ML_F_END:]

    def to_chunks(t, d):
        return t.reshape(B, nc, L, H, d).transpose(1, 0, 3, 2, 4).astype(jnp.float32)

    def gate_chunks(t):
        return t.reshape(B, nc, L, H).transpose(1, 0, 3, 2)

    qc = to_chunks(q, ML_QK_DIM)
    kc = to_chunks(k, ML_QK_DIM) * (ML_QK_DIM ** -0.5)
    vc = to_chunks(v, ML_V_DIM)
    b_if = b_if.astype(jnp.float32)
    ig = gate_chunks(gi.astype(jnp.float32) + b_if[0])
    lf = gate_chunks(jax.nn.log_sigmoid(gf.astype(jnp.float32) + b_if[1]))
    init = (jnp.zeros((B, H, ML_QK_DIM, ML_V_DIM), jnp.float32),
            jnp.zeros((B, H, ML_QK_DIM), jnp.float32),
            jnp.zeros((B, H), jnp.float32))
    _, h = lax.scan(mlstm_chunk_step, init, (qc, kc, vc, ig, lf))
    h = h.transpose(1, 0, 3, 2, 4).reshape(B, S, H, ML_V_DIM)
    mu = jnp.mean(h, -1, keepdims=True)
    var = jnp.mean(jnp.square(h - mu), -1, keepdims=True)
    hn = (h - mu) * lax.rsqrt(var + NORM_EPS) * hn_g.astype(jnp.float32).reshape(H, ML_V_DIM)
    out = jax.nn.sigmoid(og.astype(jnp.float32)) * hn.reshape(B, S, H * ML_V_DIM)
    return out.astype(x.dtype) @ w_out

def mla_shared_kv(xs, w_down, kv_norm_g, w_up, cos, sin):
    B, S, _ = xs.shape
    ckr = xs @ w_down
    c_kv = rms_norm(ckr[..., :MLA_KV_RANK], kv_norm_g)
    kv = (c_kv @ w_up).reshape(B, S, MLA_HEADS, MLA_NOPE_DIM + MLA_V_DIM)
    k_nope = kv[..., :MLA_NOPE_DIM].transpose(0, 2, 1, 3)
    v = kv[..., MLA_NOPE_DIM:].transpose(0, 2, 1, 3)
    k_rope = apply_rope(ckr[..., MLA_KV_RANK:], cos, sin)
    return k_nope, k_rope, v

def mla_mixer(x, w_dq, q_norm_g, w_uq, w_out, k_nope, k_rope, v, cos, sin):
    B, S, _ = x.shape
    H = MLA_HEADS
    c_q = rms_norm(x @ w_dq, q_norm_g)
    q = (c_q @ w_uq).reshape(B, S, H, MLA_NOPE_DIM + MLA_ROPE_DIM).transpose(0, 2, 1, 3)
    q_nope = q[..., :MLA_NOPE_DIM]
    q_rope = apply_rope(q[..., MLA_NOPE_DIM:], cos[:, None], sin[:, None])
    nb = S // ATTN_BLOCK

    def blocks(t):
        return t.reshape(B, H, nb, ATTN_BLOCK, t.shape[-1]).transpose(2, 0, 1, 3, 4)

    scale = (MLA_NOPE_DIM + MLA_ROPE_DIM) ** -0.5
    key_pos = jnp.arange(S)

    def attend(args):
        idx, qn, qr = args
        s = jnp.einsum('bhqd,bhkd->bhqk', qn, k_nope) + jnp.einsum('bhqd,bkd->bhqk', qr, k_rope)
        s = s.astype(jnp.float32) * scale
        q_pos = idx * ATTN_BLOCK + jnp.arange(ATTN_BLOCK)
        s = jnp.where(key_pos[None, :] <= q_pos[:, None], s, -jnp.inf)
        p = jax.nn.softmax(s, axis=-1).astype(v.dtype)
        return jnp.einsum('bhqk,bhkd->bhqd', p, v)

    o = lax.map(attend, (jnp.arange(nb), blocks(q_nope), blocks(q_rope)))
    o = o.transpose(1, 0, 3, 2, 4).reshape(B, S, H * MLA_V_DIM)
    return o @ w_out

def peer_ffn(x, w_q, sub_keys, u, v):
    B, S, D = x.shape
    T = B * S
    K = PEER_TOPK
    xt = x.reshape(T, D)
    q = (xt @ w_q).reshape(T, PEER_HEADS, 2, PEER_HALF)
    s = jnp.einsum('thcd,hcnd->thcn', q, sub_keys).astype(jnp.float32)
    s1, i1 = lax.top_k(s[:, :, 0], K)
    s2, i2 = lax.top_k(s[:, :, 1], K)
    cand_s = (s1[..., :, None] + s2[..., None, :]).reshape(T, PEER_HEADS, K * K)
    cand_i = (i1[..., :, None] * PEER_N_KEYS + i2[..., None, :]).reshape(T, PEER_HEADS, K * K)
    top_s, top_pos = lax.top_k(cand_s, K)
    expert_idx = jnp.take_along_axis(cand_i, top_pos, axis=-1)
    gates = jax.nn.softmax(top_s, axis=-1).astype(x.dtype)
    nb = T // PEER_BLOCK

    def expert_block(args):
        xb, eb, gb = args
        ub = jnp.take(u, eb, axis=0)
        act = jax.nn.gelu(jnp.einsum('thkd,td->thk', ub, xb), approximate=False)
        vb = jnp.take(v, eb, axis=0)
        return jnp.einsum('thk,thkd->td', gb * act, vb)

    out = lax.map(expert_block, (xt.reshape(nb, PEER_BLOCK, D),
                                 expert_idx.reshape(nb, PEER_BLOCK, PEER_HEADS, K),
                                 gates.reshape(nb, PEER_BLOCK, PEER_HEADS, K)))
    return out.reshape(B, S, D)

def first_inputs(seed: int = 0) -> dict:
    key = jax.random.key(seed)
    ks = jax.random.split(key, 24)
    D = D_MODEL
    nrm = jax.random.normal
    f32 = jnp.float32
    x = nrm(ks[0], (BATCH, SEQ, D), f32)
    p = nrm(ks[1], (DEPTH, BATCH, SEQ, PLE_DIM), f32)
    positions = jnp.broadcast_to(jnp.arange(SEQ, dtype=jnp.int32), (BATCH, SEQ))
    ln_g = 1.0 + 0.05 * nrm(ks[2], (DEPTH, 2, D), f32)
    ln_b = 0.02 * nrm(ks[3], (DEPTH, 2, D), f32)
    a_w_in = nrm(ks[4], (N_A_LAYERS, D, ML_IN_COLS), f32) * D ** -0.5
    b_i = 0.1 * nrm(ks[5], (N_A_LAYERS, ML_HEADS), f32)
    b_f = jnp.linspace(3.0, 6.0, ML_HEADS, dtype=f32) + 0.1 * nrm(ks[6], (N_A_LAYERS, ML_HEADS), f32)
    a_b_if = jnp.stack([b_i, b_f], axis=1)
    a_hn_g = 1.0 + 0.05 * nrm(ks[7], (N_A_LAYERS, D), f32)
    a_w_out = nrm(ks[8], (N_A_LAYERS, D, D), f32) * (D ** -0.5 * DN_BETA)
    kv_w_down = nrm(ks[9], (D, MLA_KV_RANK + MLA_ROPE_DIM), f32) * D ** -0.5
    kv_norm_g = 1.0 + 0.05 * nrm(ks[10], (MLA_KV_RANK,), f32)
    kv_w_up = nrm(ks[11], (MLA_KV_RANK, MLA_HEADS * (MLA_NOPE_DIM + MLA_V_DIM)), f32) * MLA_KV_RANK ** -0.5
    b_w_dq = nrm(ks[12], (N_B_LAYERS, D, MLA_Q_RANK), f32) * D ** -0.5
    b_q_norm_g = 1.0 + 0.05 * nrm(ks[13], (N_B_LAYERS, MLA_Q_RANK), f32)
    b_w_uq = nrm(ks[14], (N_B_LAYERS, MLA_Q_RANK, MLA_HEADS * (MLA_NOPE_DIM + MLA_ROPE_DIM)), f32) * MLA_Q_RANK ** -0.5
    b_w_out = nrm(ks[15], (N_B_LAYERS, MLA_HEADS * MLA_V_DIM, D), f32) * ((MLA_HEADS * MLA_V_DIM) ** -0.5 * DN_BETA)
    peer_w_q = nrm(ks[16], (DEPTH, D, PEER_HEADS * PEER_KEY_DIM), f32) * D ** -0.5
    peer_sub_keys = nrm(ks[17], (DEPTH, PEER_HEADS, 2, PEER_N_KEYS, PEER_HALF), f32) * PEER_HALF ** -0.5
    peer_u = nrm(ks[18], (DEPTH, PEER_N_EXPERTS, D), f32) * D ** -0.5
    peer_v = nrm(ks[19], (DEPTH, PEER_N_EXPERTS, D), f32) * (DN_BETA * PEER_HEADS ** -0.5)
    ple_w_proj = nrm(ks[20], (DEPTH, PLE_DIM, D), f32) * (0.5 * PLE_DIM ** -0.5)
    ple_w_gate = nrm(ks[21], (DEPTH, D, D), f32) * D ** -0.5
    return {"x": x, "p": p, "positions": positions, "ln_g": ln_g, "ln_b": ln_b,
            "a_w_in": a_w_in, "a_b_if": a_b_if, "a_hn_g": a_hn_g, "a_w_out": a_w_out,
            "kv_w_down": kv_w_down, "kv_norm_g": kv_norm_g, "kv_w_up": kv_w_up,
            "b_w_dq": b_w_dq, "b_q_norm_g": b_q_norm_g, "b_w_uq": b_w_uq, "b_w_out": b_w_out,
            "peer_w_q": peer_w_q, "peer_sub_keys": peer_sub_keys, "peer_u": peer_u, "peer_v": peer_v,
            "ple_w_proj": ple_w_proj, "ple_w_gate": ple_w_gate}

def first_block(x, p, positions, ln_g, ln_b, a_w_in, a_b_if, a_hn_g, a_w_out,
              kv_w_down, kv_norm_g, kv_w_up, b_w_dq, b_q_norm_g, b_w_uq, b_w_out,
              peer_w_q, peer_sub_keys, peer_u, peer_v, ple_w_proj, ple_w_gate):
    cos, sin = rope_angles(positions, MLA_ROPE_DIM)
    shared = None
    for i in range(DEPTH):
        if i < N_A_LAYERS:
            mix = mlstm_mixer(x, a_w_in[i], a_b_if[i], a_hn_g[i], a_w_out[i])
        else:
            j = i - N_A_LAYERS
            if j == 0:
                shared = mla_shared_kv(x, kv_w_down, kv_norm_g, kv_w_up, cos, sin)
            k_nope, k_rope, v = shared
            mix = mla_mixer(x, b_w_dq[j], b_q_norm_g[j], b_w_uq[j], b_w_out[j],
                            k_nope, k_rope, v, cos, sin)
        x = layer_norm(DN_ALPHA * x + mix, ln_g[i, 0], ln_b[i, 0])
        x = layer_norm(DN_ALPHA * x + peer_ffn(x, peer_w_q[i], peer_sub_keys[i], peer_u[i], peer_v[i]),
                       ln_g[i, 1], ln_b[i, 1])
        x = x + jax.nn.sigmoid(x @ ple_w_gate[i]) * (p[i] @ ple_w_proj[i])
    return x


DEPTH_2 = 1

HEAD_DIM = 64
NSA_HEADS = 8
NSA_KV_HEADS = 2
NSA_GROUP = NSA_HEADS // NSA_KV_HEADS
CMP_BLOCK = 32
CMP_STRIDE = 16
CMP_HIDDEN = 256
SLC_BLOCK = 64
N_SELECT = 16
WINDOW = 512
NSA_Q_BLOCK = 64
N_BRANCH = 3
CONV_CHANNELS = 256
CONV_WIDTH = 31
GLA_HEADS = 4
GLA_KEY_DIM = 128
GLA_VALUE_DIM = 256
GLA_GATE_RANK = 16
GLA_TAU = 16.0
GLA_CHUNK = 64
REL_BUCKETS = 32
REL_MAX_DIST = 128
D_FF = -(-8 * D_MODEL // (3 * 256)) * 256
EPS = 1e-6
NEG = -1e30
BIG = 1e30

D_MIX = NSA_HEADS * HEAD_DIM + CONV_CHANNELS + GLA_VALUE_DIM
IN_SPLITS = (
    NSA_HEADS * HEAD_DIM,
    NSA_KV_HEADS * HEAD_DIM, NSA_KV_HEADS * HEAD_DIM,
    NSA_KV_HEADS * HEAD_DIM, NSA_KV_HEADS * HEAD_DIM,
    NSA_KV_HEADS * HEAD_DIM, NSA_KV_HEADS * HEAD_DIM,
    NSA_HEADS * N_BRANCH,
    2 * CONV_CHANNELS,
    GLA_KEY_DIM, GLA_KEY_DIM, GLA_VALUE_DIM,
    GLA_GATE_RANK,
    GLA_VALUE_DIM,
)
D_IN = sum(IN_SPLITS)


def rms_norm_2(x, g):
    x32 = x.astype(jnp.float32)
    y = x32 * lax.rsqrt(jnp.mean(x32 * x32, axis=-1, keepdims=True) + EPS)
    return (y * g.astype(jnp.float32)).astype(x.dtype)

def layer_norm_2(x, g, b):
    x32 = x.astype(jnp.float32)
    mu = jnp.mean(x32, axis=-1, keepdims=True)
    xc = x32 - mu
    y = xc * lax.rsqrt(jnp.mean(xc * xc, axis=-1, keepdims=True) + EPS)
    return (y * g.astype(jnp.float32) + b.astype(jnp.float32)).astype(x.dtype)

def t5_bucket(dist):
    n = jnp.maximum(dist, 0)
    max_exact = REL_BUCKETS // 2
    nf = jnp.maximum(n, 1).astype(jnp.float32)
    large = max_exact + (jnp.log(nf / max_exact) / math.log(REL_MAX_DIST / max_exact)
                         * (REL_BUCKETS - max_exact)).astype(jnp.int32)
    large = jnp.minimum(large, REL_BUCKETS - 1)
    return jnp.where(n < max_exact, n, large)

def masked_softmax(s, mask):
    p = jax.nn.softmax(jnp.where(mask, s, NEG), axis=-1)
    return jnp.where(mask, p, 0.0)

def compress_kv(kv, pos, w1, b1, w2):
    B, S, Hk, D = kv.shape
    r = CMP_BLOCK // CMP_STRIDE
    nsub = S // CMP_STRIDE
    ncmp = nsub - r + 1
    sub = kv.reshape(B, nsub, CMP_STRIDE, Hk, D)
    blocks = jnp.concatenate([sub[:, j:ncmp + j] for j in range(r)], axis=2)
    blocks = blocks + pos[None, None, :, None, :]
    flat = blocks.transpose(0, 1, 3, 2, 4).reshape(B, ncmp, Hk, CMP_BLOCK * D)
    return jax.nn.silu(flat @ w1 + b1) @ w2

def nsa_attention(q, kc, vc, ks, vs, kw, vw, gates, rel_bias):
    B, S = q.shape[0], q.shape[1]
    Hk, G, D = NSA_KV_HEADS, NSA_GROUP, HEAD_DIM
    ncmp = kc.shape[1]
    nsel = S // SLC_BLOCK
    n_top = min(N_SELECT, nsel)
    q = q.reshape(B, S, Hk, G, D) * (D ** -0.5)
    gates = gates.reshape(B, S, Hk, G, N_BRANCH)
    bias_h = rel_bias.T.astype(jnp.float32)
    bias_hkg = bias_h.reshape(Hk, G, REL_BUCKETS).transpose(0, 2, 1)
    cmp_end = jnp.arange(ncmp, dtype=jnp.int32) * CMP_STRIDE + (CMP_BLOCK - 1)
    rs, rc = SLC_BLOCK // CMP_STRIDE, CMP_BLOCK // CMP_STRIDE
    agg = (np.arange(nsel)[:, None, None] * rs + np.arange(rs)[None, :, None]
           - np.arange(rc)[None, None, :]).reshape(nsel, rs * rc)
    agg_valid = jnp.asarray((agg >= 0) & (agg < ncmp))
    agg_idx = jnp.asarray(np.clip(agg, 0, ncmp - 1), dtype=jnp.int32)
    ks_blk = ks.reshape(B, nsel, SLC_BLOCK, Hk, D).transpose(0, 3, 1, 2, 4)
    vs_blk = vs.reshape(B, nsel, SLC_BLOCK, Hk, D).transpose(0, 3, 1, 2, 4)
    kw_pad = jnp.pad(kw, ((0, 0), (WINDOW, 0), (0, 0), (0, 0)))
    vw_pad = jnp.pad(vw, ((0, 0), (WINDOW, 0), (0, 0), (0, 0)))
    b_idx = jnp.arange(B)[:, None, None, None]
    h_idx = jnp.arange(Hk)[None, :, None, None]
    blk_ids = jnp.arange(nsel, dtype=jnp.int32)
    offs = jnp.arange(SLC_BLOCK, dtype=jnp.int32)
    win_offs = jnp.arange(NSA_Q_BLOCK + WINDOW, dtype=jnp.int32)
    Q = NSA_Q_BLOCK

    def head_bias(dist):
        return bias_h[:, t5_bucket(dist)].reshape(Hk, G, *dist.shape)

    def block_fn(c):
        q0 = c * Q
        t = q0 + jnp.arange(Q, dtype=jnp.int32)
        qc = lax.dynamic_slice_in_dim(q, q0, Q, axis=1)
        gc = lax.dynamic_slice_in_dim(gates, q0, Q, axis=1)
        dist_c = t[:, None] - cmp_end[None, :]
        s_c = jnp.einsum('bqhgd,bnhd->bhgqn', qc, kc).astype(jnp.float32) + head_bias(dist_c)
        p_c = masked_softmax(s_c, dist_c >= 0)
        o_c = jnp.einsum('bhgqn,bnhd->bqhgd', p_c.astype(vc.dtype), vc)
        imp = p_c.sum(axis=2)
        imp = jnp.where(agg_valid, jnp.take(imp, agg_idx, axis=-1), 0.0).sum(-1)
        cur = t // SLC_BLOCK
        forced = ((blk_ids[None, :] == 0) | (blk_ids[None, :] == cur[:, None])
                  | (blk_ids[None, :] == cur[:, None] - 1))
        causal_blk = blk_ids[None, :] * SLC_BLOCK <= t[:, None]
        score = jnp.where(causal_blk, jnp.where(forced, BIG, imp), NEG)
        top_val, top_idx = lax.top_k(score, n_top)
        sel_ok = top_val > 0.5 * NEG
        k_sel = ks_blk[b_idx, h_idx, top_idx]
        v_sel = vs_blk[b_idx, h_idx, top_idx]
        key_pos = top_idx[..., None] * SLC_BLOCK + offs
        dist_s = t[None, None, :, None, None] - key_pos
        s_s = jnp.einsum('bqhgd,bhqnkd->bhgqnk', qc, k_sel).astype(jnp.float32)
        bias_s = bias_hkg[h_idx[..., None], t5_bucket(dist_s)]
        s_s = s_s + jnp.moveaxis(bias_s, -1, 2)
        mask_s = (sel_ok[..., None] & (dist_s >= 0))[:, :, None]
        p_s = masked_softmax(s_s.reshape(B, Hk, G, Q, n_top * SLC_BLOCK),
                             mask_s.reshape(B, Hk, 1, Q, n_top * SLC_BLOCK)).reshape(s_s.shape)
        o_s = jnp.einsum('bhgqnk,bhqnkd->bqhgd', p_s.astype(v_sel.dtype), v_sel)
        kwc = lax.dynamic_slice_in_dim(kw_pad, q0, Q + WINDOW, axis=1)
        vwc = lax.dynamic_slice_in_dim(vw_pad, q0, Q + WINDOW, axis=1)
        key_pos_w = q0 - WINDOW + win_offs
        dist_w = t[:, None] - key_pos_w[None, :]
        mask_w = (dist_w >= 0) & (dist_w < WINDOW) & (key_pos_w[None, :] >= 0)
        s_w = jnp.einsum('bqhgd,bkhd->bhgqk', qc, kwc).astype(jnp.float32) + head_bias(dist_w)
        p_w = masked_softmax(s_w, mask_w)
        o_w = jnp.einsum('bhgqk,bkhd->bqhgd', p_w.astype(vwc.dtype), vwc)
        return gc[..., 0:1] * o_c + gc[..., 1:2] * o_s + gc[..., 2:3] * o_w

    out = lax.map(block_fn, jnp.arange(S // Q, dtype=jnp.int32))
    return out.transpose(1, 0, 2, 3, 4, 5).reshape(B, S, NSA_HEADS * HEAD_DIM)

def conformer_conv(u, w_dw, b_dw, ln_g, ln_b):
    a, g = jnp.split(u, 2, axis=-1)
    h = a * jax.nn.sigmoid(g)
    h = lax.conv_general_dilated(h, w_dw[:, None, :], window_strides=(1,),
                                 padding=[(CONV_WIDTH - 1, 0)],
                                 dimension_numbers=('NWC', 'WIO', 'NWC'),
                                 feature_group_count=CONV_CHANNELS) + b_dw
    return jax.nn.silu(layer_norm_2(h, ln_g, ln_b))

def gla_chunked(q, k, v, log_a):
    B, S, H, dk = q.shape
    dv = v.shape[-1]
    C = GLA_CHUNK
    N = S // C

    def chunks(a):
        return a.astype(jnp.float32).reshape(B, N, C, H, a.shape[-1]).transpose(0, 3, 1, 2, 4)

    q, k, v, la = chunks(q), chunks(k), chunks(v), chunks(log_a)
    b = jnp.cumsum(la, axis=3)
    b_last = b[:, :, :, -1:]
    q_t = q * (dk ** -0.5) * jnp.exp(b)
    k_t = k * jnp.exp(-b)
    k_d = k * jnp.exp(b_last - b)
    causal = jnp.tril(jnp.ones((C, C), dtype=bool))
    attn = jnp.where(causal, jnp.einsum('bhncd,bhnsd->bhncs', q_t, k_t), 0.0)
    o_intra = jnp.einsum('bhncs,bhnsv->bhncv', attn, v)

    def step(state, xs):
        qn, kn, vn, dn = xs
        o = jnp.einsum('bhcd,bhdv->bhcv', qn, state)
        state = dn[..., None] * state + jnp.einsum('bhcd,bhcv->bhdv', kn, vn)
        return state, o

    xs = (jnp.moveaxis(q_t, 2, 0), jnp.moveaxis(k_d, 2, 0), jnp.moveaxis(v, 2, 0),
          jnp.moveaxis(jnp.exp(b_last[:, :, :, 0]), 2, 0))
    _, o_inter = lax.scan(step, jnp.zeros((B, H, dk, dv), jnp.float32), xs)
    o = o_intra + jnp.moveaxis(o_inter, 0, 2)
    return o.transpose(0, 2, 3, 1, 4).reshape(B, S, H, dv)

def second_inputs(seed: int = 0) -> dict:
    key = jax.random.key(seed)
    ks = jax.random.split(key, 32)
    L = DEPTH_2

    def nrm(k, shape, scale):
        return jax.random.normal(k, shape, jnp.float32) * scale

    def gain(k, shape):
        return 1.0 + 0.05 * jax.random.normal(k, shape, jnp.float32)

    return {
        "x": nrm(ks[0], (BATCH, SEQ, D_MODEL), 1.0),
        "p": nrm(ks[1], (DEPTH_2, BATCH, SEQ, PLE_DIM), 1.0),
        "rel_bias": nrm(ks[2], (REL_BUCKETS, NSA_HEADS), 0.5),
        "mix_norm_g": gain(ks[3], (L, D_MODEL)),
        "w_in": nrm(ks[4], (L, D_MODEL, D_IN), D_MODEL ** -0.5),
        "w_out": nrm(ks[5], (L, D_MIX, D_MODEL), D_MIX ** -0.5),
        "cmp_pos_k": nrm(ks[6], (L, CMP_BLOCK, HEAD_DIM), 0.1),
        "cmp_w1_k": nrm(ks[7], (L, CMP_BLOCK * HEAD_DIM, CMP_HIDDEN), (CMP_BLOCK * HEAD_DIM) ** -0.5),
        "cmp_b1_k": nrm(ks[8], (L, CMP_HIDDEN), 0.02),
        "cmp_w2_k": nrm(ks[9], (L, CMP_HIDDEN, HEAD_DIM), CMP_HIDDEN ** -0.5),
        "cmp_pos_v": nrm(ks[10], (L, CMP_BLOCK, HEAD_DIM), 0.1),
        "cmp_w1_v": nrm(ks[11], (L, CMP_BLOCK * HEAD_DIM, CMP_HIDDEN), (CMP_BLOCK * HEAD_DIM) ** -0.5),
        "cmp_b1_v": nrm(ks[12], (L, CMP_HIDDEN), 0.02),
        "cmp_w2_v": nrm(ks[13], (L, CMP_HIDDEN, HEAD_DIM), CMP_HIDDEN ** -0.5),
        "conv_w": nrm(ks[14], (L, CONV_WIDTH, CONV_CHANNELS), CONV_WIDTH ** -0.5),
        "conv_b": nrm(ks[15], (L, CONV_CHANNELS), 0.02),
        "conv_ln_g": gain(ks[16], (L, CONV_CHANNELS)),
        "conv_ln_b": nrm(ks[17], (L, CONV_CHANNELS), 0.02),
        "gla_w_alpha": nrm(ks[18], (L, GLA_GATE_RANK, GLA_KEY_DIM), GLA_GATE_RANK ** -0.5),
        "gla_b_alpha": nrm(ks[19], (L, GLA_KEY_DIM), 0.02),
        "gla_norm_g": gain(ks[20], (L, GLA_VALUE_DIM)),
        "ffn_norm_g": gain(ks[21], (L, D_MODEL)),
        "ffn_w_gate": nrm(ks[22], (L, D_MODEL, D_FF), D_MODEL ** -0.5),
        "ffn_w_up": nrm(ks[23], (L, D_MODEL, D_FF), D_MODEL ** -0.5),
        "ffn_w_down": nrm(ks[24], (L, D_FF, D_MODEL), D_FF ** -0.5),
        "ple_norm_g": gain(ks[25], (L, D_MODEL)),
        "ple_w_gate": nrm(ks[26], (L, D_MODEL, D_MODEL), D_MODEL ** -0.5),
        "ple_w_proj": nrm(ks[27], (L, PLE_DIM, D_MODEL), PLE_DIM ** -0.5),
        "final_norm_g": gain(ks[28], (D_MODEL,)),
    }

def second_block(x, p, rel_bias, mix_norm_g, w_in, w_out,
              cmp_pos_k, cmp_w1_k, cmp_b1_k, cmp_w2_k,
              cmp_pos_v, cmp_w1_v, cmp_b1_v, cmp_w2_v,
              conv_w, conv_b, conv_ln_g, conv_ln_b,
              gla_w_alpha, gla_b_alpha, gla_norm_g,
              ffn_norm_g, ffn_w_gate, ffn_w_up, ffn_w_down,
              ple_norm_g, ple_w_gate, ple_w_proj, final_norm_g):
    B, S, _ = x.shape
    split_at = np.cumsum(IN_SPLITS)[:-1].tolist()

    def heads(a, n):
        return a.reshape(B, S, n, -1)

    for i in range(DEPTH_2):
        h = rms_norm_2(x, mix_norm_g[i])
        z = h @ w_in[i]
        (nq, kc, vc, ks_, vs_, kw, vw, ng, cu, gq, gk, gv, ga, gr) = jnp.split(z, split_at, axis=-1)
        kc = compress_kv(heads(kc, NSA_KV_HEADS), cmp_pos_k[i], cmp_w1_k[i], cmp_b1_k[i], cmp_w2_k[i])
        vc = compress_kv(heads(vc, NSA_KV_HEADS), cmp_pos_v[i], cmp_w1_v[i], cmp_b1_v[i], cmp_w2_v[i])
        y_nsa = nsa_attention(heads(nq, NSA_HEADS), kc, vc,
                              heads(ks_, NSA_KV_HEADS), heads(vs_, NSA_KV_HEADS),
                              heads(kw, NSA_KV_HEADS), heads(vw, NSA_KV_HEADS),
                              jax.nn.sigmoid(ng).reshape(B, S, NSA_HEADS, N_BRANCH), rel_bias)
        y_conv = conformer_conv(cu, conv_w[i], conv_b[i], conv_ln_g[i], conv_ln_b[i])
        log_a = jax.nn.log_sigmoid((ga @ gla_w_alpha[i] + gla_b_alpha[i]).astype(jnp.float32)) / GLA_TAU
        o = gla_chunked(heads(gq, GLA_HEADS), heads(gk, GLA_HEADS), heads(gv, GLA_HEADS),
                        heads(log_a, GLA_HEADS))
        o = rms_norm_2(o, gla_norm_g[i].reshape(GLA_HEADS, -1)).reshape(B, S, GLA_VALUE_DIM)
        y_gla = (o * jax.nn.silu(gr)).astype(x.dtype)
        x = x + jnp.concatenate([y_nsa, y_conv, y_gla], axis=-1) @ w_out[i]
        h = rms_norm_2(x, ffn_norm_g[i])
        x = x + (jax.nn.silu(h @ ffn_w_gate[i]) * (h @ ffn_w_up[i])) @ ffn_w_down[i]
        gate = jax.nn.sigmoid(rms_norm_2(x, ple_norm_g[i]) @ ple_w_gate[i])
        x = x + (p[i] @ ple_w_proj[i]) * gate
    return rms_norm_2(x, final_norm_g)


def setup_inputs(seed=0):
    out = dict(first_inputs(seed))
    for name, value in second_inputs(seed + 1).items():
        if name != "x":
            out[name + "_2"] = value
    return out


def reference(
    x, p, positions, ln_g, ln_b, a_w_in, a_b_if, a_hn_g, a_w_out, kv_w_down, kv_norm_g, kv_w_up,
    b_w_dq, b_q_norm_g, b_w_uq, b_w_out, peer_w_q, peer_sub_keys, peer_u, peer_v, ple_w_proj,
    ple_w_gate, p_2, rel_bias_2, mix_norm_g_2, w_in_2, w_out_2, cmp_pos_k_2, cmp_w1_k_2,
    cmp_b1_k_2, cmp_w2_k_2, cmp_pos_v_2, cmp_w1_v_2, cmp_b1_v_2, cmp_w2_v_2, conv_w_2, conv_b_2,
    conv_ln_g_2, conv_ln_b_2, gla_w_alpha_2, gla_b_alpha_2, gla_norm_g_2, ffn_norm_g_2,
    ffn_w_gate_2, ffn_w_up_2, ffn_w_down_2, ple_norm_g_2, ple_w_gate_2, ple_w_proj_2,
    final_norm_g_2,
):
    x = first_block(
        x, p, positions, ln_g, ln_b, a_w_in, a_b_if, a_hn_g, a_w_out, kv_w_down, kv_norm_g,
        kv_w_up, b_w_dq, b_q_norm_g, b_w_uq, b_w_out, peer_w_q, peer_sub_keys, peer_u, peer_v,
        ple_w_proj, ple_w_gate,
    )
    return second_block(
        x, p_2, rel_bias_2, mix_norm_g_2, w_in_2, w_out_2, cmp_pos_k_2, cmp_w1_k_2, cmp_b1_k_2,
        cmp_w2_k_2, cmp_pos_v_2, cmp_w1_v_2, cmp_b1_v_2, cmp_w2_v_2, conv_w_2, conv_b_2,
        conv_ln_g_2, conv_ln_b_2, gla_w_alpha_2, gla_b_alpha_2, gla_norm_g_2, ffn_norm_g_2,
        ffn_w_gate_2, ffn_w_up_2, ffn_w_down_2, ple_norm_g_2, ple_w_gate_2, ple_w_proj_2,
        final_norm_g_2,
    )


_drawn_inputs = setup_inputs


def setup_inputs(seed=0):
    import zlib

    import numpy as np

    out = dict(_drawn_inputs(seed))
    spreads = {}
    factors = {'a_hn_g': 3.746,
     'kv_norm_g': 7.147,
     'b_q_norm_g': 8.0,
     'cmp_pos_k_2': 48.537,
     'cmp_b1_k_2': 200.0,
     'cmp_pos_v_2': 3.539,
     'cmp_b1_v_2': 28.634,
     'conv_b_2': 5.374,
     'conv_ln_g_2': 2.997,
     'conv_ln_b_2': 8.0,
     'gla_b_alpha_2': 8.0,
     'gla_norm_g_2': 4.3,
     'ple_norm_g_2': 25.849,
     'cmp_w1_k_2': 2.677}
    for name, (base, spread) in spreads.items():
        noise = np.random.default_rng([zlib.crc32(name.encode()), seed]).standard_normal(out[name].shape)
        drawn = base * np.exp(spread * noise) if base else spread * noise
        out[name] = jnp.asarray(drawn.astype(out[name].dtype))
    for name, factor in factors.items():
        out[name] = (out[name] * factor).astype(out[name].dtype)
    return out
```

```python
import math
from contextlib import ExitStack

import concourse.bass as bass
import numpy as np
from concourse import mybir

F32 = mybir.dt.float32
I32 = mybir.dt.int32
U32 = mybir.dt.uint32
ALU = mybir.AluOpType
ACT = mybir.ActivationFunctionType
AX = mybir.AxisListType

P = 128
T = 256
TT = T // P
D = 1024
KD = D // P
NEG = -1e30
FLOOR = -3e38
DEPTH = 2
ALPHA = (2.0 * DEPTH) ** 0.25
EPS1, EPS2 = 1e-5, 1e-6
MH, MQK, MV = 8, 64, 128
AH, NOPE, ROPE, AV, KVR, QR = 8, 128, 64, 128, 256, 384
PH, NK, TOPK, NEXP = 8, 128, 16, 128 * 128
PICKS = PH * TOPK
SLOTS = 8
NH, NKV, HD = 8, 2, 64
CB, CS, NCMP, CHID = 32, 16, 15, 256
CC, CW = 256, 31
GH, GK, GV, GR, GCH = 4, 128, 256, 16, 64
FF = 2816
W2SPLIT = (512, 128, 128, 128, 128, 128, 128, 24, 512, 128, 128, 256, 16, 256)
W2AT = [sum(W2SPLIT[:i]) for i in range(len(W2SPLIT) + 1)]
BUCKETS, MAXDIST = 32, 128
VEC = 383
STRIP = 384 + NCMP + 7
RING, SLOT = 4, 4096


def bucket_of(dist):
    half = BUCKETS // 2
    if dist < half:
        return dist
    return min(half + int(math.log(dist / half) / math.log(MAXDIST / half) * (BUCKETS - half)), BUCKETS - 1)


def constants():
    r, c = np.arange(P)[:, None], np.arange(P)[None, :]
    parts = {
        "ident": (r == c) * 1.0,
        "mask_q": np.where(c > r, NEG, 0.0),
        "mask_s": np.where(c < r, NEG, 0.0),
        "tri": ((r <= c) & (r // GCH == c // GCH)) * 1.0,
        "sel": np.repeat(np.eye(P, 8), P, axis=1),
        "freq": np.broadcast_to(10000.0 ** (-np.arange(0, ROPE, 2, dtype=np.float32) / np.float32(ROPE)), (P, ROPE // 2)),
        "seen": np.stack([(np.arange(P) >= CB - 1) * 1.0, np.ones(P)], axis=1),
        "i16": np.broadcast_to(np.arange(TOPK), (P, TOPK)),
        "minus_half": np.full((P, 32), -0.5),
    }
    onehot = np.zeros((P, 384))
    for j in range(256):
        onehot[bucket_of(255 - j), j] = 1.0
    parts["onehot"] = onehot
    parts["future"] = np.broadcast_to(np.where(np.arange(384) > 255, NEG, 0.0), (P, 384))
    at, where = 0, {}
    for k, v in parts.items():
        where[k] = (at, v.shape[1])
        at += v.shape[1]
    return np.concatenate([np.asarray(v, np.float32) for v in parts.values()], axis=1).astype(np.float32), where


def build(nc, a, consts, cwhere, scratch, out):
    ctx = ExitStack()
    with ctx:
        named = {}

        def sb(name, shape, dt=F32, stack=ctx):
            named[name] = named.get(name, 0) + 1
            name += f"_{named[name]}" if named[name] > 1 else ""
            return stack.enter_context(nc.sbuf_tensor(name, shape, dt))

        bank = [ctx.enter_context(nc.psum_tensor(f"bank{i}", [P, 512], F32)) for i in range(8)]
        CN = sb("CN", [P, consts.shape[1]])
        X = sb("X", [P, TT, D])
        Y = sb("Y", [P, TT, D])
        XT = sb("XT", [P, KD, T])
        ring = [sb(f"ring{i}", [P, SLOT]) for i in range(RING)]
        rows = [sb(f"rows{i}", [P, 3 - i, D]) for i in range(2)]
        stat = sb("stat", [P, 64])

        def con(name, rows_=P):
            at, n = cwhere[name]
            return CN[0:rows_, at:at + n]

        ident = con("ident")

        sems, count, base = {}, {}, {}

        def S(name):
            if name not in sems:
                sems[name] = ctx.enter_context(nc.semaphore(name))
                count[name] = 0
            return sems[name]

        def tick(name, n=1):
            S(name)
            count[name] += n
            return sems[name], n

        def now(name):
            return S(name), count[name]

        def nth(name, n):
            return S(name), base.get(name, 0) + n

        chain = {nc.vector: "dve_step", nc.scalar: "act_step", nc.gpsimd: "pool_step"}

        jobs, numbered = {}, [0]

        def job(name):
            jobs[name] = numbered[0]
            numbered[0] += 1
            return result(name)

        def result(name):
            return bank[jobs[name] % 8]

        def turn(name):
            return jobs[name] // 8 + 1

        def bank_ready(name):
            return S(f"bank_ready{jobs[name] % 8}")

        def bank_free(name):
            return S(f"bank_free{jobs[name] % 8}")

        def cols(w, c0, c1):
            return w.rearrange("(k p) n -> p k n", p=P)[:, :, c0:c1]

        stream, place = [], {}

        def enter(key, ap):
            place[key] = len(stream)
            stream.append(ap)

        def enter_cols(key, w, edges):
            for i in range(len(edges) - 1):
                enter(f"{key}{i}", cols(w, edges[i], edges[i + 1]))

        w_in = a["a_w_in"][0]
        for key, c0, c1 in (("a_gate", 2048, 2064), ("a_q", 0, 512), ("a_k", 512, 1024), ("a_v0", 1024, 1536),
                            ("a_v1", 1536, 2048), ("a_og0", 2064, 2576), ("a_og1", 2576, 3088)):
            enter(key, cols(w_in, c0, c1))
        enter_cols("a_out", a["a_w_out"][0], [0, 512, 1024])

        def enter_peer(l):
            enter(f"keys{l}", a["peer_sub_keys"][l].rearrange("h c n d -> n (h c) d"))
            enter_cols(f"peer_q{l}_", a["peer_w_q"][l], [0, 512, 1024, 1536, 2048])
            enter_cols(f"ple_gate{l}_", a["ple_w_gate"][l], [0, 512, 1024])
            enter(f"ple_proj{l}", cols(a["ple_w_proj"][l], 0, D))

        enter_peer(0)
        enter("kv_down", cols(a["kv_w_down"], 0, KVR + ROPE))
        enter("dq", cols(a["b_w_dq"][0], 0, QR))
        enter("kv_up", cols(a["kv_w_up"], 0, 2048))
        enter_cols("uq", a["b_w_uq"][0], [0, 768, 1536])
        enter_cols("b_out", a["b_w_out"][0], [0, 512, 1024])
        enter_peer(1)
        enter_cols("n_in", a["w_in_2"][0], [0, 512, 1024, 1304, 1816, 2328, 2600])
        for s in "kv":
            enter(f"w1{s}", a[f"cmp_w1_{s}_2"][0].rearrange("(j p) n -> p j n", p=P))
        enter_cols("n_out", a["w_out_2"][0], [0, 512, 1024])
        ffe = list(range(0, FF, 512)) + [FF]
        for i in range(len(ffe) - 1):
            enter(f"ffg{i}", cols(a["ffn_w_gate_2"][0], ffe[i], ffe[i + 1]))
            enter(f"ffu{i}", cols(a["ffn_w_up_2"][0], ffe[i], ffe[i + 1]))
        for cb in range(2):
            for i, (k0, k1) in enumerate(((0, 8), (8, 16), (16, 22))):
                enter(f"ffd{cb}{i}", cols(a["ffn_w_down_2"][0], cb * 512, cb * 512 + 512)[:, k0:k1, :])
        enter_cols("ple2_gate", a["ple_w_gate_2"][0], [0, 512, 1024])
        enter("ple2_proj", cols(a["ple_w_proj_2"][0], 0, D))

        def slot_view(n):
            _, k, m = stream[n].shape
            return ring[n % RING][:, 0:k * m].rearrange("p (k m) -> p k m", k=k)

        taken, released = [0], {}

        def landed(key):
            n = place[key]
            assert n == taken[0], (key, n, taken[0])
            taken[0] += 1
            return S(f"weight_in{n % RING}"), 16 * (n // RING + 1)

        def slot_of(key):
            return slot_view(place[key])

        def weight_read(key, name):
            released[place[key]] = jobs[name]

        mm, tr = nc.tensor.matmul, nc.tensor.transpose

        def mul(out_, lhsT, rhs, start, stop):
            return mm(out_, lhsT, rhs, start=start, stop=stop, skip_group_check=True)

        def pe_turn(pe, tag, src, wait_name, nk=KD):
            for tt in range(TT):
                if wait_name:
                    pe.wait_ge(*nth(wait_name, tt + 1))
                for g in range(0, nk, 4):
                    b = job(f"{tag}{tt}{g // 4}")
                    if turn(f"{tag}{tt}{g // 4}") > 1:
                        pe.wait_ge(bank_free(f"{tag}{tt}{g // 4}"), turn(f"{tag}{tt}{g // 4}") - 1)
                    n = min(4, nk - g)
                    for j in range(n):
                        last = tr(b[:, j * P:(j + 1) * P], src[:, tt, (g + j) * P:(g + j + 1) * P], ident)
                    last.then_inc(bank_ready(f"{tag}{tt}{g // 4}"), 1)

        def take_turn(e, tag, dst, groups, nk=KD):
            for tt, g in groups:
                e.wait_ge(bank_ready(f"{tag}{tt}{g}"), turn(f"{tag}{tt}{g}"))
                b = result(f"{tag}{tt}{g}")
                n = min(4, nk - 4 * g)
                o = dst[:, 4 * g:4 * g + n, tt * P:(tt + 1) * P]
                i = b[:, 0:n * P].rearrange("p (k t) -> p k t", k=n)
                copy(e, o, i).then_inc(bank_free(f"{tag}{tt}{g}"), 1)

        def copy(e, o, i, scale=None):
            if e is nc.scalar:
                return nc.scalar.activation(o, i, ACT.Copy, scale=scale or 1.0)
            if scale:
                return nc.vector.tensor_scalar(o, i, scale, None, ALU.mult)
            return nc.vector.tensor_copy(o, i)

        def pe_rows(pe, w, name, lhs, tt, c0, n):
            b = job(name)
            if turn(name) > 1:
                pe.wait_ge(bank_free(name), turn(name) - 1)
            k = w.shape[1]
            for i in range(k):
                last = mul(b[:, 0:n], lhs[:, i, tt * P:(tt + 1) * P], w[:, i, c0:c0 + n], i == 0, i == k - 1)
            last.then_inc(bank_ready(name), 1)
            return last

        def pe_colpair(pe, w, name, rhs, starts, m=P):
            b = job(name)
            if turn(name) > 1:
                pe.wait_ge(bank_free(name), turn(name) - 1)
            k = w.shape[1]
            for s, c in enumerate(starts):
                for i in range(k):
                    last = mul(b[0:m, s * T:(s + 1) * T], w[:, i, c:c + m], rhs[:, i, :], i == 0, i == k - 1)
            last.then_inc(bank_ready(name), 1)
            return last

        def pair(b, m=P):
            return b[0:m, 0:2 * T].rearrange("p (s t) -> p s t", s=2)

        V = nc.vector
        A = nc.scalar
        G = nc.gpsimd

        def pool_power(name_in, n_in, name_out, cells):
            G.wait_ge(*nth(name_in, n_in))
            at, _ = cwhere["minus_half"]
            G.tensor_tensor(cells, cells, CN[:, at:at + cells.shape[1]], ALU.pow).then_inc(*tick(name_out))
            G.wait_ge(*now(name_out))

        def dve_residual(tag, scale):
            for tt in range(TT):
                for cb in range(2):
                    s = slice(cb * 512, cb * 512 + 512)
                    V.wait_ge(bank_ready(f"{tag}{cb}{tt}"), turn(f"{tag}{cb}{tt}"))
                    b = result(f"{tag}{cb}{tt}")
                    V.scalar_tensor_tensor(Y[:, tt, s], X[:, tt, s], scale, b[:, :], ALU.mult, ALU.add).then_inc(bank_free(f"{tag}{cb}{tt}"), 1)
            for name in [f"{tag}{cb}{tt}" for tt in range(TT) for cb in range(2)]:
                V.wait_ge(bank_free(name), turn(name))

        def dve_layer_norm(src, dst, g, b, eps, key, done):
            n = src.shape[2]
            for tt in range(TT):
                pieces = max(1, n // 512)
                for c in range(pieces):
                    w = n // pieces
                    V.bn_stats(stat[:, 16 + 6 * c:22 + 6 * c], src[:, tt, c * w:(c + 1) * w]).then_inc(*tick("dve_step"))
                    V.wait_ge(*now("dve_step"))
                V.bn_aggr(stat[:, 4 * tt:4 * tt + 2], stat[:, 16:16 + 6 * pieces]).then_inc(*tick("dve_step"))
                V.wait_ge(*now("dve_step"))
                V.tensor_scalar(stat[:, 8 + tt:9 + tt], stat[:, 4 * tt + 1:4 * tt + 2], eps, None, ALU.add).then_inc(*tick(key + "_var"))
                V.wait_ge(*now(key + "_var"))
            V.wait_ge(*nth(key + "_rstd", 1))
            for tt in range(TT):
                V.scalar_tensor_tensor(src[:, tt, :], src[:, tt, :], stat[:, 4 * tt:4 * tt + 1], g, ALU.subtract, ALU.mult).then_inc(*tick("dve_step"))
                V.wait_ge(*now("dve_step"))
                V.scalar_tensor_tensor(dst[:, tt, :], src[:, tt, :], stat[:, 8 + tt:9 + tt], b, ALU.mult, ALU.add).then_inc(*tick(done))
                V.wait_ge(*now(done))

        def pool_layer_norm(key):
            pool_power(key + "_var", TT, key + "_rstd", stat[:, 8:8 + TT])

        def act_squares(src, junk, name, n):
            for tt in range(TT):
                A.activation(junk[:, tt, 0:n], src[:, tt, 0:n], ACT.Square, accum_out=stat[:, 12 + tt:13 + tt]).then_inc(*tick(name))
                A.wait_ge(*now(name))

        def dve_mean_square(key, n, eps):
            V.wait_ge(*nth(key + "_sq", TT))
            V.tensor_scalar(stat[:, 12:14], stat[:, 12:14], 1.0 / n, eps, ALU.mult, ALU.add).then_inc(*tick(key + "_var"))
            V.wait_ge(*now(key + "_var"))
            V.wait_ge(*nth(key + "_rstd", 1))

        phase_no = [0]

        def end_phase(block):
            phase_no[0] += 1
            n = 4 * phase_no[0]

            def meet(e):
                if e in chain and count.get(chain[e]):
                    e.wait_ge(S(chain[e]), count[chain[e]])
                e.sem_inc(S("phase_end"), 1)
                e.wait_ge(S("phase_end"), n)

            block.tensor(lambda e: meet(nc.tensor))
            block.scalar(lambda e: meet(A))
            block.vector(lambda e: meet(V))
            block.gpsimd(lambda e: meet(G))
            base.clear()
            base.update(count)
            jobs.clear()

        rows_total = [0, 0]

        def load_rows(which, aps):
            for i, ap in enumerate(aps):
                G.dma_start(rows[which][:, i, 0:ap.shape[-1]], ap.partition_broadcast(P)).then_inc(S(f"rows_in{which}"), 16)

        def rows_here(which, n):
            rows_total[which] += 16 * n
            V.wait_ge(S(f"rows_in{which}"), rows_total[which])

        PE = nc.tensor

        BIF = sb("BIF", [MH, 2])
        POS = sb("POS", [P, TT], I32)
        SMALL = sb("SMALL", [P, KVR + QR + 3 * CC + GK])
        RELB = sb("RELB", [BUCKETS, NH])
        B1 = sb("B1", [P, 2, 2])
        W2 = sb("W2", [P, 2, 2, HD])
        CPOS = sb("CPOS", [CB // 2, 2, P])
        CONVW = sb("CONVW", [CW, CC])
        CONVB = sb("CONVB", [P, 2])
        WAL = sb("WAL", [GR, GK])
        PIN = sb("PIN", [P, 3, TT, 256])
        small_at, at = {}, 0
        small_src = [("kv_norm_g", a["kv_norm_g"]), ("b_q_norm_g", a["b_q_norm_g"][0]), ("conv_ln_g_2", a["conv_ln_g_2"][0]),
                     ("conv_ln_b_2", a["conv_ln_b_2"][0]), ("gla_norm_g_2", a["gla_norm_g_2"][0]), ("gla_b_alpha_2", a["gla_b_alpha_2"][0])]
        params = [(POS[:, :], a["positions"][0].rearrange("(t p) -> p t", p=P)), (RELB[:, :], a["rel_bias_2"]),
                  (CONVW[:, :], a["conv_w_2"][0]), (CONVB[:, :], a["conv_b_2"][0].rearrange("(t p) -> p t", p=P)),
                  (WAL[:, :], a["gla_w_alpha_2"][0])]
        for k, src in small_src:
            n = src.shape[0]
            small_at[k] = (at, n)
            params.append((SMALL[:, at:at + n], src.partition_broadcast(P)))
            at += n
        for i, s in enumerate("kv"):
            params.append((B1[:, i, :], a[f"cmp_b1_{s}_2"][0].rearrange("(t p) -> p t", p=P)))
            params.append((W2[:, i, :, :], a[f"cmp_w2_{s}_2"][0].rearrange("(t p) d -> p t d", p=P)))
            params.append((CPOS[:, i, :], a[f"cmp_pos_{s}_2"][0].rearrange("(j e) d -> j (e d)", e=2)))
        for i, src in enumerate((a["p"][0, 0], a["p"][1, 0], a["p_2"][0, 0])):
            params.append((PIN[:, i, :, :], src.rearrange("(t p) d -> p t d", p=P)))

        def small(k):
            at, n = small_at[k]
            return SMALL[:, at:at + n]

        def params_here(e):
            e.wait_ge(S("params_in"), 16 * len(params))

        def store_and_load(block):
            @block.sync
            def _(sp):
                sp.dma_start(X[:, :, :], a["x"][0].rearrange("(t p) d -> p t d", p=P)).then_inc(S("first_in"), 16)
                sp.dma_start(CN[:, :], consts).then_inc(S("first_in"), 16)
                with nc.allow_non_contiguous_dma(reason="16 gate biases"):
                    sp.dma_start(BIF[:, :], a["a_b_if"][0].rearrange("t h -> h t")).then_inc(S("first_in"), 16)
                for n, ap in enumerate(stream):
                    if n >= RING:
                        j = released[n - RING]
                        sp.wait_ge(sems[f"bank_ready{j % 8}"], j // 8 + 1)
                    sp.dma_start(slot_view(n), ap).then_inc(S(f"weight_in{n % RING}"), 16)
                sp.wait_ge(S("out_ready"), TT)
                sp.dma_start(out[0].rearrange("(t p) d -> p t d", p=P), Y[:, :, :]).then_inc(S("out_stored"), 16)
                sp.wait_ge(S("out_stored"), 16)

        def logsig_steps(tmp, name):
            A.wait_ge(*nth(name + "_abs", 1))
            A.activation(tmp, tmp, ACT.Exp, scale=-1.0).then_inc(*tick("act_step"))
            A.wait_ge(*now("act_step"))
            A.activation(tmp, tmp, ACT.Ln, bias=1.0).then_inc(*tick(name + "_ln"))
            A.wait_ge(*now(name + "_ln"))

        def mlstm(block, st):
            QT = sb("QT", [P, MH // 2, T], F32, st)
            KT = sb("KT", [P, MH // 2, T], F32, st)
            VA = sb("VA", [P, TT, MH, MV + 1], F32, st)
            OG = sb("OG", [P, TT, D], F32, st)
            GA = sb("GA", [MH, 8, T], F32, st)
            IG, GF, LN, CUM, GM, MM, NM, NMT = (GA[:, i, :] for i in range(8))
            ONE8 = sb("ONE8", [MH, T], F32, st)
            GTS = sb("GTS", [P, TT, MH], F32, st)
            EMS = sb("EMS", [P, TT, MH], F32, st)
            DN = sb("DN", [P, MH, TT], F32, st)
            WT = [sb(f"WT{i}", [P, 384], F32, st) for i in range(2)]
            PT = [sb(f"PT{i}", [P, 384], F32, st) for i in range(2)]
            MU = sb("MU", [P, 16], F32, st)
            VR = sb("VR", [P, 16], F32, st)
            sel = con("sel", MH)

            @block.tensor
            def _(pe):
                pe.wait_ge(S("first_in"), 48)
                pe_turn(PE, "xt", X, None)
                pe.wait_ge(bank_free("xt00"), turn("xt00"))
                pe.wait_ge(bank_free("xt01"), turn("xt01"))
                pe.wait_ge(bank_free("xt10"), turn("xt10"))
                pe.wait_ge(bank_free("xt11"), turn("xt11"))
                pe.wait_ge(*landed("a_gate"))
                w = slot_of("a_gate")
                pe_colpair(PE, w, "gate", XT, [0, MH], MH)
                weight_read("a_gate", "gate")
                for s in "qk":
                    pe.wait_ge(*landed(f"a_{s}"))
                    w = slot_of(f"a_{s}")
                    for i in range(2):
                        pe_colpair(PE, w, f"{s}{i}", XT, [256 * i, 256 * i + 128])
                    weight_read(f"a_{s}", f"{s}1")
                pe.wait_ge(*nth("gates_done", 1))
                b = job("gt")
                if turn("gt") > 1:
                    PE.wait_ge(bank_free("gt"), turn("gt") - 1)
                for i in range(TT):
                    tr(b[:, i * MH:(i + 1) * MH], GM[:, i * P:(i + 1) * P], ident[0:MH, 0:MH])
                for i in range(TT):
                    last = tr(b[:, (TT + i) * MH:(TT + i + 1) * MH], NMT[:, i * P:(i + 1) * P], ident[0:MH, 0:MH])
                last.then_inc(bank_ready("gt"), 1)
                for s in ("v", "og"):
                    for cb in range(2):
                        pe.wait_ge(*landed(f"a_{s}{cb}"))
                        w = slot_of(f"a_{s}{cb}")
                        for tt in range(TT):
                            pe_rows(PE, w, f"{s}{cb}{tt}", XT, tt, 0, 512)
                        weight_read(f"a_{s}{cb}", f"{s}{cb}1")
                for i in range(MH + 1):
                    if i < MH:
                        h, hp = i, i // 2
                        b = job(f"w{h}")
                        if turn(f"w{h}") > 1:
                            PE.wait_ge(bank_free(f"w{h}"), turn(f"w{h}") - 1)
                        sh = sel[:, h * P:(h + 1) * P]
                        mul(b[:, 0:T], sh, NM, True, False)
                        mul(b[:, 0:P], ident, con("mask_s"), False, True)
                        mul(b[:, T:T + P], sh, NM[:, P:T], True, False)
                        mul(b[:, T:T + P], ident, con("mask_s"), False, True).then_inc(bank_ready(f"w{h}"), 1)
                        r = slice(64 * (h % 2), 64 * (h % 2) + 64)
                        if h == 0:
                            pe.wait_ge(bank_free("q0"), turn("q0"))
                            pe.wait_ge(bank_free("q1"), turn("q1"))
                            pe.wait_ge(bank_free("k0"), turn("k0"))
                            pe.wait_ge(bank_free("k1"), turn("k1"))
                        b = job(f"s{h}")
                        if turn(f"s{h}") > 1:
                            PE.wait_ge(bank_free(f"s{h}"), turn(f"s{h}") - 1)
                        mul(b[:, 0:T], KT[r, hp, 0:P], QT[r, hp, :], True, True)
                        mul(b[:, T:T + P], KT[r, hp, P:T], QT[r, hp, P:T], True, True).then_inc(bank_ready(f"s{h}"), 1)
                    if i >= 1:
                        h = i - 1
                        pe.wait_ge(bank_free(f"s{h}"), turn(f"s{h}"))
                        if h == 0:
                            for name in [f"v{cb}{tt}" for cb in range(2) for tt in range(TT)]:
                                pe.wait_ge(bank_free(name), turn(name))
                        b = job(f"n{h}")
                        if turn(f"n{h}") > 1:
                            PE.wait_ge(bank_free(f"n{h}"), turn(f"n{h}") - 1)
                        n = MV + 1
                        mul(b[:, 0:n], PT[h % 2][:, 0:P], VA[:, 0, h, :], True, True)
                        mul(b[:, n:2 * n], PT[h % 2][:, P:T], VA[:, 0, h, :], True, False)
                        mul(b[:, n:2 * n], PT[h % 2][:, T:T + P], VA[:, 1, h, :], False, True).then_inc(bank_ready(f"n{h}"), 1)
                pe_turn(PE, "yt", Y, "y_ready")
                pe.wait_ge(bank_free("yt00"), turn("yt00"))
                pe.wait_ge(bank_free("yt01"), turn("yt01"))
                pe.wait_ge(bank_free("yt10"), turn("yt10"))
                pe.wait_ge(bank_free("yt11"), turn("yt11"))
                for cb in range(2):
                    pe.wait_ge(*landed(f"a_out{cb}"))
                    w = slot_of(f"a_out{cb}")
                    for tt in range(TT):
                        pe_rows(PE, w, f"o{cb}{tt}", XT, tt, 0, 512)
                    weight_read(f"a_out{cb}", f"o{cb}1")

            @block.scalar
            def _(act):
                with nc.allow_non_contiguous_dma(reason="a few hundred parameters"):
                    for o, i in params:
                        act.dma_start(o, i).then_inc(S("params_in"), 16)
                take_turn(A, "xt", XT, [(0, 0), (1, 0)])
                logsig_steps(LN, "gate")
                for s, dst in (("q", QT), ("k", KT)):
                    for i in range(2):
                        A.wait_ge(bank_ready(f"{s}{i}"), turn(f"{s}{i}"))
                        b = result(f"{s}{i}")
                        copy(A, dst[:, 2 * i:2 * i + 2, :], pair(b)).then_inc(bank_free(f"{s}{i}"), 1)
                A.wait_ge(bank_ready("gt"), turn("gt"))
                b = result("gt")
                A.activation(GTS[:, :, :], b[:, 0:2 * MH].rearrange("p (t h) -> p t h", t=TT), ACT.Copy).then_inc(*tick("act_step"))
                A.wait_ge(*now("act_step"))
                A.activation(EMS[:, :, :], b[:, 2 * MH:4 * MH].rearrange("p (t h) -> p t h", t=TT), ACT.Exp).then_inc(bank_free("gt"), 1)
                for cb in range(2):
                    for tt in range(TT):
                        A.wait_ge(bank_ready(f"v{cb}{tt}"), turn(f"v{cb}{tt}"))
                        b = result(f"v{cb}{tt}")
                        copy(A, VA[:, tt, 4 * cb:4 * cb + 4, 0:MV], b[:, :].rearrange("p (h v) -> p h v", h=4)).then_inc(bank_free(f"v{cb}{tt}"), 1)
                for cb in range(2):
                    for tt in range(TT):
                        A.wait_ge(bank_ready(f"og{cb}{tt}"), turn(f"og{cb}{tt}"))
                        b = result(f"og{cb}{tt}")
                        A.activation(OG[:, tt, cb * 512:cb * 512 + 512], b[:, :], ACT.Sigmoid).then_inc(bank_free(f"og{cb}{tt}"), 1)
                for h in range(MH):
                    A.wait_ge(bank_ready(f"w{h}"), turn(f"w{h}"))
                    b = result(f"w{h}")
                    if h >= 2:
                        A.wait_ge(bank_free(f"s{h - 2}"), turn(f"s{h - 2}"))
                    A.activation(WT[h % 2][:, 0:T], b[:, 0:T], ACT.Exp, bias=GTS[:, 0, h:h + 1]).then_inc(*tick("act_step"))
                    A.activation(WT[h % 2][:, T:T + P], b[:, T:T + P], ACT.Exp, bias=GTS[:, 1, h:h + 1]).then_inc(bank_free(f"w{h}"), 1)
                A.wait_ge(*nth("centred", 1))
                sq = XT[:, :, :].rearrange("p k t -> p (k t)")
                A.activation(sq, Y[:, :, :].rearrange("p t d -> p (t d)"), ACT.Square).then_inc(*tick("h_sq"))
                A.wait_ge(*now("h_sq"))
                take_turn(A, "yt", XT, [(0, 0), (1, 0)])

            @block.vector
            def _(dve):
                V.memset(ONE8[:, :], 1.0).then_inc(*tick("dve_step"))
                V.memset(VA[:, :, :, MV:MV + 1], 1.0).then_inc(*tick("dve_step"))
                take_turn(V, "xt", XT, [(0, 1), (1, 1)])
                V.wait_ge(bank_ready("gate"), turn("gate"))
                b = result("gate")
                dve.wait_ge(S("first_in"), 48)
                V.tensor_scalar(IG, b[0:MH, 0:T], BIF[:, 0:1], None, ALU.add).then_inc(*tick("dve_step"))
                V.wait_ge(*now("dve_step"))
                V.tensor_scalar(GF, b[0:MH, T:2 * T], BIF[:, 1:2], None, ALU.add).then_inc(bank_free("gate"), 1)
                V.wait_ge(bank_free("gate"), turn("gate"))
                V.scalar_tensor_tensor(LN, GF, -1.0, GF, ALU.mult, ALU.max).then_inc(*tick("gate_abs"))
                V.wait_ge(*now("gate_abs"))
                V.wait_ge(*nth("gate_ln", 1))
                V.scalar_tensor_tensor(GF, GF, 0.0, LN, ALU.min, ALU.subtract).then_inc(*tick("dve_step"))
                V.wait_ge(*now("dve_step"))
                V.tensor_tensor_scan(CUM, ONE8[:, :], GF, 0.0, ALU.mult, ALU.add).then_inc(*tick("dve_step"))
                V.wait_ge(*now("dve_step"))
                V.tensor_tensor(GM, IG, CUM, ALU.subtract).then_inc(*tick("dve_step"))
                V.wait_ge(*now("dve_step"))
                V.tensor_tensor_scan(MM, GM, GM, 0.0, ALU.max, ALU.max).then_inc(*tick("dve_step"))
                V.wait_ge(*now("dve_step"))
                V.tensor_scalar(NM, MM, -1.0, None, ALU.mult).then_inc(*tick("dve_step"))
                V.wait_ge(*now("dve_step"))
                V.scalar_tensor_tensor(NMT, CUM, -1.0, MM, ALU.mult, ALU.subtract).then_inc(*tick("gates_done"))
                V.wait_ge(*now("gates_done"))
                V.wait_ge(bank_free("gt"), turn("gt"))
                for i in range(MH + 1):
                    if i < MH:
                        h = i
                        V.wait_ge(bank_ready(f"s{h}"), turn(f"s{h}"))
                        b = result(f"s{h}")
                        V.wait_ge(bank_free(f"w{h}"), turn(f"w{h}"))
                        if h >= 2:
                            V.wait_ge(bank_ready(f"n{h - 2}"), turn(f"n{h - 2}"))
                        V.scalar_tensor_tensor(PT[h % 2][:, :], b[:, 0:384], MQK ** -0.5, WT[h % 2][:, :], ALU.mult, ALU.mult).then_inc(bank_free(f"s{h}"), 1)
                    if i >= 1:
                        h = i - 1
                        V.wait_ge(bank_ready(f"n{h}"), turn(f"n{h}"))
                        b = result(f"n{h}")
                        n2 = b[:, 0:2 * (MV + 1)].rearrange("p (t v) -> p t v", t=TT)
                        V.tensor_tensor(DN[:, h, :], n2[:, :, MV], EMS[:, :, h], ALU.max).then_inc(*tick("dve_step"))
                        V.wait_ge(*now("dve_step"))
                        V.scalar_tensor_tensor(DN[:, h, :], n2[:, :, MV], -1.0, DN[:, h, :], ALU.mult, ALU.max).then_inc(*tick("dve_step"))
                        V.wait_ge(*now("dve_step"))
                        V.reciprocal(DN[:, h, :], DN[:, h, :]).then_inc(*tick("dve_step"))
                        V.wait_ge(*now("dve_step"))
                        V.tensor_scalar(Y[:, 0, h * MV:(h + 1) * MV], n2[:, 0, 0:MV], DN[:, h, 0:1], None, ALU.mult).then_inc(*tick("dve_step"))
                        V.tensor_scalar(Y[:, 1, h * MV:(h + 1) * MV], n2[:, 1, 0:MV], DN[:, h, 1:2], None, ALU.mult).then_inc(bank_free(f"n{h}"), 1)
                V.wait_ge(bank_free(f"n{MH - 1}"), turn(f"n{MH - 1}"))
                yh = Y[:, :, :].rearrange("p t (h v) -> p (t h) v", v=MV)
                wide = lambda c: c[:, :].unsqueeze(2).broadcast_to([P, 16, MV])
                V.tensor_reduce(MU[:, :], yh, AX.X, ALU.add).then_inc(*tick("dve_step"))
                V.wait_ge(*now("dve_step"))
                V.tensor_scalar(MU[:, :], MU[:, :], 1.0 / MV, None, ALU.mult).then_inc(*tick("dve_step"))
                V.wait_ge(*now("dve_step"))
                V.tensor_tensor(yh, yh, wide(MU), ALU.subtract).then_inc(*tick("centred"))
                V.wait_ge(*now("centred"))
                V.wait_ge(*nth("h_sq", 1))
                V.tensor_reduce(VR[:, :], XT[:, :, :].rearrange("p k t -> p (k t)").rearrange("p (g v) -> p g v", v=MV), AX.X, ALU.add).then_inc(*tick("dve_step"))
                V.wait_ge(*now("dve_step"))
                V.tensor_scalar(VR[:, :], VR[:, :], 1.0 / MV, EPS1, ALU.mult, ALU.add).then_inc(*tick("h_var"))
                V.wait_ge(*now("h_var"))
                V.wait_ge(*nth("h_rstd", 1))
                V.tensor_tensor(yh, yh, wide(VR), ALU.mult).then_inc(*tick("dve_step"))
                V.wait_ge(*now("dve_step"))
                rows_here(0, 3)
                V.tensor_tensor(Y[:, :, :], Y[:, :, :], rows[0][:, 0:1, :].broadcast_to([P, TT, D]), ALU.mult).then_inc(*tick("dve_step"))
                V.wait_ge(*now("dve_step"))
                for name in [f"og{cb}{tt}" for cb in range(2) for tt in range(TT)]:
                    V.wait_ge(bank_free(name), turn(name))
                for tt in range(TT):
                    V.tensor_tensor(Y[:, tt, :], Y[:, tt, :], OG[:, tt, :], ALU.mult).then_inc(*tick("y_ready"))
                    V.wait_ge(*now("y_ready"))
                take_turn(V, "yt", XT, [(0, 1), (1, 1)])
                dve_residual("o", ALPHA)
                dve_layer_norm(Y, X, rows[0][:, 1, :], rows[0][:, 2, :], EPS1, "a_ln", "x_ready")

            @block.gpsimd
            def _(pool):
                load_rows(0, [a["a_hn_g"][0], a["ln_g"][0, 0], a["ln_b"][0, 0]])
                pool.wait_ge(S("first_in"), 48)
                pool_power("h_var", 1, "h_rstd", VR[:, :])
                pool_layer_norm("a_ln")

        def peer_route(block, st, l, IDX, GATE):
            QP = sb("QP", [P, 2 * PH, T], F32, st)
            KEYT = sb("KEYT", [P, 2 * PH, NK], F32, st)
            SC = sb("SC", [P, 2 * PH, NK], F32, st)
            CAND = SC[:, :, :].rearrange("p a b -> p (a b)").rearrange("p (h i j) -> p h i j", h=PH, i=TOPK)
            HOT = sb("HOT", [P, PICKS, TOPK], F32, st)
            TV = sb("TV", [P, 2 * PH, TOPK], F32, st)
            TI = sb("TI", [P, 2 * PH, TOPK], U32, st)
            TF = sb("TF", [P, 2 * PH, TOPK], F32, st)
            BV = sb("BV", [P, PH, TOPK], F32, st)
            BI = sb("BI", [P, PH, TOPK], U32, st)
            HALF = sb("HALF", [P, 2, PICKS], U32, st)
            HALFF = sb("HALFF", [P, 2, PICKS], F32, st)
            EX = sb("EX", [P, 2, PICKS], F32, st)
            SUM = sb("SUM", [P, PH], F32, st)

            @block.tensor
            def _(pe):
                pe.wait_ge(*landed(f"keys{l}"))
                w = slot_of(f"keys{l}")
                for g in range(4):
                    b = job(f"kt{g}")
                    if turn(f"kt{g}") > 1:
                        PE.wait_ge(bank_free(f"kt{g}"), turn(f"kt{g}") - 1)
                    for j in range(4):
                        last = tr(b[:, j * P:(j + 1) * P], w[:, 4 * g + j, :], ident)
                    last.then_inc(bank_ready(f"kt{g}"), 1)
                weight_read(f"keys{l}", "kt3")
                pe_turn(PE, "xt", X, None)
                pe.wait_ge(bank_free("xt00"), turn("xt00"))
                pe.wait_ge(bank_free("xt01"), turn("xt01"))
                pe.wait_ge(bank_free("xt10"), turn("xt10"))
                pe.wait_ge(bank_free("xt11"), turn("xt11"))
                for e in range(4):
                    pe.wait_ge(*landed(f"peer_q{l}_{e}"))
                    w = slot_of(f"peer_q{l}_{e}")
                    for i in range(2):
                        pe_colpair(PE, w, f"q{e}{i}", XT, [256 * i, 256 * i + 128])
                    weight_read(f"peer_q{l}_{e}", f"q{e}1")
                for tt in range(TT):
                    for g in range(4):
                        if tt == 0:
                            pe.wait_ge(bank_free(f"kt{g}"), turn(f"kt{g}"))
                            pe.wait_ge(bank_free(f"q{g}0"), turn(f"q{g}0"))
                            pe.wait_ge(bank_free(f"q{g}1"), turn(f"q{g}1"))
                        b = job(f"s{tt}{g}")
                        if turn(f"s{tt}{g}") > 1:
                            PE.wait_ge(bank_free(f"s{tt}{g}"), turn(f"s{tt}{g}") - 1)
                        for j in range(4):
                            last = mul(b[:, j * P:(j + 1) * P], QP[:, 4 * g + j, tt * P:(tt + 1) * P], KEYT[:, 4 * g + j, :], True, True)
                        last.then_inc(bank_ready(f"s{tt}{g}"), 1)

            @block.scalar
            def _(act):
                for g in range(4):
                    A.wait_ge(bank_ready(f"kt{g}"), turn(f"kt{g}"))
                    b = result(f"kt{g}")
                    copy(A, KEYT[:, 4 * g:4 * g + 4, :], b[:, :].rearrange("p (k n) -> p k n", k=4)).then_inc(bank_free(f"kt{g}"), 1)
                take_turn(A, "xt", XT, [(0, 0), (1, 0)])
                for e in range(4):
                    for i in range(2):
                        A.wait_ge(bank_ready(f"q{e}{i}"), turn(f"q{e}{i}"))
                        b = result(f"q{e}{i}")
                        copy(A, QP[:, 4 * e + 2 * i:4 * e + 2 * i + 2, :], pair(b)).then_inc(bank_free(f"q{e}{i}"), 1)
                for tt in range(TT):
                    A.wait_ge(*nth("top_shifted", tt + 1))
                    A.activation(GATE[:, tt, :], GATE[:, tt, :], ACT.Exp).then_inc(*tick("gate_exp"))
                    A.wait_ge(*now("gate_exp"))

            @block.vector
            def _(dve):
                def top16(values, vals, idxs, n):
                    for k in range(n):
                        V.max(vals[:, k, 0:8], values(k)).then_inc(*tick("dve_step"))
                    V.memset(stat[:, 63:64], 0.0).then_inc(*tick("dve_step"))
                    V.wait_ge(*now("dve_step"))
                    for k in range(n):
                        V.max_index(idxs[:, k, 0:8], vals[:, k, 0:8], values(k)).then_inc(*tick("dve_step"))
                    for k in range(n):
                        V.match_replace(values(k), vals[:, k, 0:8], values(k), FLOOR).then_inc(*tick("dve_step"))
                    V.memset(stat[:, 63:64], 0.0).then_inc(*tick("dve_step"))
                    V.wait_ge(*now("dve_step"))
                    for k in range(n):
                        V.max(vals[:, k, 8:16], values(k)).then_inc(*tick("dve_step"))
                    V.memset(stat[:, 63:64], 0.0).then_inc(*tick("dve_step"))
                    V.wait_ge(*now("dve_step"))
                    for k in range(n):
                        V.max_index(idxs[:, k, 8:16], vals[:, k, 8:16], values(k)).then_inc(*tick("dve_step"))
                    V.memset(stat[:, 63:64], 0.0).then_inc(*tick("dve_step"))
                    V.wait_ge(*now("dve_step"))

                take_turn(V, "xt", XT, [(0, 1), (1, 1)])
                for tt in range(TT):
                    for g in range(4):
                        V.wait_ge(bank_ready(f"s{tt}{g}"), turn(f"s{tt}{g}"))
                        b = result(f"s{tt}{g}")
                        copy(V, SC[:, 4 * g:4 * g + 4, :], b[:, :].rearrange("p (k n) -> p k n", k=4)).then_inc(bank_free(f"s{tt}{g}"), 1)
                    for name in [f"s{tt}{g}" for g in range(4)]:
                        V.wait_ge(bank_free(name), turn(name))
                    top16(lambda k: SC[:, k, :], TV, TI, 2 * PH)
                    V.tensor_copy(TF[:, :, :], TI[:, :, :]).then_inc(*tick("dve_step"))
                    V.wait_ge(*now("dve_step"))
                    tv = TV[:, :, :].rearrange("p (h c) k -> p h c k", c=2)
                    V.tensor_tensor(CAND, tv[:, :, 0, :].unsqueeze(3).broadcast_to([P, PH, TOPK, TOPK]),
                                          tv[:, :, 1, :].unsqueeze(2).broadcast_to([P, PH, TOPK, TOPK]), ALU.add).then_inc(*tick("dve_step"))
                    V.wait_ge(*now("dve_step"))
                    top16(lambda h: CAND[:, h, :, :].rearrange("p i j -> p (i j)"), BV, BI, PH)
                    g3 = GATE[:, tt, :].rearrange("p (h k) -> p h k", h=PH)
                    V.tensor_tensor(g3, BV[:, :, :], BV[:, :, 0:1].broadcast_to([P, PH, TOPK]), ALU.subtract).then_inc(*tick("top_shifted"))
                    V.wait_ge(*now("top_shifted"))
                    bi = BI[:, :, :].rearrange("p h k -> p (h k)")
                    V.tensor_scalar(HALF[:, 0, :], bi, 4, None, ALU.logical_shift_right).then_inc(*tick("dve_step"))
                    V.tensor_scalar(HALF[:, 1, :], bi, TOPK - 1, None, ALU.bitwise_and).then_inc(*tick("dve_step"))
                    V.wait_ge(*now("dve_step"))
                    V.tensor_copy(HALFF[:, :, :], HALF[:, :, :]).then_inc(*tick("dve_step"))
                    V.wait_ge(*now("dve_step"))
                    tf = TF[:, :, :].rearrange("p (h c) k -> p h c k", c=2)
                    at16, _ = cwhere["i16"]
                    for c in range(2):
                        V.tensor_tensor(HOT[:, :, :], HALFF[:, c, :].unsqueeze(2).broadcast_to([P, PICKS, TOPK]),
                                              CN[:, at16:at16 + TOPK].unsqueeze(1).broadcast_to([P, PICKS, TOPK]), ALU.is_equal).then_inc(*tick("dve_step"))
                        V.wait_ge(*now("dve_step"))
                        hot4 = HOT[:, :, :].rearrange("p (h k) j -> p h k j", h=PH)
                        V.tensor_tensor(hot4, hot4, tf[:, :, c, :].unsqueeze(2).broadcast_to([P, PH, TOPK, TOPK]), ALU.mult).then_inc(*tick("dve_step"))
                        V.wait_ge(*now("dve_step"))
                        V.tensor_reduce(EX[:, c, :], HOT[:, :, :], AX.X, ALU.add).then_inc(*tick("dve_step"))
                        V.wait_ge(*now("dve_step"))
                    V.scalar_tensor_tensor(EX[:, 0, :], EX[:, 0, :], float(NK), EX[:, 1, :], ALU.mult, ALU.add).then_inc(*tick("dve_step"))
                    V.wait_ge(*now("dve_step"))
                    V.tensor_scalar(IDX[:, tt, :], EX[:, 0, :], float(l * NEXP), None, ALU.add).then_inc(*tick("dve_step"))
                    V.wait_ge(*now("dve_step"))
                    V.wait_ge(*nth("gate_exp", tt + 1))
                    V.tensor_reduce(SUM[:, :], g3, AX.X, ALU.add).then_inc(*tick("dve_step"))
                    V.wait_ge(*now("dve_step"))
                    V.reciprocal(SUM[:, :], SUM[:, :]).then_inc(*tick("dve_step"))
                    V.wait_ge(*now("dve_step"))
                    V.tensor_tensor(g3, g3, SUM[:, :].unsqueeze(2).broadcast_to([P, PH, TOPK]), ALU.mult).then_inc(*tick("dve_step"))
                    V.wait_ge(*now("dve_step"))

        gather_base = {"row_used": 0, "cur": 0, "row_in": 0, "kept": 0}

        def peer_gather(block, st, l, IDX, GATE):
            ROWBUF = [sb(f"ROW{s}", [P, D], F32, st) for s in range(SLOTS)]
            CUR = [sb(f"CUR{i}", [P, SLOTS], I32, st) for i in range(2)]
            DOT = sb("DOT", [P, 2 * SLOTS], F32, st)
            ACTV = sb("ACTV", [P, TT, PICKS], F32, st)
            u = a["peer_u"].rearrange("l e d -> (l e) d")
            v = a["peer_v"].rearrange("l e d -> (l e) d")
            STEP = 2 * SLOTS
            passes = [(tab, tt) for tab in (u, v) for tt in range(TT)]
            row_in = [S(f"row_in{s}") for s in range(SLOTS)]
            row_used, cur_ready, pick_go, kept = S("row_used"), S("cur_ready"), S("pick_go"), S("dots_kept")
            g0 = dict(gather_base)

            @block.gpsimd
            def _(pool):
                load_rows(1, [a["ln_g"][l, 1], a["ln_b"][l, 1]])
                for n, (tab, tt) in enumerate(passes):
                    used0 = g0["row_used"] + n * PICKS
                    cur0 = g0["cur"] + n * (PICKS // SLOTS)
                    with pool.Fori(0, PICKS // STEP) as i:
                        for half in range(2):
                            nc.gpsimd.tensor_copy(CUR[half][:, :], IDX[:, tt, bass.ds(i * STEP + half * SLOTS, SLOTS)]).then_inc(cur_ready, 1)
                            pool.wait_ge(cur_ready, i * 2 + (cur0 + half + 1))
                            pool.sem_inc(pick_go, 1)
                            for s in range(SLOTS):
                                if s % 2 == 0:
                                    pool.wait_ge(row_used, i * STEP + (used0 + half * SLOTS + s + 2))
                                    pool.sem_inc(pick_go, 1)
                                nc.gpsimd.indirect_dma_start(ROWBUF[s][:, :], None, tab, bass.IndirectOffsetOnAxis(CUR[half][:, s:s + 1], axis=0)).then_inc(row_in[s], 16)

            @block.vector
            def _(dve):
                if l == 0:
                    dve.sem_inc(row_used, SLOTS)
                for n, (tab, tt) in enumerate(passes[:TT]):
                    used0 = g0["row_used"] + n * PICKS + SLOTS
                    in0 = g0["row_in"] + n * (PICKS // SLOTS)
                    kept0 = g0["kept"] + n * (PICKS // STEP)
                    with dve.Fori(0, PICKS // STEP) as i:
                        for s in range(STEP):
                            r = s % SLOTS
                            dve.wait_ge(row_in[r], i * 32 + 16 * (in0 + s // SLOTS + 1))
                            nc.vector.scalar_tensor_tensor(ROWBUF[r][:, :], ROWBUF[r][:, :], 1.0, X[:, tt, :], ALU.mult, ALU.mult,
                                                           accum_out=DOT[:, s:s + 1]).then_inc(row_used, 1)
                        dve.wait_ge(row_used, i * STEP + (used0 + STEP))
                        nc.vector.tensor_copy(ACTV[:, tt, bass.ds(i * STEP, STEP)], DOT[:, :]).then_inc(kept, 1)
                        dve.wait_ge(kept, i + (kept0 + 1))
                for tt in range(TT):
                    V.tensor_scalar(Y[:, tt, :], X[:, tt, :], ALPHA, None, ALU.mult).then_inc(*tick("dots_done"))
                    V.wait_ge(*now("dots_done"))
                V.wait_ge(*nth("gelu_done", TT))
                V.tensor_tensor(GATE[:, :, :], GATE[:, :, :], ACTV[:, :, :], ALU.mult).then_inc(*tick("dve_step"))
                V.wait_ge(*now("dve_step"))
                for n, (tab, tt) in list(enumerate(passes))[TT:]:
                    used0 = g0["row_used"] + n * PICKS + SLOTS
                    in0 = g0["row_in"] + n * (PICKS // SLOTS)
                    with dve.Fori(0, PICKS // STEP) as i:
                        for s in range(STEP):
                            r = s % SLOTS
                            dve.wait_ge(row_used, i * STEP + (used0 + s))
                            dve.wait_ge(row_in[r], i * 32 + 16 * (in0 + s // SLOTS + 1))
                            nc.vector.scalar_tensor_tensor(Y[:, tt, :], ROWBUF[r][:, :], GATE[:, tt, bass.ds(i * STEP + s, 1)], Y[:, tt, :],
                                                           ALU.mult, ALU.add).then_inc(row_used, 1)
                dve.wait_ge(row_used, g0["row_used"] + len(passes) * PICKS + SLOTS)
                rows_here(1, 2)
                dve_layer_norm(Y, X, rows[1][:, 0, :], rows[1][:, 1, :], EPS1, f"p_ln", "x_ready")

            @block.scalar
            def _(act):
                for tt in range(TT):
                    A.wait_ge(*nth("dots_done", TT))
                    A.activation(ACTV[:, tt, :], ACTV[:, tt, :], ACT.Gelu).then_inc(*tick("gelu_done"))
                    A.wait_ge(*now("gelu_done"))

            block.gpsimd(lambda pool: pool_layer_norm("p_ln"))
            gather_base["row_used"] += len(passes) * PICKS
            gather_base["cur"] += len(passes) * (PICKS // SLOTS)
            gather_base["row_in"] += len(passes) * (PICKS // SLOTS)
            gather_base["kept"] += TT * (PICKS // STEP)

        def embed(block, st, src, gate_key, proj_key, which, before=None):
            SG = sb("SG", [P, TT, D], F32, st)
            PTT = sb("PTT", [P, 2, T], F32, st)

            @block.tensor
            def _(pe):
                params_here(pe)
                for tt in range(TT):
                    b = job(f"pt{tt}")
                    if turn(f"pt{tt}") > 1:
                        PE.wait_ge(bank_free(f"pt{tt}"), turn(f"pt{tt}") - 1)
                    for j in range(2):
                        last = tr(b[:, j * P:(j + 1) * P], PIN[:, which, tt, j * P:(j + 1) * P], ident)
                    last.then_inc(bank_ready(f"pt{tt}"), 1)
                pe_turn(PE, "xt", src, "h_ready" if before else None)
                pe.wait_ge(bank_free("xt00"), turn("xt00"))
                pe.wait_ge(bank_free("xt01"), turn("xt01"))
                pe.wait_ge(bank_free("xt10"), turn("xt10"))
                pe.wait_ge(bank_free("xt11"), turn("xt11"))
                pe.wait_ge(bank_free("pt0"), turn("pt0"))
                pe.wait_ge(bank_free("pt1"), turn("pt1"))
                for cb in range(2):
                    pe.wait_ge(*landed(f"{gate_key}{cb}"))
                    w = slot_of(f"{gate_key}{cb}")
                    for tt in range(TT):
                        pe_rows(PE, w, f"g{cb}{tt}", XT, tt, 0, 512)
                    weight_read(f"{gate_key}{cb}", f"g{cb}1")
                pe.wait_ge(*landed(proj_key))
                w = slot_of(proj_key)
                for cb in range(2):
                    for tt in range(TT):
                        pe_rows(PE, w, f"p{cb}{tt}", PTT, tt, cb * 512, 512)
                weight_read(proj_key, "p11")

            @block.scalar
            def _(act):
                for tt in range(TT):
                    A.wait_ge(bank_ready(f"pt{tt}"), turn(f"pt{tt}"))
                    b = result(f"pt{tt}")
                    copy(A, PTT[:, :, tt * P:(tt + 1) * P], b[:, 0:T].rearrange("p (k t) -> p k t", k=2)).then_inc(bank_free(f"pt{tt}"), 1)
                if before:
                    before[0]()
                take_turn(A, "xt", XT, [(0, 0), (1, 0)])
                for cb in range(2):
                    for tt in range(TT):
                        A.wait_ge(bank_ready(f"g{cb}{tt}"), turn(f"g{cb}{tt}"))
                        b = result(f"g{cb}{tt}")
                        A.activation(SG[:, tt, cb * 512:cb * 512 + 512], b[:, :], ACT.Sigmoid).then_inc(bank_free(f"g{cb}{tt}"), 1)

            @block.vector
            def _(dve):
                if before:
                    before[1]()
                take_turn(V, "xt", XT, [(0, 1), (1, 1)])
                for cb in range(2):
                    for tt in range(TT):
                        s = slice(cb * 512, cb * 512 + 512)
                        V.wait_ge(bank_ready(f"p{cb}{tt}"), turn(f"p{cb}{tt}"))
                        b = result(f"p{cb}{tt}")
                        V.wait_ge(bank_free(f"g{cb}{tt}"), turn(f"g{cb}{tt}"))
                        V.tensor_tensor(SG[:, tt, s], b[:, :], SG[:, tt, s], ALU.mult).then_inc(bank_free(f"p{cb}{tt}"), 1)
                V.wait_ge(bank_free("p00"), turn("p00"))
                V.wait_ge(bank_free("p01"), turn("p01"))
                V.wait_ge(bank_free("p10"), turn("p10"))
                V.wait_ge(bank_free("p11"), turn("p11"))
                for tt in range(TT):
                    V.tensor_tensor(X[:, tt, :], X[:, tt, :], SG[:, tt, :], ALU.add).then_inc(*tick("x_ready"))
                    V.wait_ge(*now("x_ready"))

        def mla(block, st):
            CK = sb("CK", [P, TT, KVR + ROPE], F32, st)
            CQ = sb("CQ", [P, TT, QR], F32, st)
            JUNK = sb("JUNK", [P, TT, QR], F32, st)
            MS = sb("MS", [P, 2 * TT], F32, st)
            CKT = sb("CKT", [P, KVR // P, T], F32, st)
            CQT = sb("CQT", [P, QR // P, T], F32, st)
            KRT = sb("KRT", [ROPE, T], F32, st)
            KNT = sb("KNT", [P, AH, T], F32, st)
            VM = sb("VM", [P, TT, AH * AV], F32, st)
            QNT = sb("QNT", [P, AH, T], F32, st)
            QRR = sb("QRR", [P, TT, AH, ROPE], F32, st)
            QRT = sb("QRT", [ROPE, AH, T], F32, st)
            KRR = sb("KRR", [P, TT, 1, ROPE], F32, st)
            HR = ROPE // 2
            ANG = sb("ANG", [P, 2, TT, HR], F32, st)
            TURN = sb("TURN", [P, TT, HR], F32, st)
            TRIG = sb("TRIG", [P, 2, TT, HR], F32, st)
            RT = sb("RT", [P, 4, AH, HR], F32, st)
            PR = [sb(f"PR{i}", [P, 384], F32, st) for i in range(2)]
            PRT = [sb(f"PRT{i}", [P, 384], F32, st) for i in range(2)]
            MX = sb("MX", [P, AH, TT], F32, st)
            SM = sb("SM", [P, AH, TT], F32, st)
            RS = sb("RS", [P, AH, TT], F32, st)
            POSF = sb("POSF", [P, TT], F32, st)
            scale = (NOPE + ROPE) ** -0.5

            @block.tensor
            def _(pe):
                pe_turn(PE, "xt", X, None)
                pe.wait_ge(bank_free("xt00"), turn("xt00"))
                pe.wait_ge(bank_free("xt01"), turn("xt01"))
                pe.wait_ge(bank_free("xt10"), turn("xt10"))
                pe.wait_ge(bank_free("xt11"), turn("xt11"))
                for key, name, n in (("kv_down", "ck", KVR + ROPE), ("dq", "cq", QR)):
                    pe.wait_ge(*landed(key))
                    w = slot_of(key)
                    for tt in range(TT):
                        pe_rows(PE, w, f"{name}{tt}", XT, tt, 0, n)
                    weight_read(key, f"{name}1")
                for tt in range(TT):
                    pe.wait_ge(*nth("latents_ready", tt + 1))
                    b = job(f"ckt{tt}")
                    if turn(f"ckt{tt}") > 1:
                        PE.wait_ge(bank_free(f"ckt{tt}"), turn(f"ckt{tt}") - 1)
                    for j in range(KVR // P):
                        tr(b[:, j * P:(j + 1) * P], CK[:, tt, j * P:(j + 1) * P], ident)
                    tr(b[0:ROPE, KVR:KVR + P], KRR[:, tt, 0, :], ident).then_inc(bank_ready(f"ckt{tt}"), 1)
                    b = job(f"cqt{tt}")
                    if turn(f"cqt{tt}") > 1:
                        PE.wait_ge(bank_free(f"cqt{tt}"), turn(f"cqt{tt}") - 1)
                    for j in range(QR // P):
                        last = tr(b[:, j * P:(j + 1) * P], CQ[:, tt, j * P:(j + 1) * P], ident)
                    last.then_inc(bank_ready(f"cqt{tt}"), 1)
                pe.wait_ge(bank_free("ckt0"), turn("ckt0"))
                pe.wait_ge(bank_free("ckt1"), turn("ckt1"))
                pe.wait_ge(bank_free("cqt0"), turn("cqt0"))
                pe.wait_ge(bank_free("cqt1"), turn("cqt1"))
                pe.wait_ge(*landed("kv_up"))
                w = slot_of("kv_up")
                for i in range(AH // 2):
                    pe_colpair(PE, w, f"kn{i}", CKT, [512 * i, 512 * i + 256])
                wh = w.rearrange("p k (h c) -> p k h c", h=AH)
                for hb in range(2):
                    for tt in range(TT):
                        b = job(f"vv{hb}{tt}")
                        if turn(f"vv{hb}{tt}") > 1:
                            PE.wait_ge(bank_free(f"vv{hb}{tt}"), turn(f"vv{hb}{tt}") - 1)
                        for k in range(KVR // P):
                            last = mul(b[:, :], CKT[:, k, tt * P:(tt + 1) * P], wh[:, k, 4 * hb:4 * hb + 4, NOPE:NOPE + AV], k == 0, k == 1)
                        last.then_inc(bank_ready(f"vv{hb}{tt}"), 1)
                weight_read("kv_up", "vv11")
                for e in range(2):
                    pe.wait_ge(*landed(f"uq{e}"))
                    w = slot_of(f"uq{e}")
                    wh = w.rearrange("p k (h c) -> p k h c", h=4)
                    for tt in range(TT):
                        b = job(f"qr{e}{tt}")
                        if turn(f"qr{e}{tt}") > 1:
                            PE.wait_ge(bank_free(f"qr{e}{tt}"), turn(f"qr{e}{tt}") - 1)
                        for k in range(QR // P):
                            last = mul(b[:, 0:4 * ROPE], CQT[:, k, tt * P:(tt + 1) * P], wh[:, k, :, NOPE:NOPE + ROPE], k == 0, k == 2)
                        last.then_inc(bank_ready(f"qr{e}{tt}"), 1)
                    for i in range(2):
                        pe_colpair(PE, w, f"qn{e}{i}", CQT, [384 * i, 384 * i + 192])
                    weight_read(f"uq{e}", f"qn{e}1")
                for e in range(2):
                    for tt in range(TT):
                        pe.wait_ge(*nth("q_rotated", 2 * e + tt + 1))
                        b = job(f"qrt{e}{tt}")
                        if turn(f"qrt{e}{tt}") > 1:
                            PE.wait_ge(bank_free(f"qrt{e}{tt}"), turn(f"qrt{e}{tt}") - 1)
                        for j in range(4):
                            last = tr(b[0:ROPE, j * P:(j + 1) * P], QRR[:, tt, 4 * e + j, :], ident)
                        last.then_inc(bank_ready(f"qrt{e}{tt}"), 1)
                for name in [f"kn{i}" for i in range(4)]:
                    pe.wait_ge(bank_free(name), turn(name))
                for name in [f"qn{e}{i}" for e in range(2) for i in range(2)]:
                    pe.wait_ge(bank_free(name), turn(name))
                for name in [f"qrt{e}{tt}" for e in range(2) for tt in range(TT)]:
                    pe.wait_ge(bank_free(name), turn(name))
                for i in range(AH + 2):
                    if i < AH:
                        h = i
                        b = job(f"s{h}")
                        if turn(f"s{h}") > 1:
                            PE.wait_ge(bank_free(f"s{h}"), turn(f"s{h}") - 1)
                        for tt, o, n in ((0, 0, P), (1, P, T)):
                            q = slice(tt * P, (tt + 1) * P)
                            mul(b[:, o:o + n], QNT[:, h, q], KNT[:, h, 0:n], True, False)
                            mul(b[:, o:o + n], QRT[:, h, q], KRT[:, 0:n], False, False)
                            last = mul(b[:, o + n - P:o + n], ident, con("mask_q"), False, True)
                        last.then_inc(bank_ready(f"s{h}"), 1)
                    if 1 <= i <= AH:
                        h = i - 1
                        pe.wait_ge(bank_free(f"s{h}"), turn(f"s{h}"))
                        b = job(f"t{h}")
                        if turn(f"t{h}") > 1:
                            PE.wait_ge(bank_free(f"t{h}"), turn(f"t{h}") - 1)
                        for j in range(3):
                            last = tr(b[:, j * P:(j + 1) * P], PR[h % 2][:, j * P:(j + 1) * P], ident)
                        last.then_inc(bank_ready(f"t{h}"), 1)
                    if i >= 2:
                        h = i - 2
                        if h == 0:
                            pe.wait_ge(bank_free("vv00"), turn("vv00"))
                            pe.wait_ge(bank_free("vv01"), turn("vv01"))
                            pe.wait_ge(bank_free("vv10"), turn("vv10"))
                            pe.wait_ge(bank_free("vv11"), turn("vv11"))
                        pe.wait_ge(bank_free(f"t{h}"), turn(f"t{h}"))
                        b = job(f"o{h}")
                        if turn(f"o{h}") > 1:
                            PE.wait_ge(bank_free(f"o{h}"), turn(f"o{h}") - 1)
                        v = slice(h * AV, (h + 1) * AV)
                        mul(b[:, 0:AV], PRT[h % 2][:, 0:P], VM[:, 0, v], True, True)
                        mul(b[:, AV:2 * AV], PRT[h % 2][:, P:2 * P], VM[:, 0, v], True, False)
                        mul(b[:, AV:2 * AV], PRT[h % 2][:, 2 * P:3 * P], VM[:, 1, v], False, True).then_inc(bank_ready(f"o{h}"), 1)
                pe_turn(PE, "yt", Y, "y_ready")
                pe.wait_ge(bank_free("yt00"), turn("yt00"))
                pe.wait_ge(bank_free("yt01"), turn("yt01"))
                pe.wait_ge(bank_free("yt10"), turn("yt10"))
                pe.wait_ge(bank_free("yt11"), turn("yt11"))
                for cb in range(2):
                    pe.wait_ge(*landed(f"b_out{cb}"))
                    w = slot_of(f"b_out{cb}")
                    for tt in range(TT):
                        pe_rows(PE, w, f"m{cb}{tt}", XT, tt, 0, 512)
                    weight_read(f"b_out{cb}", f"m{cb}1")

            @block.scalar
            def _(act):
                take_turn(A, "xt", XT, [(0, 0), (1, 0)])
                A.wait_ge(*nth("angles", 1))
                A.activation(TRIG[:, :, :, :], ANG[:, :, :, :], ACT.Sin).then_inc(*tick("trig"))
                A.wait_ge(*now("trig"))
                for i, (c, n) in enumerate((("ck", KVR), ("cq", QR))):
                    src = CK if i == 0 else CQ
                    A.wait_ge(bank_free(f"{c}0"), turn(f"{c}0"))
                    A.wait_ge(bank_free(f"{c}1"), turn(f"{c}1"))
                    for tt in range(TT):
                        if i == 0:
                            A.activation(JUNK[:, tt, 0:n], src[:, tt, 0:n], ACT.Square, accum_out=MS[:, tt:tt + 1]).then_inc(*tick("latent_sq"))
                            A.wait_ge(*now("latent_sq"))
                        else:
                            A.activation(JUNK[:, tt, 0:n], src[:, tt, 0:n], ACT.Square, accum_out=MS[:, 2 + tt:3 + tt]).then_inc(*tick("latent_sq"))
                            A.wait_ge(*now("latent_sq"))
                for tt in range(TT):
                    t = slice(tt * P, (tt + 1) * P)
                    A.wait_ge(bank_ready(f"ckt{tt}"), turn(f"ckt{tt}"))
                    b = result(f"ckt{tt}")
                    copy(A, CKT[:, :, t], b[:, 0:KVR].rearrange("p (k t) -> p k t", k=2)).then_inc(*tick("act_step"))
                    copy(A, KRT[:, t], b[0:ROPE, KVR:KVR + P]).then_inc(bank_free(f"ckt{tt}"), 1)
                    A.wait_ge(bank_ready(f"cqt{tt}"), turn(f"cqt{tt}"))
                    b = result(f"cqt{tt}")
                    copy(A, CQT[:, :, t], b[:, 0:QR].rearrange("p (k t) -> p k t", k=3)).then_inc(bank_free(f"cqt{tt}"), 1)
                for i in range(AH // 2):
                    A.wait_ge(bank_ready(f"kn{i}"), turn(f"kn{i}"))
                    b = result(f"kn{i}")
                    copy(A, KNT[:, 2 * i:2 * i + 2, :], pair(b)).then_inc(bank_free(f"kn{i}"), 1)
                for hb in range(2):
                    for tt in range(TT):
                        A.wait_ge(bank_ready(f"vv{hb}{tt}"), turn(f"vv{hb}{tt}"))
                        b = result(f"vv{hb}{tt}")
                        copy(A, VM[:, tt, hb * 512:hb * 512 + 512], b[:, :]).then_inc(bank_free(f"vv{hb}{tt}"), 1)
                for e in range(2):
                    for i in range(2):
                        A.wait_ge(bank_ready(f"qn{e}{i}"), turn(f"qn{e}{i}"))
                        b = result(f"qn{e}{i}")
                        copy(A, QNT[:, 4 * e + 2 * i:4 * e + 2 * i + 2, :], pair(b)).then_inc(bank_free(f"qn{e}{i}"), 1)
                for e in range(2):
                    for tt in range(TT):
                        A.wait_ge(bank_ready(f"qrt{e}{tt}"), turn(f"qrt{e}{tt}"))
                        b = result(f"qrt{e}{tt}")
                        copy(A, QRT[:, 4 * e:4 * e + 4, tt * P:(tt + 1) * P], b[0:ROPE, :].rearrange("p (h t) -> p h t", h=4)).then_inc(bank_free(f"qrt{e}{tt}"), 1)
                for h in range(AH):
                    A.wait_ge(bank_ready(f"s{h}"), turn(f"s{h}"))
                    b = result(f"s{h}")
                    A.wait_ge(*nth("max_ready", h + 1))
                    if h >= 2:
                        A.wait_ge(bank_ready(f"t{h - 2}"), turn(f"t{h - 2}"))
                    A.activation(PR[h % 2][:, 0:P], b[:, 0:P], ACT.Exp, bias=MX[:, h, 0:1], scale=scale, accum_out=SM[:, h, 0:1]).then_inc(*tick("act_step"))
                    A.activation(PR[h % 2][:, P:3 * P], b[:, P:3 * P], ACT.Exp, bias=MX[:, h, 1:2], scale=scale, accum_out=SM[:, h, 1:2]).then_inc(bank_free(f"s{h}"), 1)
                take_turn(A, "yt", XT, [(0, 0), (1, 0)])

            @block.vector
            def _(dve):
                params_here(dve)
                V.tensor_copy(POSF[:, :], POS[:, :]).then_inc(*tick("dve_step"))
                V.wait_ge(*now("dve_step"))
                for tt in range(TT):
                    V.tensor_scalar(ANG[:, 0, tt, :], con("freq"), POSF[:, tt:tt + 1], None, ALU.mult).then_inc(*tick("dve_step"))
                V.memset(stat[:, 63:64], 0.0).then_inc(*tick("dve_step"))
                V.wait_ge(*now("dve_step"))
                magic, tau = 1.5 * 2.0 ** 23, 2.0 * math.pi
                hi = 6.28125
                mid = math.floor((tau - hi) * 2.0 ** 20) / 2.0 ** 20
                lo = tau - hi - mid
                V.tensor_scalar(TURN[:, :, :], ANG[:, 0, :, :], 1.0 / tau, magic, ALU.mult, ALU.add).then_inc(*tick("dve_step"))
                V.wait_ge(*now("dve_step"))
                V.tensor_scalar(TURN[:, :, :], TURN[:, :, :], magic, None, ALU.subtract).then_inc(*tick("dve_step"))
                V.wait_ge(*now("dve_step"))
                for part in (hi, mid, lo):
                    V.scalar_tensor_tensor(ANG[:, 0, :, :], TURN[:, :, :], -part, ANG[:, 0, :, :], ALU.mult, ALU.add).then_inc(*tick("dve_step"))
                    V.wait_ge(*now("dve_step"))
                V.tensor_scalar(ANG[:, 1, :, :], ANG[:, 0, :, :], 0.5 * math.pi, None, ALU.add).then_inc(*tick("dve_step"))
                V.wait_ge(*now("dve_step"))
                V.tensor_scalar(TURN[:, :, :], ANG[:, 1, :, :], math.pi, -tau, ALU.is_gt, ALU.mult).then_inc(*tick("dve_step"))
                V.wait_ge(*now("dve_step"))
                V.tensor_tensor(ANG[:, 1, :, :], ANG[:, 1, :, :], TURN[:, :, :], ALU.add).then_inc(*tick("dve_step"))
                V.wait_ge(*now("dve_step"))
                V.tensor_scalar(ANG[:, :, :, :], ANG[:, :, :, :], 3.1415925, -3.1415925, ALU.min, ALU.max).then_inc(*tick("angles"))
                V.wait_ge(*now("angles"))

                take_turn(V, "xt", XT, [(0, 1), (1, 1)])
                for tt in range(TT):
                    V.wait_ge(bank_ready(f"ck{tt}"), turn(f"ck{tt}"))
                    b = result(f"ck{tt}")
                    copy(V, CK[:, tt, :], b[:, 0:KVR + ROPE]).then_inc(bank_free(f"ck{tt}"), 1)
                for tt in range(TT):
                    V.wait_ge(bank_ready(f"cq{tt}"), turn(f"cq{tt}"))
                    b = result(f"cq{tt}")
                    copy(V, CQ[:, tt, :], b[:, 0:QR]).then_inc(bank_free(f"cq{tt}"), 1)
                V.wait_ge(bank_free("ck0"), turn("ck0"))
                V.wait_ge(bank_free("ck1"), turn("ck1"))
                V.wait_ge(bank_free("cq0"), turn("cq0"))
                V.wait_ge(bank_free("cq1"), turn("cq1"))

                def rotate(dst, src, tt, last):
                    n = src.shape[1]
                    wide = lambda f: TRIG[:, f, tt, :].unsqueeze(1).broadcast_to([P, n, HR])
                    sin, cos = wide(0), wide(1)
                    x1, x2 = src[:, :, 0:HR], src[:, :, HR:ROPE]
                    r = RT[:, :, 0:n, :]
                    V.tensor_tensor(r[:, 0], x1, cos, ALU.mult).then_inc(*tick("dve_step"))
                    V.tensor_tensor(r[:, 1], x2, sin, ALU.mult).then_inc(*tick("dve_step"))
                    V.tensor_tensor(r[:, 2], x1, sin, ALU.mult).then_inc(*tick("dve_step"))
                    last(V.tensor_tensor(r[:, 3], x2, cos, ALU.mult))
                    V.tensor_tensor(dst[:, :, 0:HR], r[:, 0], r[:, 1], ALU.subtract).then_inc(*tick("dve_step"))
                    V.wait_ge(*now("dve_step"))
                    return V.tensor_tensor(dst[:, :, HR:ROPE], r[:, 2], r[:, 3], ALU.add)

                V.wait_ge(*nth("trig", 1))
                for tt in range(TT):
                    def products_made(ins):
                        ins.then_inc(*tick("dve_step"))
                        V.wait_ge(*now("dve_step"))
                    rotate(KRR[:, tt], CK[:, tt, KVR:KVR + ROPE].unsqueeze(1), tt, products_made).then_inc(*tick("dve_step"))
                    V.wait_ge(*now("dve_step"))
                V.wait_ge(*nth("latent_sq", 2 * TT))
                V.tensor_scalar(MS[:, 0:2], MS[:, 0:2], 1.0 / KVR, EPS1, ALU.mult, ALU.add).then_inc(*tick("dve_step"))
                V.tensor_scalar(MS[:, 2:4], MS[:, 2:4], 1.0 / QR, EPS1, ALU.mult, ALU.add).then_inc(*tick("latent_var"))
                V.wait_ge(*now("latent_var"))
                V.wait_ge(*nth("latent_rstd", 1))
                for tt in range(TT):
                    V.scalar_tensor_tensor(CK[:, tt, 0:KVR], CK[:, tt, 0:KVR], MS[:, tt:tt + 1], small("kv_norm_g"), ALU.mult, ALU.mult).then_inc(*tick("dve_step"))
                    V.wait_ge(*now("dve_step"))
                    V.scalar_tensor_tensor(CQ[:, tt, :], CQ[:, tt, :], MS[:, 2 + tt:3 + tt], small("b_q_norm_g"), ALU.mult, ALU.mult).then_inc(*tick("latents_ready"))
                    V.wait_ge(*now("latents_ready"))
                for e in range(2):
                    for tt in range(TT):
                        V.wait_ge(bank_ready(f"qr{e}{tt}"), turn(f"qr{e}{tt}"))
                        b = result(f"qr{e}{tt}")
                        src = b[:, 0:4 * ROPE].rearrange("p (h r) -> p h r", h=4)
                        name = f"qr{e}{tt}"

                        def last(ins):
                            ins.then_inc(bank_free(name), 1)
                            V.wait_ge(bank_free(name), turn(name))

                        rotate(QRR[:, tt, 4 * e:4 * e + 4, :], src, tt, last).then_inc(*tick("q_rotated"))
                        V.wait_ge(*now("q_rotated"))
                for i in range(AH + 2):
                    if i < AH:
                        h = i
                        V.wait_ge(bank_ready(f"s{h}"), turn(f"s{h}"))
                        b = result(f"s{h}")
                        V.tensor_reduce(MX[:, h, 0:1], b[:, 0:P], AX.X, ALU.max).then_inc(*tick("dve_step"))
                        V.tensor_reduce(MX[:, h, 1:2], b[:, P:3 * P], AX.X, ALU.max).then_inc(*tick("dve_step"))
                        V.wait_ge(*now("dve_step"))
                        V.tensor_scalar(MX[:, h, :], MX[:, h, :], -scale, None, ALU.mult).then_inc(*tick("max_ready"))
                        V.wait_ge(*now("max_ready"))
                    if 1 <= i <= AH:
                        h = i - 1
                        V.wait_ge(bank_ready(f"t{h}"), turn(f"t{h}"))
                        b = result(f"t{h}")
                        if h >= 2:
                            V.wait_ge(bank_ready(f"o{h - 2}"), turn(f"o{h - 2}"))
                        copy(V, PRT[h % 2][:, :], b[:, 0:384]).then_inc(bank_free(f"t{h}"), 1)
                    if i >= 2:
                        h = i - 2
                        V.wait_ge(bank_ready(f"o{h}"), turn(f"o{h}"))
                        b = result(f"o{h}")
                        V.wait_ge(bank_free(f"s{h}"), turn(f"s{h}"))
                        V.reciprocal(RS[:, h, :], SM[:, h, :]).then_inc(*tick("dve_step"))
                        V.wait_ge(*now("dve_step"))
                        v = slice(h * AV, (h + 1) * AV)
                        V.tensor_scalar(Y[:, 0, v], b[:, 0:AV], RS[:, h, 0:1], None, ALU.mult).then_inc(*tick("dve_step"))
                        V.tensor_scalar(Y[:, 1, v], b[:, AV:2 * AV], RS[:, h, 1:2], None, ALU.mult).then_inc(bank_free(f"o{h}"), 1)
                V.wait_ge(bank_free(f"o{AH - 1}"), turn(f"o{AH - 1}"))
                for tt in range(TT):
                    V.memset(stat[:, 60 + tt:61 + tt], 0.0).then_inc(*tick("y_ready"))
                    V.wait_ge(*now("y_ready"))
                take_turn(V, "yt", XT, [(0, 1), (1, 1)])
                dve_residual("m", ALPHA)
                rows_here(0, 2)
                dve_layer_norm(Y, X, rows[0][:, 0, :], rows[0][:, 1, :], EPS1, "b_ln", "x_ready")

            @block.gpsimd
            def _(pool):
                load_rows(0, [a["ln_g"][1, 0], a["ln_b"][1, 0]])
                pool_power("latent_var", 1, "latent_rstd", MS[:, :])
                pool_layer_norm("b_ln")

        def dve_rms(key, g):
            dve_mean_square(key, D, EPS2)
            for tt in range(TT):
                V.scalar_tensor_tensor(Y[:, tt, :], X[:, tt, :], stat[:, 12 + tt:13 + tt], g, ALU.mult, ALU.mult).then_inc(*tick("h_ready"))
                V.wait_ge(*now("h_ready"))

        def pool_rms(key):
            pool_power(key + "_var", 1, key + "_rstd", stat[:, 12:14])

        def nsa():
            with ExitStack() as st:
                QT = sb("QT2", [P, NH // 2, T], F32, st)
                KS = sb("KS", [P, 2, NKV, T], F32, st)
                VS = sb("VS", [P, 2, TT, NKV * HD], F32, st)
                NG = sb("NG", [P, TT, NH, 3], F32, st)
                KCMP = sb("KCMP", [P, NKV * NCMP], F32, st)
                VCMP = sb("VCMP", [NCMP, NKV, HD], F32, st)
                BIAS = sb("BIAS", [P, NH, STRIP], F32, st)
                phase(mixers_in, QT, KS, VS, NG, KCMP, VCMP, BIAS)
                phase(nsa_attention, QT, KS, VS, NG, KCMP, VCMP, BIAS)
            phase(mixers_out)

        def mixers_in(block, st, QT, KS, VS, NG, KCMP, VCMP, BIAS):
            CT = sb("CT", [P, 2, NKV, T], F32, st)
            FLT = sb("FLT", [P, 2, CB // 2, NKV * NCMP], F32, st)
            HID = sb("HID", [P, 2, 2, NKV * NCMP], F32, st)
            POST = sb("POST", [P, 2, CB // 2], F32, st)
            BVEC = sb("BVEC", [NH, 384], F32, st)
            CWT = sb("CWT", [P, 2, 32], F32, st)
            SGC = sb("SGC", [P, 2, T], F32, st)
            CH = sb("CH", [P, 2, CW - 1 + T], F32, st)
            CACC = sb("CACC", [P, 2, T], F32, st)
            CV = sb("CV", [P, TT, CC], F32, st)
            CV2 = SGC
            GAT = sb("GAT", [GR, T], F32, st)
            LX = sb("LX", [P, TT, GK], F32, st)
            LA = sb("LA", [P, TT, GK], F32, st)
            E1 = sb("E1", [P, T], F32, st)
            E2 = sb("E2", [P, T], F32, st)
            E3 = sb("E3", [P, T], F32, st)
            BS = sb("BS", [P, T], F32, st)
            QG = sb("QG", [P, T], F32, st)
            KG = sb("KG", [P, T], F32, st)
            KDC = sb("KDC", [P, T], F32, st)
            KDT = sb("KDT", [P, TT, GK], F32, st)
            QBD = sb("QBD", [P, TT, GH, P], F32, st)
            AM = sb("AM", [P, TT, GH, P], F32, st)
            STB = sb("STB", [P, 3, GV], F32, st)
            GVS = sb("GVS", [P, TT, GV], F32, st)
            GRS = sb("GRS", [P, TT, GV], F32, st)
            GO = sb("GO", [P, TT, GV], F32, st)
            GSQ = CACC
            GST = sb("GST", [P, TT * GH], F32, st)
            DK, DV = GK // GH, GV // GH
            NCH = T // GCH

            @block.tensor
            def _(pe):
                b = job("bvec")
                if turn("bvec") > 1:
                    PE.wait_ge(bank_free("bvec"), turn("bvec") - 1)
                mul(b[0:NH, 0:384], RELB[:, :], con("onehot", BUCKETS), True, True).then_inc(bank_ready("bvec"), 1)
                b = job("post")
                if turn("post") > 1:
                    PE.wait_ge(bank_free("post"), turn("post") - 1)
                for k in range(2):
                    last = tr(b[:, k * 16:(k + 1) * 16], CPOS[:, k, :], ident[0:CB // 2, 0:CB // 2])
                last.then_inc(bank_ready("post"), 1)
                b = job("cwt")
                if turn("cwt") > 1:
                    PE.wait_ge(bank_free("cwt"), turn("cwt") - 1)
                for k in range(2):
                    last = tr(b[:, k * 32:k * 32 + CW], CONVW[:, k * P:(k + 1) * P], ident[0:CW, 0:CW])
                last.then_inc(bank_ready("cwt"), 1)
                pe_turn(PE, "xt", Y, "h_ready")
                pe.wait_ge(bank_free("xt00"), turn("xt00"))
                pe.wait_ge(bank_free("xt01"), turn("xt01"))
                pe.wait_ge(bank_free("xt10"), turn("xt10"))
                pe.wait_ge(bank_free("xt11"), turn("xt11"))
                pe.wait_ge(*landed("n_in0"))
                w = slot_of("n_in0")
                for i in range(2):
                    pe_colpair(PE, w, f"nq{i}", XT, [256 * i, 256 * i + 128])
                weight_read("n_in0", "nq1")
                pe.wait_ge(*landed("n_in1"))
                w = slot_of("n_in1")
                pe_colpair(PE, w, "ck", XT, [0, 128])
                pe_colpair(PE, w, "ks0", XT, [256])
                for tt in range(TT):
                    pe_rows(PE, w, f"vs0{tt}", XT, tt, 384, 128)
                weight_read("n_in1", "vs01")
                pe.wait_ge(*landed("n_in2"))
                w = slot_of("n_in2")
                pe_colpair(PE, w, "ks1", XT, [0])
                for tt in range(TT):
                    pe_rows(PE, w, f"vs1{tt}", XT, tt, 128, 128 + 24)
                weight_read("n_in2", "vs11")
                pe.wait_ge(*landed("n_in3"))
                w = slot_of("n_in3")
                pe_colpair(PE, w, "ca", XT, [0, 128])
                pe_colpair(PE, w, "cg", XT, [256, 384])
                weight_read("n_in3", "cg")
                pe.wait_ge(*landed("n_in4"))
                w = slot_of("n_in4")
                pe_colpair(PE, w, "gqk", XT, [0, 128])
                for tt in range(TT):
                    pe_rows(PE, w, f"gv{tt}", XT, tt, 256, 256)
                weight_read("n_in4", "gv1")
                pe.wait_ge(*landed("n_in5"))
                w = slot_of("n_in5")
                pe_colpair(PE, w, "ga", XT, [0], GR)
                for tt in range(TT):
                    pe_rows(PE, w, f"gr{tt}", XT, tt, GR, 256)
                weight_read("n_in5", "gr1")
                pe.wait_ge(bank_free("ga"), turn("ga"))
                for tt in range(TT):
                    b = job(f"la{tt}")
                    if turn(f"la{tt}") > 1:
                        PE.wait_ge(bank_free(f"la{tt}"), turn(f"la{tt}") - 1)
                    mul(b[:, 0:GK], GAT[:, tt * P:(tt + 1) * P], WAL[:, :], True, True).then_inc(bank_ready(f"la{tt}"), 1)
                for k in range(2):
                    pe.wait_ge(*landed(f"w1{'kv'[k]}"))
                    w = slot_of(f"w1{'kv'[k]}")
                    pe.wait_ge(*nth("blocks_ready", 4 * (k + 1)))
                    b = job(f"hid{k}")
                    if turn(f"hid{k}") > 1:
                        PE.wait_ge(bank_free(f"hid{k}"), turn(f"hid{k}") - 1)
                    for t2 in range(2):
                        for j in range(CB // 2):
                            last = mul(b[:, t2 * 32:t2 * 32 + NKV * NCMP], w[:, j, t2 * P:(t2 + 1) * P], FLT[:, k, j, :], j == 0, j == 15)
                    last.then_inc(bank_ready(f"hid{k}"), 1)
                    weight_read(f"w1{'kv'[k]}", f"hid{k}")
                pe.wait_ge(bank_free("hid0"), turn("hid0"))
                pe.wait_ge(bank_free("hid1"), turn("hid1"))
                b = job("kcmp")
                if turn("kcmp") > 1:
                    PE.wait_ge(bank_free("kcmp"), turn("kcmp") - 1)
                for t2 in range(2):
                    last = mul(b[0:HD, 0:NKV * NCMP], W2[:, 0, t2, :], HID[:, 0, t2, :], t2 == 0, t2 == 1)
                last.then_inc(bank_ready("kcmp"), 1)
                b = job("vcmp")
                if turn("vcmp") > 1:
                    PE.wait_ge(bank_free("vcmp"), turn("vcmp") - 1)
                for g in range(NKV):
                    for t2 in range(2):
                        last = mul(b[0:NCMP, g * HD:(g + 1) * HD], HID[:, 1, t2, g * NCMP:(g + 1) * NCMP], W2[:, 1, t2, :], t2 == 0, t2 == 1)
                last.then_inc(bank_ready("vcmp"), 1)
                pe.wait_ge(*nth("decay_ready", 1))
                b = job("gb")
                if turn("gb") > 1:
                    PE.wait_ge(bank_free("gb"), turn("gb") - 1)
                for tt in range(TT):
                    last = mul(b[:, tt * P:(tt + 1) * P], LA[:, tt, :], con("tri"), True, True)
                last.then_inc(bank_ready("gb"), 1)
                pe.wait_ge(*nth("k_decayed", 1))
                b = job("kdt")
                if turn("kdt") > 1:
                    PE.wait_ge(bank_free("kdt"), turn("kdt") - 1)
                for tt in range(TT):
                    last = tr(b[:, tt * P:(tt + 1) * P], KDC[:, tt * P:(tt + 1) * P], ident)
                last.then_inc(bank_ready("kdt"), 1)
                pe.wait_ge(*nth("q_spread", 1))
                for tt in range(TT):
                    b = job(f"at{tt}")
                    if turn(f"at{tt}") > 1:
                        PE.wait_ge(bank_free(f"at{tt}"), turn(f"at{tt}") - 1)
                    mul(b[:, :], KG[:, tt * P:(tt + 1) * P], QBD[:, tt, :, :], True, True).then_inc(bank_ready(f"at{tt}"), 1)
                pe.wait_ge(bank_free("kdt"), turn("kdt"))
                pe.wait_ge(bank_free("gv0"), turn("gv0"))
                pe.wait_ge(bank_free("gv1"), turn("gv1"))
                for c in range(NCH - 1):
                    r = slice(GCH * (c % 2), GCH * (c % 2) + GCH)
                    b = job(f"sd{c}")
                    if turn(f"sd{c}") > 1:
                        PE.wait_ge(bank_free(f"sd{c}"), turn(f"sd{c}") - 1)
                    mul(b[:, 0:GV], KDT[r, c // 2, :], GVS[r, c // 2, :], True, True).then_inc(bank_ready(f"sd{c}"), 1)
                for tt in range(TT):
                    pe.wait_ge(bank_free(f"at{tt}"), turn(f"at{tt}"))
                    pe.wait_ge(*nth("state_ready", 2 * tt + 1))
                    b = job(f"go{tt}")
                    if turn(f"go{tt}") > 1:
                        PE.wait_ge(bank_free(f"go{tt}"), turn(f"go{tt}") - 1)
                    for h in range(GH):
                        mul(b[:, h * DV:(h + 1) * DV], AM[:, tt, h, :], GVS[:, tt, h * DV:(h + 1) * DV], h == 0, False)
                    for c in range(2 * tt, 2 * tt + 2):
                        if c:
                            r = GCH * (c % 2)
                            last = mul(b[r:r + GCH, 0:GV], QG[:, c * GCH:(c + 1) * GCH], STB[:, c - 1, :], False, True)
                    last.then_inc(bank_ready(f"go{tt}"), 1)
                pe.wait_ge(*nth("conv_ready", 1))
                b = job("cvt")
                if turn("cvt") > 1:
                    PE.wait_ge(bank_free("cvt"), turn("cvt") - 1)
                for tt in range(TT):
                    for c in range(2):
                        last = tr(b[:, (2 * tt + c) * P:(2 * tt + c + 1) * P], CACC[:, c, tt * P:(tt + 1) * P], ident)
                last.then_inc(bank_ready("cvt"), 1)

            @block.scalar
            def _(act):
                act_squares(X, Y, "mix_sq", D)
                A.wait_ge(bank_ready("post"), turn("post"))
                b = result("post")
                copy(A, POST[:, :, :], b[:, 0:32].rearrange("p (k j) -> p k j", k=2)).then_inc(bank_free("post"), 1)
                A.wait_ge(bank_ready("cwt"), turn("cwt"))
                b = result("cwt")
                copy(A, CWT[:, :, 0:CW], b[:, 0:64].rearrange("p (k j) -> p k j", k=2)[:, :, 0:CW]).then_inc(bank_free("cwt"), 1)
                take_turn(A, "xt", XT, [(0, 0), (1, 0)])
                for i in range(2):
                    A.wait_ge(bank_ready(f"nq{i}"), turn(f"nq{i}"))
                    b = result(f"nq{i}")
                    copy(A, QT[:, 2 * i:2 * i + 2, :], pair(b), HD ** -0.5).then_inc(bank_free(f"nq{i}"), 1)

                def spread(dst, src, name):
                    for head in range(NKV):
                        for half in range(2):
                            ins = copy(A, dst(slice(HD * half, HD * half + HD), head), src(slice(HD * head, HD * head + HD)))
                            if (head, half) == (1, 1):
                                ins.then_inc(bank_free(name), 1)
                            else:
                                ins.then_inc(*tick("act_step"))

                A.wait_ge(bank_ready("ck"), turn("ck"))
                b = result("ck")
                spread(lambda r, g: CT[r, :, g, :], lambda r: b[r, 0:2 * T].rearrange("p (k t) -> p k t", k=2), "ck")
                for s in range(2):
                    A.wait_ge(bank_ready(f"ks{s}"), turn(f"ks{s}"))
                    b = result(f"ks{s}")
                    spread(lambda r, g: KS[r, s, g, :], lambda r: b[r, 0:T], f"ks{s}")
                    for tt in range(TT):
                        A.wait_ge(bank_ready(f"vs{s}{tt}"), turn(f"vs{s}{tt}"))
                        b = result(f"vs{s}{tt}")
                        if s == 1:
                            A.activation(NG[:, tt, :, :].rearrange("p h n -> p (h n)"), b[:, 128:152], ACT.Sigmoid).then_inc(*tick("act_step"))
                            A.wait_ge(*now("act_step"))
                        copy(A, VS[:, s, tt, :], b[:, 0:128]).then_inc(bank_free(f"vs{s}{tt}"), 1)
                A.wait_ge(bank_ready("cg"), turn("cg"))
                b = result("cg")
                A.activation(SGC[:, :, :], pair(b), ACT.Sigmoid).then_inc(bank_free("cg"), 1)
                A.wait_ge(bank_ready("gqk"), turn("gqk"))
                b = result("gqk")
                copy(A, QG[:, :], b[:, 0:T], DK ** -0.5).then_inc(*tick("act_step"))
                copy(A, KG[:, :], b[:, T:2 * T]).then_inc(bank_free("gqk"), 1)
                for tt in range(TT):
                    A.wait_ge(bank_ready(f"gv{tt}"), turn(f"gv{tt}"))
                    b = result(f"gv{tt}")
                    copy(A, GVS[:, tt, :], b[:, 0:GV]).then_inc(bank_free(f"gv{tt}"), 1)
                A.wait_ge(bank_ready("ga"), turn("ga"))
                b = result("ga")
                copy(A, GAT[:, :], b[0:GR, 0:T]).then_inc(bank_free("ga"), 1)
                for tt in range(TT):
                    A.wait_ge(bank_ready(f"gr{tt}"), turn(f"gr{tt}"))
                    b = result(f"gr{tt}")
                    A.activation(GRS[:, tt, :], b[:, 0:GV], ACT.Silu).then_inc(bank_free(f"gr{tt}"), 1)
                for k in range(2):
                    A.wait_ge(bank_ready(f"hid{k}"), turn(f"hid{k}"))
                    b = result(f"hid{k}")
                    for t2 in range(2):
                        ins = A.activation(HID[:, k, t2, :], b[:, t2 * 32:t2 * 32 + NKV * NCMP], ACT.Silu, bias=B1[:, k, t2:t2 + 1])
                        if t2 == 0:
                            ins.then_inc(*tick("act_step"))
                        else:
                            ins.then_inc(bank_free(f"hid{k}"), 1)
                logsig_steps(LA[:, :, :], "decay")
                A.wait_ge(bank_ready("kcmp"), turn("kcmp"))
                b = result("kcmp")
                copy(A, KCMP[0:HD, :], b[0:HD, 0:NKV * NCMP]).then_inc(*tick("act_step"))
                copy(A, KCMP[HD:P, :], b[0:HD, 0:NKV * NCMP]).then_inc(bank_free("kcmp"), 1)
                A.wait_ge(bank_ready("vcmp"), turn("vcmp"))
                b = result("vcmp")
                copy(A, VCMP[:, :, :], b[0:NCMP, 0:NKV * HD].rearrange("p (g d) -> p g d", g=NKV)).then_inc(bank_free("vcmp"), 1)
                A.wait_ge(bank_ready("gb"), turn("gb"))
                b = result("gb")
                copy(A, BS[:, :], b[:, 0:T]).then_inc(*tick("decay_sums"))
                A.wait_ge(*now("decay_sums"))
                A.activation(E1[:, :], b[:, 0:T], ACT.Exp).then_inc(*tick("act_step"))
                A.activation(E2[:, :], b[:, 0:T], ACT.Exp, scale=-1.0).then_inc(*tick("act_step"))
                for c in range(NCH):
                    s = slice(c * GCH, (c + 1) * GCH)
                    ins = A.activation(E3[:, s], b[:, s], ACT.Exp, scale=-1.0, bias=BS[:, (c + 1) * GCH - 1:(c + 1) * GCH])
                    if c < NCH - 1:
                        ins.then_inc(*tick("act_step"))
                    else:
                        ins.then_inc(bank_free("gb"), 1)
                A.wait_ge(bank_ready("kdt"), turn("kdt"))
                b = result("kdt")
                copy(A, KDT[:, :, :], b[:, 0:T].rearrange("p (t d) -> p t d", t=TT)).then_inc(bank_free("kdt"), 1)
                A.wait_ge(*nth("conv_normed", TT))
                for tt in range(TT):
                    A.activation(Y[:, tt, 512:512 + CC], CV2[:, tt, :], ACT.Silu).then_inc(*tick("act_step"))
                    A.wait_ge(*now("act_step"))

            @block.vector
            def _(dve):
                params_here(dve)
                for c in range(2):
                    V.memset(CH[:, c, 0:CW - 1], 0.0).then_inc(*tick("dve_step"))
                rows_here(1, 1)
                dve_rms("mix", rows[1][:, 0, :])
                V.wait_ge(bank_ready("bvec"), turn("bvec"))
                b = result("bvec")
                V.tensor_tensor(BVEC[:, :], b[0:NH, 0:384], con("future", NH), ALU.add).then_inc(bank_free("bvec"), 1)
                take_turn(V, "xt", XT, [(0, 1), (1, 1)])
                V.wait_ge(bank_free("ck"), turn("ck"))
                V.wait_ge(bank_free("post"), turn("post"))
                for k in range(2):
                    for g in range(NKV):
                        for half in range(2):
                            r = slice(HD * half, HD * half + HD)
                            row = CT[r, k, g, half:half + 1]
                            blocks = bass.AP(row.tensor, row.offset, [list(row.ap[0]), [2, CB // 2], [CS, NCMP]])
                            pos = POST[r, k, :].unsqueeze(2).broadcast_to([HD, CB // 2, NCMP])
                            V.tensor_tensor(FLT[r, k, :, g * NCMP:(g + 1) * NCMP], blocks, pos, ALU.add).then_inc(*tick("blocks_ready"))
                            V.wait_ge(*now("blocks_ready"))
                V.wait_ge(bank_ready("ca"), turn("ca"))
                b = result("ca")
                V.wait_ge(bank_free("cg"), turn("cg"))
                V.wait_ge(bank_free("cwt"), turn("cwt"))
                V.tensor_tensor(CH[:, :, CW - 1:], pair(b), SGC[:, :, :], ALU.mult).then_inc(bank_free("ca"), 1)
                V.wait_ge(bank_free("ca"), turn("ca"))
                for tt in range(TT):
                    V.wait_ge(bank_ready(f"la{tt}"), turn(f"la{tt}"))
                    b = result(f"la{tt}")
                    V.tensor_tensor(LX[:, tt, :], b[:, 0:GK], small("gla_b_alpha_2"), ALU.add).then_inc(bank_free(f"la{tt}"), 1)
                V.wait_ge(bank_free("la0"), turn("la0"))
                V.wait_ge(bank_free("la1"), turn("la1"))
                V.scalar_tensor_tensor(LA[:, :, :], LX[:, :, :], -1.0, LX[:, :, :], ALU.mult, ALU.max).then_inc(*tick("decay_abs"))
                V.wait_ge(*now("decay_abs"))
                V.wait_ge(*nth("decay_ln", 1))
                V.scalar_tensor_tensor(LA[:, :, :], LX[:, :, :], 0.0, LA[:, :, :], ALU.min, ALU.subtract).then_inc(*tick("dve_step"))
                V.wait_ge(*now("dve_step"))
                V.tensor_scalar(LA[:, :, :], LA[:, :, :], 1.0 / 16.0, None, ALU.mult).then_inc(*tick("decay_ready"))
                V.wait_ge(*now("decay_ready"))
                for j in range(CW):
                    for c in range(2):
                        x = CH[:, c, j:j + T]
                        if j == 0:
                            ins = V.tensor_scalar(CACC[:, c, :], x, CWT[:, c, 0:1], CONVB[:, c:c + 1], ALU.mult, ALU.add)
                        else:
                            dve.wait_ge(S("dve_step"), count["dve_step"] - 1)
                            ins = V.scalar_tensor_tensor(CACC[:, c, :], x, CWT[:, c, j:j + 1], CACC[:, c, :], ALU.mult, ALU.add)
                        if (j, c) == (CW - 1, 1):
                            ins.then_inc(*tick("conv_ready"))
                            V.wait_ge(*now("conv_ready"))
                        else:
                            ins.then_inc(*tick("dve_step"))
                V.wait_ge(bank_free("gb"), turn("gb"))
                V.wait_ge(bank_free("gqk"), turn("gqk"))
                V.tensor_tensor(KDC[:, :], KG[:, :], E3[:, :], ALU.mult).then_inc(*tick("k_decayed"))
                V.wait_ge(*now("k_decayed"))
                V.tensor_tensor(KG[:, :], KG[:, :], E2[:, :], ALU.mult).then_inc(*tick("dve_step"))
                V.tensor_tensor(QG[:, :], QG[:, :], E1[:, :], ALU.mult).then_inc(*tick("dve_step"))
                V.wait_ge(*now("dve_step"))
                V.wait_ge(*nth("cleared", 3))
                for h in range(GH):
                    r = slice(DK * h, DK * h + DK)
                    ins = V.tensor_copy(QBD[r, :, h, :], QG[r, :].rearrange("p (t q) -> p t q", t=TT))
                    if h < GH - 1:
                        ins.then_inc(*tick("dve_step"))
                    else:
                        ins.then_inc(*tick("q_spread"))
                        V.wait_ge(*now("q_spread"))
                mask = con("tri").bitcast(I32).unsqueeze(1).broadcast_to([P, GH, P])
                for tt in range(TT):
                    V.wait_ge(bank_ready(f"at{tt}"), turn(f"at{tt}"))
                    b = result(f"at{tt}")
                    V.copy_predicated(AM[:, tt, :, :], mask, b[:, :].rearrange("p (h t) -> p h t", h=GH)).then_inc(bank_free(f"at{tt}"), 1)
                for c in range(NCH - 1):
                    V.wait_ge(bank_ready(f"sd{c}"), turn(f"sd{c}"))
                    b = result(f"sd{c}")
                    end = (c + 1) * GCH - 1
                    for h in range(GH):
                        r, s = slice(DK * h, DK * h + DK), slice(h * DV, (h + 1) * DV)
                        if c == 0:
                            ins = V.tensor_copy(STB[r, 0, s], b[r, s])
                        else:
                            ins = V.scalar_tensor_tensor(STB[r, c, s], STB[r, c - 1, s], E1[r, end:end + 1], b[r, s], ALU.mult, ALU.add)
                        if h == GH - 1:
                            ins.then_inc(bank_free(f"sd{c}"), 1)
                            V.wait_ge(bank_free(f"sd{c}"), turn(f"sd{c}"))
                        else:
                            ins.then_inc(*tick("dve_step"))
                    V.memset(stat[:, 48 + c:49 + c], 0.0).then_inc(*tick("state_ready"))
                    V.wait_ge(*now("state_ready"))
                V.wait_ge(bank_ready("cvt"), turn("cvt"))
                b = result("cvt")
                copy(V, CV[:, :, :], b[:, :].rearrange("p (t c) -> p t c", t=TT)).then_inc(bank_free("cvt"), 1)
                V.wait_ge(bank_free("cvt"), turn("cvt"))
                dve_layer_norm(CV, CV2, small("conv_ln_g_2"), small("conv_ln_b_2"), EPS2, "conv", "conv_normed")
                for tt in range(TT):
                    V.wait_ge(bank_ready(f"go{tt}"), turn(f"go{tt}"))
                    b = result(f"go{tt}")
                    copy(V, GO[:, tt, :], b[:, 0:GV]).then_inc(bank_free(f"go{tt}"), 1)
                V.wait_ge(bank_free("go0"), turn("go0"))
                V.wait_ge(bank_free("go1"), turn("go1"))
                V.tensor_tensor(GSQ[:, :, :], GO[:, :, :], GO[:, :, :], ALU.mult).then_inc(*tick("dve_step"))
                V.wait_ge(*now("dve_step"))
                heads = lambda x: x[:, :, :].rearrange("p t (h v) -> p (t h) v", v=DV)
                V.tensor_reduce(GST[:, :], heads(GSQ), AX.X, ALU.add).then_inc(*tick("dve_step"))
                V.wait_ge(*now("dve_step"))
                V.tensor_scalar(GST[:, :], GST[:, :], 1.0 / DV, EPS2, ALU.mult, ALU.add).then_inc(*tick("gla_var"))
                V.wait_ge(*now("gla_var"))
                V.wait_ge(*nth("gla_rstd", 1))
                V.tensor_tensor(heads(GO), heads(GO), GST[:, :].unsqueeze(2).broadcast_to([P, TT * GH, DV]), ALU.mult).then_inc(*tick("dve_step"))
                V.wait_ge(*now("dve_step"))
                V.tensor_tensor(GO[:, :, :], GO[:, :, :], small("gla_norm_g_2").unsqueeze(1).broadcast_to([P, TT, GV]), ALU.mult).then_inc(*tick("dve_step"))
                V.wait_ge(*now("dve_step"))
                V.wait_ge(bank_free("gr0"), turn("gr0"))
                V.wait_ge(bank_free("gr1"), turn("gr1"))
                V.tensor_tensor(Y[:, :, 768:1024], GO[:, :, :], GRS[:, :, :], ALU.mult).then_inc(*tick("dve_step"))
                V.wait_ge(*now("dve_step"))
                V.wait_ge(*nth("bias_here", 1))
                V.tensor_copy(BIAS[:, :, 384:384 + NCMP], BIAS[:, :, CB - 1:T:CS]).then_inc(*tick("dve_step"))
                V.tensor_copy(BIAS[:, :, 384 + NCMP:STRIP], BIAS[:, :, P + CB - 1:T:CS]).then_inc(*tick("dve_step"))
                V.wait_ge(*now("dve_step"))
                at, _ = cwhere["seen"]
                for tt in range(TT):
                    V.tensor_scalar(NG[:, tt, :, 0], NG[:, tt, :, 0], CN[:, at + tt:at + tt + 1], None, ALU.mult).then_inc(*tick("dve_step"))
                    V.wait_ge(*now("dve_step"))

            @block.gpsimd
            def _(pool):
                load_rows(1, [a["mix_norm_g_2"][0]])
                pool_rms("mix")
                for t in (QBD, AM, STB):
                    G.memset(t[:], 0.0).then_inc(*tick("cleared"))
                    G.wait_ge(*now("cleared"))
                pool.wait_ge(bank_free("bvec"), turn("bvec"))
                n = BVEC.shape[1]
                pool.dma_start(scratch, BVEC[:, :].unsqueeze(1).broadcast_to([NH, P, n])).then_inc(S("bias_out"), 16)
                pool.wait_ge(S("bias_out"), 16)
                t1 = bass.AP(scratch.tensor, P - 1, [[n - 1, P], [P * n, NH], [1, T]])
                t0 = bass.AP(scratch.tensor, 2 * P - 1, [[n - 1, P], [P * n, NH], [1, P]])
                pool.dma_start(BIAS[:, :, 0:T], t1).then_inc(S("bias_in"), 16)
                pool.dma_start(BIAS[:, :, T:T + P], t0).then_inc(S("bias_in"), 16)
                pool.wait_ge(S("bias_in"), 32)
                G.memset(stat[:, 56:57], 0.0).then_inc(*tick("bias_here"))
                G.wait_ge(*now("bias_here"))
                pool_layer_norm("conv")
                pool_power("gla_var", 1, "gla_rstd", GST[:, :])

        def nsa_attention(block, st, QT, KS, VS, NG, KCMP, VCMP, BIAS):
            N0 = 7
            WIN = 384 + NCMP + N0
            groups = [(0, T), (T, P), (384, NCMP), (384 + NCMP, N0), (WIN, T), (WIN + T, P)]
            branch = [1, 1, 0, 0, 2, 2]
            PR = [sb(f"NP{i}", [P, WIN + 384], F32, st) for i in range(2)]
            PTS = [sb(f"NPT{i}", [P, 2, 384], F32, st) for i in range(2)]
            PTC = [sb(f"NPC{i}", [NCMP, 2, P], F32, st) for i in range(2)]
            MX = sb("NMX", [P, NH, 6], F32, st)
            SM = sb("NSM", [P, NH, 6], F32, st)
            FC = sb("NFC", [P, NH, 6], F32, st)
            G6 = sb("G6", [P, NH, 6], F32, st)
            MIXO = [sb(f"MIXO{i}", [P, 6, HD], F32, st) for i in range(2)]

            @block.tensor
            def _(pe):
                for i in range(NH + 2):
                    if i < NH:
                        h, g = i, i // (NH // NKV)
                        r = slice(HD * (h % 2), HD * (h % 2) + HD)
                        q = QT[r, h // 2, :]
                        b = job(f"s{h}")
                        if turn(f"s{h}") > 1:
                            PE.wait_ge(bank_free(f"s{h}"), turn(f"s{h}") - 1)
                        mul(b[:, 0:T], q[:, P:T], KS[r, 0, g, :], True, True)
                        mul(b[:, T:T + P], q[:, 0:P], KS[r, 0, g, 0:P], True, True)
                        mul(b[:, 384:384 + NCMP], q[:, P:T], KCMP[r, g * NCMP:(g + 1) * NCMP], True, True)
                        mul(b[:, 384 + NCMP:WIN], q[:, 0:P], KCMP[r, g * NCMP:g * NCMP + N0], True, True).then_inc(bank_ready(f"s{h}"), 1)
                        b = job(f"w{h}")
                        if turn(f"w{h}") > 1:
                            PE.wait_ge(bank_free(f"w{h}"), turn(f"w{h}") - 1)
                        mul(b[:, 0:T], q[:, P:T], KS[r, 1, g, :], True, True)
                        mul(b[:, T:T + P], q[:, 0:P], KS[r, 1, g, 0:P], True, True).then_inc(bank_ready(f"w{h}"), 1)
                    if 1 <= i <= NH:
                        h = i - 1
                        pe.wait_ge(*nth("probs_ready", h + 1))
                        p = PR[h % 2]
                        b = job(f"ts{h}")
                        if turn(f"ts{h}") > 1:
                            PE.wait_ge(bank_free(f"ts{h}"), turn(f"ts{h}") - 1)
                        for j in range(3):
                            tr(b[:, j * P:(j + 1) * P], p[:, j * P:(j + 1) * P], ident)
                        tr(b[0:NCMP, 384:512], p[:, 384:384 + NCMP], ident).then_inc(bank_ready(f"ts{h}"), 1)
                        b = job(f"tw{h}")
                        if turn(f"tw{h}") > 1:
                            PE.wait_ge(bank_free(f"tw{h}"), turn(f"tw{h}") - 1)
                        for j in range(3):
                            tr(b[:, j * P:(j + 1) * P], p[:, WIN + j * P:WIN + (j + 1) * P], ident)
                        tr(b[0:N0, 384:512], p[:, 384 + NCMP:WIN], ident).then_inc(bank_ready(f"tw{h}"), 1)
                    if i >= 2:
                        h = i - 2
                        g = h // (NH // NKV)
                        v = slice(g * HD, (g + 1) * HD)
                        pe.wait_ge(bank_free(f"ts{h}"), turn(f"ts{h}"))
                        pe.wait_ge(bank_free(f"tw{h}"), turn(f"tw{h}"))
                        b = job(f"o{h}")
                        if turn(f"o{h}") > 1:
                            PE.wait_ge(bank_free(f"o{h}"), turn(f"o{h}") - 1)
                        o = lambda n: b[:, n * HD:(n + 1) * HD]
                        for s, n in ((0, 0), (1, 4)):
                            mul(o(n), PTS[h % 2][:, s, 0:P], VS[:, s, 0, v], True, False)
                            mul(o(n), PTS[h % 2][:, s, P:2 * P], VS[:, s, 1, v], False, True)
                            mul(o(n + 1), PTS[h % 2][:, s, 2 * P:3 * P], VS[:, s, 0, v], True, True)
                        mul(o(2), PTC[h % 2][:, 0, :], VCMP[:, g, :], True, True)
                        mul(o(3), PTC[h % 2][0:N0, 1, :], VCMP[0:N0, g, :], True, True).then_inc(bank_ready(f"o{h}"), 1)

            @block.scalar
            def _(act):
                for i in range(NH + 1):
                    if i < NH:
                        h = i
                        A.wait_ge(*nth("max_ready", h + 1))
                        for n, (c, w) in enumerate(groups):
                            ins = A.activation(PR[h % 2][:, c:c + w], PR[h % 2][:, c:c + w], ACT.Exp, bias=MX[:, h, n:n + 1], accum_out=SM[:, h, n:n + 1])
                            if n < 5:
                                ins.then_inc(*tick("act_step"))
                            else:
                                ins.then_inc(*tick("probs_ready"))
                                A.wait_ge(*now("probs_ready"))
                    if i >= 1:
                        h = i - 1
                        if h >= 2:
                            A.wait_ge(bank_ready(f"o{h - 2}"), turn(f"o{h - 2}"))
                        A.wait_ge(bank_ready(f"ts{h}"), turn(f"ts{h}"))
                        b = result(f"ts{h}")
                        copy(A, PTS[h % 2][:, 0, :], b[:, 0:384]).then_inc(*tick("act_step"))
                        copy(A, PTC[h % 2][:, 0, :], b[0:NCMP, 384:512]).then_inc(bank_free(f"ts{h}"), 1)

            @block.vector
            def _(dve):
                for n in range(6):
                    V.tensor_copy(G6[:, :, n], NG[:, 1 - n % 2, :, branch[n]]).then_inc(*tick("dve_step"))
                for i in range(NH + 2):
                    if i < NH:
                        h = i
                        if h >= 2:
                            V.wait_ge(bank_ready(f"tw{h - 2}"), turn(f"tw{h - 2}"))
                        for n, (c, w) in enumerate(groups):
                            name = f"s{h}" if n < 4 else f"w{h}"
                            if n in (0, 4):
                                V.wait_ge(bank_ready(name), turn(name))
                                b = result(name)
                            bc = c if n < 4 else c - WIN
                            ins = V.tensor_tensor_reduce(out=PR[h % 2][:, c:c + w], in0=b[:, bc:bc + w], in1=BIAS[:, h, bc:bc + w], scale=1.0,
                                                         scalar=FLOOR, op0=ALU.add, op1=ALU.max, accum_out=MX[:, h, n:n + 1])
                            if n in (3, 5):
                                ins.then_inc(bank_free(name), 1)
                            else:
                                ins.then_inc(*tick("dve_step"))
                        V.wait_ge(bank_free(f"s{h}"), turn(f"s{h}"))
                        V.wait_ge(bank_free(f"w{h}"), turn(f"w{h}"))
                        V.tensor_scalar(MX[:, h, :], MX[:, h, :], -1.0, None, ALU.mult).then_inc(*tick("max_ready"))
                        V.wait_ge(*now("max_ready"))
                    if 1 <= i <= NH:
                        h = i - 1
                        if h >= 2:
                            V.wait_ge(bank_ready(f"o{h - 2}"), turn(f"o{h - 2}"))
                        V.wait_ge(bank_ready(f"tw{h}"), turn(f"tw{h}"))
                        b = result(f"tw{h}")
                        copy(V, PTS[h % 2][:, 1, :], b[:, 0:384]).then_inc(*tick("dve_step"))
                        copy(V, PTC[h % 2][0:N0, 1, :], b[0:N0, 384:512]).then_inc(bank_free(f"tw{h}"), 1)
                        V.wait_ge(*nth("probs_ready", h + 1))
                        V.reciprocal(FC[:, h, :], SM[:, h, :]).then_inc(*tick("dve_step"))
                        V.wait_ge(*now("dve_step"))
                        V.tensor_tensor(FC[:, h, :], FC[:, h, :], G6[:, h, :], ALU.mult).then_inc(*tick("dve_step"))
                        V.wait_ge(*now("dve_step"))
                    if i >= 2:
                        h = i - 2
                        V.wait_ge(bank_ready(f"o{h}"), turn(f"o{h}"))
                        b = result(f"o{h}")
                        m = MIXO[h % 2]
                        V.tensor_tensor(m[:, :, :], b[:, 0:384].rearrange("p (n d) -> p n d", n=6),
                                             FC[:, h, :].unsqueeze(2).broadcast_to([P, 6, HD]), ALU.mult).then_inc(bank_free(f"o{h}"), 1)
                        V.wait_ge(bank_free(f"o{h}"), turn(f"o{h}"))
                        for tt in range(TT):
                            V.tensor_reduce(Y[:, tt, h * HD:(h + 1) * HD], m[:, 1 - tt::2, :].rearrange("p n d -> p d n"), AX.X, ALU.add).then_inc(*tick("dve_step"))
                        V.wait_ge(*now("dve_step"))

        def mixers_out(block, st):
            @block.tensor
            def _(pe):
                pe_turn(PE, "yt", Y, None)
                pe.wait_ge(bank_free("yt00"), turn("yt00"))
                pe.wait_ge(bank_free("yt01"), turn("yt01"))
                pe.wait_ge(bank_free("yt10"), turn("yt10"))
                pe.wait_ge(bank_free("yt11"), turn("yt11"))
                for cb in range(2):
                    pe.wait_ge(*landed(f"n_out{cb}"))
                    w = slot_of(f"n_out{cb}")
                    for tt in range(TT):
                        pe_rows(PE, w, f"o{cb}{tt}", XT, tt, 0, 512)
                    weight_read(f"n_out{cb}", f"o{cb}1")

            block.scalar(lambda act: take_turn(A, "yt", XT, [(0, 0), (1, 0)]))

            @block.vector
            def _(dve):
                take_turn(V, "yt", XT, [(0, 1), (1, 1)])
                for cb in range(2):
                    for tt in range(TT):
                        s = slice(cb * 512, cb * 512 + 512)
                        V.wait_ge(bank_ready(f"o{cb}{tt}"), turn(f"o{cb}{tt}"))
                        b = result(f"o{cb}{tt}")
                        V.tensor_tensor(X[:, tt, s], X[:, tt, s], b[:, :], ALU.add).then_inc(bank_free(f"o{cb}{tt}"), 1)
                V.wait_ge(bank_free("o00"), turn("o00"))
                V.wait_ge(bank_free("o01"), turn("o01"))
                V.wait_ge(bank_free("o10"), turn("o10"))
                V.wait_ge(bank_free("o11"), turn("o11"))

        def ffn(block, st):
            FT = sb("FT", [P, FF // P, T], F32, st)
            SG = [sb(f"SGF{i}", [P, T], F32, st) for i in range(2)]

            @block.tensor
            def _(pe):
                pe_turn(PE, "xt", Y, "h_ready")
                pe.wait_ge(bank_free("xt00"), turn("xt00"))
                pe.wait_ge(bank_free("xt01"), turn("xt01"))
                pe.wait_ge(bank_free("xt10"), turn("xt10"))
                pe.wait_ge(bank_free("xt11"), turn("xt11"))
                for e in range(len(ffe) - 1):
                    pe.wait_ge(*landed(f"ffg{e}"))
                    pe.wait_ge(*landed(f"ffu{e}"))
                    wg, wu = slot_of(f"ffg{e}"), slot_of(f"ffu{e}")
                    for i in range((ffe[e + 1] - ffe[e]) // P):
                        f = 4 * e + i
                        b = job(f"gu{f}")
                        if turn(f"gu{f}") > 1:
                            PE.wait_ge(bank_free(f"gu{f}"), turn(f"gu{f}") - 1)
                        for s, w in enumerate((wg, wu)):
                            for k in range(KD):
                                last = mul(b[:, s * T:(s + 1) * T], w[:, k, i * P:(i + 1) * P], XT[:, k, :], k == 0, k == KD - 1)
                        last.then_inc(bank_ready(f"gu{f}"), 1)
                    weight_read(f"ffg{e}", f"gu{f}")
                    weight_read(f"ffu{e}", f"gu{f}")
                for cb in range(2):
                    bs = [job(f"d{cb}{tt}") for tt in range(TT)]
                    for tt in range(TT):
                        pe.wait_ge(bank_free(f"d{cb}{tt}"), turn(f"d{cb}{tt}") - 1)
                    for e, (k0, k1) in enumerate(((0, 8), (8, 16), (16, 22))):
                        pe.wait_ge(*landed(f"ffd{cb}{e}"))
                        w = slot_of(f"ffd{cb}{e}")
                        for tt in range(TT):
                            for k in range(k0, k1):
                                if cb == 0 and tt == 0:
                                    pe.wait_ge(bank_free(f"gu{k}"), turn(f"gu{k}"))
                                last = mul(bs[tt][:, :], FT[:, k, tt * P:(tt + 1) * P], w[:, k - k0, :], k == 0, k == FF // P - 1)
                            if k1 == FF // P:
                                last.then_inc(bank_ready(f"d{cb}{tt}"), 1)
                        weight_read(f"ffd{cb}{e}", f"d{cb}1")

            @block.scalar
            def _(act):
                act_squares(X, Y, "ffn_sq", D)
                take_turn(A, "xt", XT, [(0, 0), (1, 0)])
                for f in range(FF // P):
                    A.wait_ge(bank_ready(f"gu{f}"), turn(f"gu{f}"))
                    b = result(f"gu{f}")
                    if f >= 2:
                        A.wait_ge(bank_free(f"gu{f - 2}"), turn(f"gu{f - 2}"))
                    A.activation(SG[f % 2][:, :], b[:, 0:T], ACT.Silu).then_inc(*tick("silu_done"))
                    A.wait_ge(*now("silu_done"))

            @block.vector
            def _(dve):
                rows_here(0, 1)
                dve_rms("ffn", rows[0][:, 0, :])
                take_turn(V, "xt", XT, [(0, 1), (1, 1)])
                for f in range(FF // P):
                    V.wait_ge(*nth("silu_done", f + 1))
                    V.wait_ge(bank_ready(f"gu{f}"), turn(f"gu{f}"))
                    b = result(f"gu{f}")
                    V.tensor_tensor(FT[:, f, :], b[:, T:2 * T], SG[f % 2][:, :], ALU.mult).then_inc(bank_free(f"gu{f}"), 1)
                for cb in range(2):
                    for tt in range(TT):
                        s = slice(cb * 512, cb * 512 + 512)
                        V.wait_ge(bank_ready(f"d{cb}{tt}"), turn(f"d{cb}{tt}"))
                        b = result(f"d{cb}{tt}")
                        V.tensor_tensor(X[:, tt, s], X[:, tt, s], b[:, :], ALU.add).then_inc(bank_free(f"d{cb}{tt}"), 1)
                V.wait_ge(bank_free("d00"), turn("d00"))
                V.wait_ge(bank_free("d01"), turn("d01"))
                V.wait_ge(bank_free("d10"), turn("d10"))
                V.wait_ge(bank_free("d11"), turn("d11"))

            @block.gpsimd
            def _(pool):
                load_rows(0, [a["ffn_norm_g_2"][0]])
                pool_rms("ffn")

        def last(block, st):
            @block.gpsimd
            def _(pool):
                load_rows(1, [a["ple_norm_g_2"][0], a["final_norm_g_2"]])
                pool_rms("ple")

            def dve_before():
                rows_here(1, 2)
                dve_rms("ple", rows[1][:, 0, :])

            embed(block, st, Y, "ple2_gate", "ple2_proj", 2,
                  before=(lambda: act_squares(X, Y, "ple_sq", D), dve_before))

        def final_norm(block, st):
            block.scalar(lambda act: act_squares(X, Y, "fin_sq", D))
            block.gpsimd(lambda pool: pool_rms("fin"))

            @block.vector
            def _(dve):
                dve_mean_square("fin", D, EPS2)
                for tt in range(TT):
                    V.scalar_tensor_tensor(Y[:, tt, :], X[:, tt, :], stat[:, 12 + tt:13 + tt], rows[1][:, 1, :], ALU.mult, ALU.mult).then_inc(*tick("out_ready"))
                    V.wait_ge(*now("out_ready"))

        IDX = sb("IDX", [P, TT, PICKS], I32)
        GATE = sb("GATE", [P, TT, PICKS])
        block = ctx.enter_context(nc.Block())

        def phase(make, *args, **kw):
            with ExitStack() as st:
                make(block, st, *args, **kw)
                end_phase(block)

        def peer(l):
            phase(peer_route, l, IDX, GATE)
            phase(peer_gather, l, IDX, GATE)
            phase(embed, X, f"ple_gate{l}_", f"ple_proj{l}", l)

        phase(mlstm)
        peer(0)
        phase(mla)
        peer(1)
        nsa()
        phase(ffn)
        phase(last)
        phase(final_norm)
        store_and_load(block)


_INS = [
    "x", "p", "positions", "ln_g", "ln_b", "a_w_in", "a_b_if", "a_hn_g", "a_w_out", "kv_w_down", "kv_norm_g", "kv_w_up",
    "b_w_dq", "b_q_norm_g", "b_w_uq", "b_w_out", "peer_w_q", "peer_sub_keys", "peer_u", "peer_v", "ple_w_proj",
    "ple_w_gate", "p_2", "rel_bias_2", "mix_norm_g_2", "w_in_2", "w_out_2", "cmp_pos_k_2", "cmp_w1_k_2",
    "cmp_b1_k_2", "cmp_w2_k_2", "cmp_pos_v_2", "cmp_w1_v_2", "cmp_b1_v_2", "cmp_w2_v_2", "conv_w_2", "conv_b_2",
    "conv_ln_g_2", "conv_ln_b_2", "gla_w_alpha_2", "gla_b_alpha_2", "gla_norm_g_2", "ffn_norm_g_2",
    "ffn_w_gate_2", "ffn_w_up_2", "ffn_w_down_2", "ple_norm_g_2", "ple_w_gate_2", "ple_w_proj_2", "final_norm_g_2",
]


def kernel(**inputs):
    import concourse.bacc as bacc
    from concourse.bass_utils import run_bass_kernel_spmd

    nc = bacc.Bacc("TRN2", target_bir_lowering=False, num_devices=1)
    arrays, aps = {}, {}
    for name in _INS:
        arr = np.ascontiguousarray(inputs[name])
        arrays[f"in_{name}"] = arr
        aps[name] = nc.dram_tensor(f"in_{name}", arr.shape, mybir.dt.from_np(arr.dtype), kind="ExternalInput").ap()
    table, where = constants()
    arrays["in_constants"] = table
    consts = nc.dram_tensor("in_constants", table.shape, F32, kind="ExternalInput").ap()
    scratch = nc.dram_tensor("bias_rows", (NH, P, 384), F32, kind="Internal").ap()
    out = nc.dram_tensor("out_x", (1, T, D), F32, kind="ExternalOutput").ap()
    build(nc, aps, consts, where, scratch, out)
    done = run_bass_kernel_spmd(nc, [arrays], core_ids=[0])
    return done.results[0]["out_x"]
```

```python
import math
from contextlib import ExitStack

import concourse.bass as bass
import numpy as np
from concourse import mybir

F32 = mybir.dt.float32
I32 = mybir.dt.int32
U32 = mybir.dt.uint32
ALU = mybir.AluOpType
ACT = mybir.ActivationFunctionType
AX = mybir.AxisListType

P = 128
T = 256
TT = T // P
D = 1024
KD = D // P
NEG = -1e30
FLOOR = -3e38
DEPTH = 2
ALPHA = (2.0 * DEPTH) ** 0.25
EPS1, EPS2 = 1e-5, 1e-6
MH, MQK, MV = 8, 64, 128
AH, NOPE, ROPE, AV, KVR, QR = 8, 128, 64, 128, 256, 384
PH, NK, TOPK, NEXP = 8, 128, 16, 128 * 128
PICKS = PH * TOPK
NCAND = 4 * TOPK + (TOPK - 4) * 4
SLOTS = 8
SHARE_FROM, PE_SLOTS = 5, 4
NH, NKV, HD = 8, 2, 64
CB, CS, NCMP, CHID = 32, 16, 15, 256
CC, CW = 256, 31
GH, GK, GV, GR, GCH = 4, 128, 256, 16, 64
FF = 2816
W2SPLIT = (512, 128, 128, 128, 128, 128, 128, 24, 512, 128, 128, 256, 16, 256)
W2AT = [sum(W2SPLIT[:i]) for i in range(len(W2SPLIT) + 1)]
BUCKETS, MAXDIST = 32, 128
VEC = 383
STRIP = 384 + NCMP + 7
RING, SLOT = 3, 4096
MORE = SLOTS // 2 * D // SLOT


def bucket_of(dist):
    half = BUCKETS // 2
    if dist < half:
        return dist
    return min(half + int(math.log(dist / half) / math.log(MAXDIST / half) * (BUCKETS - half)), BUCKETS - 1)


def constants():
    r, c = np.arange(P)[:, None], np.arange(P)[None, :]
    parts = {
        "ident": (r == c) * 1.0,
        "mask_q": np.where(c > r, NEG, 0.0),
        "mask_s": np.where(c < r, NEG, 0.0),
        "tri": ((r <= c) & (r // GCH == c // GCH)) * 1.0,
        "sel": np.repeat(np.eye(P, 8), P, axis=1),
        "freq": np.broadcast_to(10000.0 ** (-np.arange(0, ROPE, 2, dtype=np.float32) / np.float32(ROPE)), (P, ROPE // 2)),
        "seen": np.stack([(np.arange(P) >= CB - 1) * 1.0, np.ones(P)], axis=1),
        "i16": np.broadcast_to(np.arange(TOPK), (P, TOPK)),
        "minus_half": np.full((P, 32), -0.5),
    }
    onehot = np.zeros((P, 384))
    for j in range(256):
        onehot[bucket_of(255 - j), j] = 1.0
    parts["onehot"] = onehot
    parts["future"] = np.broadcast_to(np.where(np.arange(384) > 255, NEG, 0.0), (P, 384))
    at, where = 0, {}
    for k, v in parts.items():
        where[k] = (at, v.shape[1])
        at += v.shape[1]
    return np.concatenate([np.asarray(v, np.float32) for v in parts.values()], axis=1).astype(np.float32), where


def build(nc, a, consts, cwhere, scratch, out):
    ctx = ExitStack()
    with ctx:
        named = {}

        def sb(name, shape, dt=F32, stack=ctx):
            named[name] = named.get(name, 0) + 1
            name += f"_{named[name]}" if named[name] > 1 else ""
            return stack.enter_context(nc.sbuf_tensor(name, shape, dt))

        bank = [ctx.enter_context(nc.psum_tensor(f"bank{i}", [P, 512], F32)) for i in range(8)]
        CN = sb("CN", [P, consts.shape[1]])
        X = sb("X", [P, TT, D])
        Y = sb("Y", [P, TT, D])
        XT = sb("XT", [P, KD, T])
        ring = [sb(f"ring{i}", [P, SLOT]) for i in range(RING)]
        ROWS = sb("ROWS", [P, SLOTS, D])
        ring += [ROWS[:, i * SLOT // D:(i + 1) * SLOT // D, :].rearrange("p s d -> p (s d)") for i in range(MORE)]
        rows = [sb(f"rows{i}", [P, 3 - i, D]) for i in range(2)]
        stat = sb("stat", [P, 64])

        def con(name, rows_=P):
            at, n = cwhere[name]
            return CN[0:rows_, at:at + n]

        ident = con("ident")

        sems, count, base = {}, {}, {}

        def S(name):
            if name not in sems:
                sems[name] = ctx.enter_context(nc.semaphore(name))
                count[name] = 0
            return sems[name]

        def tick(name, n=1):
            S(name)
            count[name] += n
            return sems[name], n

        def now(name):
            return S(name), count[name]

        def nth(name, n):
            return S(name), base.get(name, 0) + n

        chain = {nc.vector: "dve_step", nc.scalar: "act_step", nc.gpsimd: "pool_step"}

        jobs, numbered = {}, [0]

        def job(name):
            jobs[name] = numbered[0]
            numbered[0] += 1
            return result(name)

        def result(name):
            return bank[jobs[name] % 8]

        def turn(name):
            return jobs[name] // 8 + 1

        def bank_ready(name):
            return S(f"bank_ready{jobs[name] % 8}")

        def bank_free(name):
            return S(f"bank_free{jobs[name] % 8}")

        def cols(w, c0, c1):
            return w.rearrange("(k p) n -> p k n", p=P)[:, :, c0:c1]

        stream, place = [], {}
        slot_no, slot_use = [], []
        last_gather = []

        def enter(key, ap):
            place[key] = n = len(stream)
            stream.append(ap)
            slot_no.append(n % RING if not last_gather else (n - last_gather[0]) % (RING + MORE))
            slot_use.append(slot_no[:n].count(slot_no[n]))

        def enter_cols(key, w, edges):
            for i in range(len(edges) - 1):
                enter(f"{key}{i}", cols(w, edges[i], edges[i + 1]))

        w_in = a["a_w_in"][0]
        for key, c0, c1 in (("a_gate", 2048, 2064), ("a_q", 0, 512), ("a_k", 512, 1024), ("a_v0", 1024, 1536),
                            ("a_v1", 1536, 2048), ("a_og0", 2064, 2576), ("a_og1", 2576, 3088)):
            enter(key, cols(w_in, c0, c1))
        enter_cols("a_out", a["a_w_out"][0], [0, 512, 1024])

        def enter_route(l, tag):
            enter(f"keys{tag}", a["peer_sub_keys"][l].rearrange("h c n d -> n (h c) d"))
            enter_cols(f"peer_q{tag}_", a["peer_w_q"][l], [0, 512, 1024, 1536, 2048])

        def enter_ple(l, tag):
            enter(f"ple_proj{tag}", cols(a["ple_w_proj"][l], 0, D))
            enter_cols(f"ple_gate{tag}_", a["ple_w_gate"][l], [0, 512, 1024])

        def enter_mla(tt):
            enter(f"kv_down{tt}", cols(a["kv_w_down"], 0, KVR + ROPE))
            enter(f"dq{tt}", cols(a["b_w_dq"][0], 0, QR))
            enter(f"kv_up{tt}", cols(a["kv_w_up"], 0, 2048))
            enter_cols(f"uq{tt}", a["b_w_uq"][0], [0, 768, 1536])
            enter_cols(f"b_out{tt}", a["b_w_out"][0], [0, 512, 1024])

        enter_route(0, "0")
        for tt in range(TT):
            enter_ple(0, f"0{tt}")
            enter_mla(tt)
            enter_route(1, f"1{tt}")
        for tt in range(TT):
            enter_ple(1, f"1{tt}")
        last_gather.append(len(stream))
        enter_cols("n_in", a["w_in_2"][0], [0, 512, 1024, 1304, 1816, 2328, 2600])
        for s in "kv":
            enter(f"w1{s}", a[f"cmp_w1_{s}_2"][0].rearrange("(j p) n -> p j n", p=P))
        enter_cols("n_out", a["w_out_2"][0], [0, 512, 1024])
        ffe = list(range(0, FF, 512)) + [FF]
        for i in range(len(ffe) - 1):
            enter(f"ffg{i}", cols(a["ffn_w_gate_2"][0], ffe[i], ffe[i + 1]))
            enter(f"ffu{i}", cols(a["ffn_w_up_2"][0], ffe[i], ffe[i + 1]))
        for cb in range(2):
            for i, (k0, k1) in enumerate(((0, 8), (8, 16), (16, 22))):
                enter(f"ffd{cb}{i}", cols(a["ffn_w_down_2"][0], cb * 512, cb * 512 + 512)[:, k0:k1, :])
        enter("ple2_proj", cols(a["ple_w_proj_2"][0], 0, D))
        enter_cols("ple2_gate", a["ple_w_gate_2"][0], [0, 512, 1024])

        def slot_view(n):
            _, k, m = stream[n].shape
            return ring[slot_no[n]][:, 0:k * m].rearrange("p (k m) -> p k m", k=k)

        taken, released = [0], {}

        def landed(key):
            n = place[key]
            assert n == taken[0], (key, n, taken[0])
            taken[0] += 1
            return S(f"weight_in{slot_no[n]}"), 16 * (slot_use[n] + 1)

        def slot_of(key):
            return slot_view(place[key])

        def weight_read(key, name):
            released[place[key]] = jobs[name]

        mm, tr = nc.tensor.matmul, nc.tensor.transpose

        def mul(out_, lhsT, rhs, start, stop):
            return mm(out_, lhsT, rhs, start=start, stop=stop, skip_group_check=True)

        BOTH = tuple(range(TT))

        def pe_turn(pe, tag, src, wait_name, nk=KD, tiles=BOTH):
            for tt in tiles:
                if wait_name:
                    pe.wait_ge(*nth(wait_name, tt + 1))
                for g in range(0, nk, 4):
                    b = job(f"{tag}{tt}{g // 4}")
                    if turn(f"{tag}{tt}{g // 4}") > 1:
                        pe.wait_ge(bank_free(f"{tag}{tt}{g // 4}"), turn(f"{tag}{tt}{g // 4}") - 1)
                    n = min(4, nk - g)
                    for j in range(n):
                        last = tr(b[:, j * P:(j + 1) * P], src[:, tt, (g + j) * P:(g + j + 1) * P], ident)
                    last.then_inc(bank_ready(f"{tag}{tt}{g // 4}"), 1)

        def take_turn(e, tag, dst, groups, nk=KD):
            for tt, g in groups:
                e.wait_ge(bank_ready(f"{tag}{tt}{g}"), turn(f"{tag}{tt}{g}"))
                b = result(f"{tag}{tt}{g}")
                n = min(4, nk - 4 * g)
                o = dst[:, 4 * g:4 * g + n, tt * P:(tt + 1) * P]
                i = b[:, 0:n * P].rearrange("p (k t) -> p k t", k=n)
                copy(e, o, i).then_inc(bank_free(f"{tag}{tt}{g}"), 1)

        def copy(e, o, i, scale=None):
            if e is nc.scalar:
                return nc.scalar.activation(o, i, ACT.Copy, scale=scale or 1.0)
            if scale:
                return nc.vector.tensor_scalar(o, i, scale, None, ALU.mult)
            return nc.vector.tensor_copy(o, i)

        def pe_rows(pe, w, name, lhs, tt, c0, n):
            b = job(name)
            if turn(name) > 1:
                pe.wait_ge(bank_free(name), turn(name) - 1)
            k = w.shape[1]
            for i in range(k):
                last = mul(b[:, 0:n], lhs[:, i, tt * P:(tt + 1) * P], w[:, i, c0:c0 + n], i == 0, i == k - 1)
            last.then_inc(bank_ready(name), 1)
            return last

        def pe_colpair(pe, w, name, rhs, starts, m=P, t=slice(0, T)):
            n = t.stop - t.start
            b = job(name)
            if turn(name) > 1:
                pe.wait_ge(bank_free(name), turn(name) - 1)
            k = w.shape[1]
            for s, c in enumerate(starts):
                for i in range(k):
                    last = mul(b[0:m, s * n:(s + 1) * n], w[:, i, c:c + m], rhs[:, i, t], i == 0, i == k - 1)
            last.then_inc(bank_ready(name), 1)
            return last

        def pair(b, m=P):
            return b[0:m, 0:2 * T].rearrange("p (s t) -> p s t", s=2)

        V = nc.vector
        A = nc.scalar
        G = nc.gpsimd

        def pool_power(name_in, n_in, name_out, cells):
            G.wait_ge(*nth(name_in, n_in))
            at, _ = cwhere["minus_half"]
            G.tensor_tensor(cells, cells, CN[:, at:at + cells.shape[1]], ALU.pow).then_inc(*tick(name_out))
            G.wait_ge(*now(name_out))

        def act_root(name_in, n_in, name_out, cells, root):
            A.wait_ge(*nth(name_in, n_in))
            A.activation(root, cells, ACT.Sqrt).then_inc(*tick(name_out))
            A.wait_ge(*now(name_out))

        def dve_rstd(cells, root):
            V.reciprocal(root, root).then_inc(*tick("dve_step"))
            V.wait_ge(*now("dve_step"))
            V.tensor_tensor(cells, cells, root, ALU.mult).then_inc(*tick("dve_step"))
            V.wait_ge(*now("dve_step"))
            V.tensor_tensor(cells, cells, root, ALU.mult).then_inc(*tick("dve_step"))
            V.wait_ge(*now("dve_step"))
            V.tensor_scalar(cells, cells, -0.5, 1.5, ALU.mult, ALU.add).then_inc(*tick("dve_step"))
            V.wait_ge(*now("dve_step"))
            V.tensor_tensor(cells, cells, root, ALU.mult).then_inc(*tick("dve_step"))
            V.wait_ge(*now("dve_step"))

        def dve_residual(tag, scale, tiles=BOTH):
            for tt in tiles:
                for cb in range(2):
                    s = slice(cb * 512, cb * 512 + 512)
                    V.wait_ge(bank_ready(f"{tag}{cb}{tt}"), turn(f"{tag}{cb}{tt}"))
                    b = result(f"{tag}{cb}{tt}")
                    V.scalar_tensor_tensor(Y[:, tt, s], X[:, tt, s], scale, b[:, :], ALU.mult, ALU.add).then_inc(bank_free(f"{tag}{cb}{tt}"), 1)
            for name in [f"{tag}{cb}{tt}" for tt in tiles for cb in range(2)]:
                V.wait_ge(bank_free(name), turn(name))

        def dve_layer_norm(src, dst, g, b, eps, key, done, tiles=BOTH, root=False):
            n = src.shape[2]
            for tt in tiles:
                pieces = max(1, n // 512)
                for c in range(pieces):
                    w = n // pieces
                    V.bn_stats(stat[:, 16 + 6 * c:22 + 6 * c], src[:, tt, c * w:(c + 1) * w]).then_inc(*tick("dve_step"))
                    V.wait_ge(*now("dve_step"))
                V.bn_aggr(stat[:, 4 * tt:4 * tt + 2], stat[:, 16:16 + 6 * pieces]).then_inc(*tick("dve_step"))
                V.wait_ge(*now("dve_step"))
                V.tensor_scalar(stat[:, 8 + tt:9 + tt], stat[:, 4 * tt + 1:4 * tt + 2], eps, None, ALU.add).then_inc(*tick(key + "_var"))
                V.wait_ge(*now(key + "_var"))
            if root:
                V.wait_ge(*nth(key + "_root", 1))
                dve_rstd(stat[:, 8 + tiles[0]:9 + tiles[-1]], stat[:, 48 + tiles[0]:49 + tiles[-1]])
            else:
                V.wait_ge(*nth(key + "_rstd", 1))
            for tt in tiles:
                V.scalar_tensor_tensor(src[:, tt, :], src[:, tt, :], stat[:, 4 * tt:4 * tt + 1], g, ALU.subtract, ALU.mult).then_inc(*tick("dve_step"))
                V.wait_ge(*now("dve_step"))
                V.scalar_tensor_tensor(dst[:, tt, :], src[:, tt, :], stat[:, 8 + tt:9 + tt], b, ALU.mult, ALU.add).then_inc(*tick(done))
                V.wait_ge(*now(done))

        def pool_layer_norm(key):
            pool_power(key + "_var", TT, key + "_rstd", stat[:, 8:8 + TT])

        def act_squares(src, junk, name, n):
            for tt in range(TT):
                A.activation(junk[:, tt, 0:n], src[:, tt, 0:n], ACT.Square, accum_out=stat[:, 12 + tt:13 + tt]).then_inc(*tick(name))
                A.wait_ge(*now(name))

        def dve_mean_square(key, n, eps):
            V.wait_ge(*nth(key + "_sq", TT))
            V.tensor_scalar(stat[:, 12:14], stat[:, 12:14], 1.0 / n, eps, ALU.mult, ALU.add).then_inc(*tick(key + "_var"))
            V.wait_ge(*now(key + "_var"))
            V.wait_ge(*nth(key + "_rstd", 1))

        meetings = [0, 0]

        def end_phase(block, with_pool):
            meetings[0] += 3
            meetings[1] += with_pool
            n, m = meetings

            def meet(e):
                if e in chain and count.get(chain[e]):
                    e.wait_ge(S(chain[e]), count[chain[e]])
                e.sem_inc(S("phase_end"), 1)
                e.wait_ge(S("phase_end"), n)
                if with_pool:
                    e.wait_ge(S("pool_here"), m)

            def pool_meets():
                if count.get("pool_step"):
                    G.wait_ge(S("pool_step"), count["pool_step"])
                G.sem_inc(S("pool_here"), 1)
                G.wait_ge(S("phase_end"), n)

            block.tensor(lambda e: meet(nc.tensor))
            block.scalar(lambda e: meet(A))
            block.vector(lambda e: meet(V))
            if with_pool:
                block.gpsimd(lambda e: pool_meets())
            base.clear()
            base.update(count)
            jobs.clear()

        rows_total = [0, 0]

        def load_rows(which, aps):
            for i, ap in enumerate(aps):
                G.dma_start(rows[which][:, i, 0:ap.shape[-1]], ap.partition_broadcast(P)).then_inc(S(f"rows_in{which}"), 16)

        def rows_here(which, n):
            rows_total[which] += 16 * n
            V.wait_ge(S(f"rows_in{which}"), rows_total[which])

        PE = nc.tensor

        BIF = sb("BIF", [MH, 2])
        POS = sb("POS", [P, TT], I32)
        SMALL = sb("SMALL", [P, KVR + QR + 3 * CC + GK])
        RELB = sb("RELB", [BUCKETS, NH])
        B1 = sb("B1", [P, 2, 2])
        W2 = sb("W2", [P, 2, 2, HD])
        CPOS = sb("CPOS", [CB // 2, 2, P])
        CONVW = sb("CONVW", [CW, CC])
        CONVB = sb("CONVB", [P, 2])
        WAL = sb("WAL", [GR, GK])
        PIN = sb("PIN", [P, 3, TT, 256])
        small_at, at = {}, 0
        small_src = [("kv_norm_g", a["kv_norm_g"]), ("b_q_norm_g", a["b_q_norm_g"][0]), ("conv_ln_g_2", a["conv_ln_g_2"][0]),
                     ("conv_ln_b_2", a["conv_ln_b_2"][0]), ("gla_norm_g_2", a["gla_norm_g_2"][0]), ("gla_b_alpha_2", a["gla_b_alpha_2"][0])]
        params = [(POS[:, :], a["positions"][0].rearrange("(t p) -> p t", p=P)), (RELB[:, :], a["rel_bias_2"]),
                  (CONVW[:, :], a["conv_w_2"][0]), (CONVB[:, :], a["conv_b_2"][0].rearrange("(t p) -> p t", p=P)),
                  (WAL[:, :], a["gla_w_alpha_2"][0])]
        for k, src in small_src:
            n = src.shape[0]
            small_at[k] = (at, n)
            params.append((SMALL[:, at:at + n], src.partition_broadcast(P)))
            at += n
        for i, s in enumerate("kv"):
            params.append((B1[:, i, :], a[f"cmp_b1_{s}_2"][0].rearrange("(t p) -> p t", p=P)))
            params.append((W2[:, i, :, :], a[f"cmp_w2_{s}_2"][0].rearrange("(t p) d -> p t d", p=P)))
            params.append((CPOS[:, i, :], a[f"cmp_pos_{s}_2"][0].rearrange("(j e) d -> j (e d)", e=2)))
        for i, src in enumerate((a["p"][0, 0], a["p"][1, 0], a["p_2"][0, 0])):
            params.append((PIN[:, i, :, :], src.rearrange("(t p) d -> p t d", p=P)))

        def small(k):
            at, n = small_at[k]
            return SMALL[:, at:at + n]

        def params_here(e):
            e.wait_ge(S("params_in"), 16 * len(params))

        def store_and_load(block):
            @block.sync
            def _(sp):
                sp.dma_start(X[:, :, :], a["x"][0].rearrange("(t p) d -> p t d", p=P)).then_inc(S("first_in"), 16)
                sp.dma_start(CN[:, :], consts).then_inc(S("first_in"), 16)
                with nc.allow_non_contiguous_dma(reason="16 gate biases"):
                    sp.dma_start(BIF[:, :], a["a_b_if"][0].rearrange("t h -> h t")).then_inc(S("first_in"), 16)
                for n, ap in enumerate(stream):
                    before = [m for m in range(n) if slot_no[m] == slot_no[n]]
                    if before:
                        j = released[before[-1]]
                        sp.wait_ge(sems[f"bank_ready{j % 8}"], j // 8 + 1)
                    elif n >= RING:
                        sp.wait_ge(row_used, SLOTS + dve_used(len(passes), 0))
                    sp.dma_start(slot_view(n), ap).then_inc(S(f"weight_in{slot_no[n]}"), 16)
                sp.wait_ge(S("out_ready"), TT)
                sp.dma_start(out[0].rearrange("(t p) d -> p t d", p=P), Y[:, :, :]).then_inc(S("out_stored"), 16)
                sp.wait_ge(S("out_stored"), 16)

        def logsig_steps(tmp, name):
            A.wait_ge(*nth(name + "_abs", 1))
            A.activation(tmp, tmp, ACT.Exp, scale=-1.0).then_inc(*tick("act_step"))
            A.wait_ge(*now("act_step"))
            A.activation(tmp, tmp, ACT.Ln, bias=1.0).then_inc(*tick(name + "_ln"))
            A.wait_ge(*now(name + "_ln"))

        def mlstm(block, st):
            QT = sb("QT", [P, MH // 2, T], F32, st)
            KT = sb("KT", [P, MH // 2, T], F32, st)
            VA = sb("VA", [P, TT, MH, MV + 1], F32, st)
            OG = sb("OG", [P, TT, D], F32, st)
            GA = sb("GA", [MH, 8, T], F32, st)
            IG, GF, LN, CUM, GM, MM, NM, NMT = (GA[:, i, :] for i in range(8))
            ONE8 = sb("ONE8", [MH, T], F32, st)
            GTS = sb("GTS", [P, TT, MH], F32, st)
            EMS = sb("EMS", [P, TT, MH], F32, st)
            DN = sb("DN", [P, MH, TT], F32, st)
            WT = [sb(f"WT{i}", [P, 384], F32, st) for i in range(2)]
            PT = [sb(f"PT{i}", [P, 384], F32, st) for i in range(2)]
            BST = sb("BST", [P, TT, 6], F32, st)
            MV2 = sb("MV2", [P, MH, TT, 2], F32, st)
            VR = sb("VR", [P, MH, TT], F32, st)
            NMR = sb("NMR", [P, MH, TT], F32, st)
            sel = con("sel", MH)

            @block.tensor
            def _(pe):
                pe.wait_ge(S("first_in"), 48)
                pe_turn(PE, "xt", X, None)
                pe.wait_ge(bank_free("xt00"), turn("xt00"))
                pe.wait_ge(bank_free("xt01"), turn("xt01"))
                pe.wait_ge(bank_free("xt10"), turn("xt10"))
                pe.wait_ge(bank_free("xt11"), turn("xt11"))
                pe.wait_ge(*landed("a_gate"))
                w = slot_of("a_gate")
                pe_colpair(PE, w, "gate", XT, [0, MH], MH)
                weight_read("a_gate", "gate")
                for s in "qk":
                    pe.wait_ge(*landed(f"a_{s}"))
                    w = slot_of(f"a_{s}")
                    for i in range(2):
                        pe_colpair(PE, w, f"{s}{i}", XT, [256 * i, 256 * i + 128])
                    weight_read(f"a_{s}", f"{s}1")
                for s in ("v", "og"):
                    for cb in range(2):
                        pe.wait_ge(*landed(f"a_{s}{cb}"))
                        w = slot_of(f"a_{s}{cb}")
                        for tt in range(TT):
                            pe_rows(PE, w, f"{s}{cb}{tt}", XT, tt, 0, 512)
                        weight_read(f"a_{s}{cb}", f"{s}{cb}1")
                pe.wait_ge(*nth("gates_done", 1))
                b = job("gt")
                if turn("gt") > 1:
                    PE.wait_ge(bank_free("gt"), turn("gt") - 1)
                for i in range(TT):
                    tr(b[:, i * MH:(i + 1) * MH], GM[:, i * P:(i + 1) * P], ident[0:MH, 0:MH])
                for i in range(TT):
                    last = tr(b[:, (TT + i) * MH:(TT + i + 1) * MH], NMT[:, i * P:(i + 1) * P], ident[0:MH, 0:MH])
                last.then_inc(bank_ready("gt"), 1)
                for i in range(MH + 1):
                    if i < MH:
                        h, hp = i, i // 2
                        b = job(f"w{h}")
                        if turn(f"w{h}") > 1:
                            PE.wait_ge(bank_free(f"w{h}"), turn(f"w{h}") - 1)
                        sh = sel[:, h * P:(h + 1) * P]
                        mul(b[:, 0:T], sh, NM, True, False)
                        mul(b[:, 0:P], ident, con("mask_s"), False, True)
                        mul(b[:, T:T + P], sh, NM[:, P:T], True, False)
                        mul(b[:, T:T + P], ident, con("mask_s"), False, True).then_inc(bank_ready(f"w{h}"), 1)
                        r = slice(64 * (h % 2), 64 * (h % 2) + 64)
                        if h == 0:
                            pe.wait_ge(bank_free("q0"), turn("q0"))
                            pe.wait_ge(bank_free("q1"), turn("q1"))
                            pe.wait_ge(bank_free("k0"), turn("k0"))
                            pe.wait_ge(bank_free("k1"), turn("k1"))
                        b = job(f"s{h}")
                        if turn(f"s{h}") > 1:
                            PE.wait_ge(bank_free(f"s{h}"), turn(f"s{h}") - 1)
                        mul(b[:, 0:T], KT[r, hp, 0:P], QT[r, hp, :], True, True)
                        mul(b[:, T:T + P], KT[r, hp, P:T], QT[r, hp, P:T], True, True).then_inc(bank_ready(f"s{h}"), 1)
                    if i >= 1:
                        h = i - 1
                        pe.wait_ge(bank_free(f"s{h}"), turn(f"s{h}"))
                        if h == 0:
                            for name in [f"v{cb}{tt}" for cb in range(2) for tt in range(TT)]:
                                pe.wait_ge(bank_free(name), turn(name))
                        b = job(f"n{h}")
                        if turn(f"n{h}") > 1:
                            PE.wait_ge(bank_free(f"n{h}"), turn(f"n{h}") - 1)
                        n = MV + 1
                        mul(b[:, 0:n], PT[h % 2][:, 0:P], VA[:, 0, h, :], True, True)
                        mul(b[:, n:2 * n], PT[h % 2][:, P:T], VA[:, 0, h, :], True, False)
                        mul(b[:, n:2 * n], PT[h % 2][:, T:T + P], VA[:, 1, h, :], False, True).then_inc(bank_ready(f"n{h}"), 1)
                pe_turn(PE, "yt", Y, "y_ready")
                pe.wait_ge(bank_free("yt00"), turn("yt00"))
                pe.wait_ge(bank_free("yt01"), turn("yt01"))
                pe.wait_ge(bank_free("yt10"), turn("yt10"))
                pe.wait_ge(bank_free("yt11"), turn("yt11"))
                for tt in range(TT):
                    for cb in range(2):
                        if tt == 0:
                            pe.wait_ge(*landed(f"a_out{cb}"))
                        pe_rows(PE, slot_of(f"a_out{cb}"), f"o{cb}{tt}", XT, tt, 0, 512)
                for cb in range(2):
                    weight_read(f"a_out{cb}", f"o{cb}1")

            @block.scalar
            def _(act):
                with nc.allow_non_contiguous_dma(reason="a few hundred parameters"):
                    for o, i in params:
                        act.dma_start(o, i).then_inc(S("params_in"), 16)
                take_turn(A, "xt", XT, [(0, 0), (1, 0)])
                logsig_steps(LN, "gate")
                for s, dst in (("q", QT), ("k", KT)):
                    for i in range(2):
                        A.wait_ge(bank_ready(f"{s}{i}"), turn(f"{s}{i}"))
                        b = result(f"{s}{i}")
                        copy(A, dst[:, 2 * i:2 * i + 2, :], pair(b)).then_inc(bank_free(f"{s}{i}"), 1)
                for cb in range(2):
                    for tt in range(TT):
                        A.wait_ge(bank_ready(f"v{cb}{tt}"), turn(f"v{cb}{tt}"))
                        b = result(f"v{cb}{tt}")
                        copy(A, VA[:, tt, 4 * cb:4 * cb + 4, 0:MV], b[:, :].rearrange("p (h v) -> p h v", h=4)).then_inc(bank_free(f"v{cb}{tt}"), 1)
                for cb in range(2):
                    for tt in range(TT):
                        A.wait_ge(bank_ready(f"og{cb}{tt}"), turn(f"og{cb}{tt}"))
                        b = result(f"og{cb}{tt}")
                        A.activation(OG[:, tt, cb * 512:cb * 512 + 512], b[:, :], ACT.Sigmoid).then_inc(bank_free(f"og{cb}{tt}"), 1)
                A.wait_ge(bank_ready("gt"), turn("gt"))
                b = result("gt")
                A.activation(GTS[:, :, :], b[:, 0:2 * MH].rearrange("p (t h) -> p t h", t=TT), ACT.Copy).then_inc(*tick("act_step"))
                A.wait_ge(*now("act_step"))
                A.activation(EMS[:, :, :], b[:, 2 * MH:4 * MH].rearrange("p (t h) -> p t h", t=TT), ACT.Exp).then_inc(bank_free("gt"), 1)
                def normalise(h):
                    A.wait_ge(*nth("head_stats", h + 1))
                    for tt in range(TT):
                        y = Y[:, tt, h * MV:(h + 1) * MV]
                        A.activation(y, y, ACT.Identity, scale=VR[:, h, tt:tt + 1], bias=NMR[:, h, tt:tt + 1]).then_inc(*tick("head_normed"))

                for h in range(MH):
                    A.wait_ge(bank_ready(f"w{h}"), turn(f"w{h}"))
                    b = result(f"w{h}")
                    if h >= 2:
                        A.wait_ge(bank_free(f"s{h - 2}"), turn(f"s{h - 2}"))
                    A.activation(WT[h % 2][:, 0:T], b[:, 0:T], ACT.Exp, bias=GTS[:, 0, h:h + 1]).then_inc(*tick("act_step"))
                    A.activation(WT[h % 2][:, T:T + P], b[:, T:T + P], ACT.Exp, bias=GTS[:, 1, h:h + 1]).then_inc(bank_free(f"w{h}"), 1)
                    if h >= 3:
                        normalise(h - 3)
                for h in range(MH - 3, MH):
                    normalise(h)
                take_turn(A, "yt", XT, [(0, 0), (1, 0)])

            @block.vector
            def _(dve):
                V.memset(ONE8[:, :], 1.0).then_inc(*tick("dve_step"))
                V.memset(VA[:, :, :, MV:MV + 1], 1.0).then_inc(*tick("dve_step"))
                take_turn(V, "xt", XT, [(0, 1), (1, 1)])
                V.wait_ge(bank_ready("gate"), turn("gate"))
                b = result("gate")
                dve.wait_ge(S("first_in"), 48)
                V.tensor_scalar(IG, b[0:MH, 0:T], BIF[:, 0:1], None, ALU.add).then_inc(*tick("dve_step"))
                V.wait_ge(*now("dve_step"))
                V.tensor_scalar(GF, b[0:MH, T:2 * T], BIF[:, 1:2], None, ALU.add).then_inc(bank_free("gate"), 1)
                V.wait_ge(bank_free("gate"), turn("gate"))
                V.scalar_tensor_tensor(LN, GF, -1.0, GF, ALU.mult, ALU.max).then_inc(*tick("gate_abs"))
                V.wait_ge(*now("gate_abs"))
                V.wait_ge(*nth("gate_ln", 1))
                V.scalar_tensor_tensor(GF, GF, 0.0, LN, ALU.min, ALU.subtract).then_inc(*tick("dve_step"))
                V.wait_ge(*now("dve_step"))
                V.tensor_tensor_scan(CUM, ONE8[:, :], GF, 0.0, ALU.mult, ALU.add).then_inc(*tick("dve_step"))
                V.wait_ge(*now("dve_step"))
                V.tensor_tensor(GM, IG, CUM, ALU.subtract).then_inc(*tick("dve_step"))
                V.wait_ge(*now("dve_step"))
                V.tensor_tensor_scan(MM, GM, GM, 0.0, ALU.max, ALU.max).then_inc(*tick("dve_step"))
                V.wait_ge(*now("dve_step"))
                V.tensor_scalar(NM, MM, -1.0, None, ALU.mult).then_inc(*tick("dve_step"))
                V.wait_ge(*now("dve_step"))
                V.scalar_tensor_tensor(NMT, CUM, -1.0, MM, ALU.mult, ALU.subtract).then_inc(*tick("gates_done"))
                V.wait_ge(*now("gates_done"))
                V.wait_ge(bank_free("gt"), turn("gt"))
                rows_here(0, 3)
                for name in [f"og{cb}{tt}" for cb in range(2) for tt in range(TT)]:
                    V.wait_ge(bank_free(name), turn(name))
                V.tensor_tensor(OG[:, :, :], OG[:, :, :], rows[0][:, 0:1, :].broadcast_to([P, TT, D]), ALU.mult).then_inc(*tick("dve_step"))
                V.wait_ge(*now("dve_step"))
                for i in range(MH + 2):
                    if i < MH:
                        h = i
                        V.wait_ge(bank_ready(f"s{h}"), turn(f"s{h}"))
                        b = result(f"s{h}")
                        V.wait_ge(bank_free(f"w{h}"), turn(f"w{h}"))
                        if h >= 2:
                            V.wait_ge(bank_ready(f"n{h - 2}"), turn(f"n{h - 2}"))
                        V.scalar_tensor_tensor(PT[h % 2][:, :], b[:, 0:384], MQK ** -0.5, WT[h % 2][:, :], ALU.mult, ALU.mult).then_inc(bank_free(f"s{h}"), 1)
                    if i >= 2:
                        h = i - 2
                        V.wait_ge(*nth("h_rstd", h + 1))
                        V.scalar_tensor_tensor(NMR[:, h, :], MV2[:, h, :, 0], -1.0, VR[:, h, :], ALU.mult, ALU.mult).then_inc(*tick("head_stats"))
                    if 1 <= i <= MH:
                        h = i - 1
                        V.wait_ge(bank_ready(f"n{h}"), turn(f"n{h}"))
                        b = result(f"n{h}")
                        n2 = b[:, 0:2 * (MV + 1)].rearrange("p (t v) -> p t v", t=TT)
                        V.tensor_tensor(DN[:, h, :], n2[:, :, MV], EMS[:, :, h], ALU.max).then_inc(*tick("dve_step"))
                        V.wait_ge(*now("dve_step"))
                        V.scalar_tensor_tensor(DN[:, h, :], n2[:, :, MV], -1.0, DN[:, h, :], ALU.mult, ALU.max).then_inc(*tick("dve_step"))
                        V.wait_ge(*now("dve_step"))
                        V.reciprocal(DN[:, h, :], DN[:, h, :]).then_inc(*tick("dve_step"))
                        V.wait_ge(*now("dve_step"))
                        V.tensor_scalar(Y[:, 0, h * MV:(h + 1) * MV], n2[:, 0, 0:MV], DN[:, h, 0:1], None, ALU.mult).then_inc(*tick("dve_step"))
                        V.tensor_scalar(Y[:, 1, h * MV:(h + 1) * MV], n2[:, 1, 0:MV], DN[:, h, 1:2], None, ALU.mult).then_inc(bank_free(f"n{h}"), 1)
                        V.wait_ge(bank_free(f"n{h}"), turn(f"n{h}"))
                        for tt in range(TT):
                            V.bn_stats(BST[:, tt, :], Y[:, tt, h * MV:(h + 1) * MV]).then_inc(*tick("dve_step"))
                        V.wait_ge(*now("dve_step"))
                        for tt in range(TT):
                            V.bn_aggr(MV2[:, h, tt, :], BST[:, tt, :]).then_inc(*tick("dve_step"))
                        V.wait_ge(*now("dve_step"))
                        V.tensor_scalar(VR[:, h, :], MV2[:, h, :, 1], EPS1, None, ALU.add).then_inc(*tick("h_var"))
                V.wait_ge(*nth("head_normed", MH * TT))
                for tt in range(TT):
                    V.tensor_tensor(Y[:, tt, :], Y[:, tt, :], OG[:, tt, :], ALU.mult).then_inc(*tick("y_ready"))
                take_turn(V, "yt", XT, [(0, 1), (1, 1)])
                for tt in range(TT):
                    dve_residual("o", ALPHA, tiles=(tt,))
                    dve_layer_norm(Y, X, rows[0][:, 1, :], rows[0][:, 2, :], EPS1, f"a_ln{tt}", "x_ready", tiles=(tt,))

            @block.gpsimd
            def _(pool):
                load_rows(0, [a["a_hn_g"][0], a["ln_g"][0, 0], a["ln_b"][0, 0]])
                pool.wait_ge(S("first_in"), 48)
                for h in range(MH):
                    pool_power("h_var", h + 1, "h_rstd", VR[:, h, :])
                for tt in range(TT):
                    pool_power(f"a_ln{tt}_var", 1, f"a_ln{tt}_rstd", stat[:, 8 + tt:9 + tt])

        peer_mem = ctx.enter_context(ExitStack())
        IDX = sb("IDX", [P, TT, PICKS], I32, peer_mem)
        GATE = sb("GATE", [P, TT, PICKS], F32, peer_mem)
        ACTV = sb("ACTV", [P, TT, PICKS], F32, peer_mem)
        CUR = [sb(f"CUR{i}", [P, SLOTS], I32, peer_mem) for i in range(2)]
        ODD = sb("ODD", [P, D], F32, peer_mem)
        ROWBUF = [ROWS[:, s, :] for s in range(SLOTS)]
        passes = [(l, tt, table) for l in range(2) for tt in range(TT) for table in "uv"]
        row_in = [S(f"row_in{s}") for s in range(SLOTS)]
        row_used, cur_ready, pick_go, picks_ready = S("row_used"), S("cur_ready"), S("pick_go"), S("picks_ready")
        pe_used, diag_ready = S("pe_used"), S("diag_ready")
        GROUPS = PICKS // SLOTS
        shared = [l == (1 - tt) and table == "v" for l, tt, table in passes]

        def by_pe(n, g):
            return shared[n] and g >= SHARE_FROM

        def dve_used(n, g):
            return sum(SLOTS - PE_SLOTS * by_pe(m, h) for m in range(len(passes)) for h in range(GROUPS) if (m, h) < (n, g))

        def tensor_used(n, g):
            return sum(PE_SLOTS * by_pe(m, h) for m in range(len(passes)) for h in range(GROUPS) if (m, h) < (n, g))

        def issue_gathers(block):
            tables = {s: a[f"peer_{s}"].rearrange("l e d -> (l e) d") for s in "uv"}

            def issue(n, g, i, step, pe_step, cur):
                l, tt, table = passes[n]
                m, h = (n, g - 1) if g else (n - 1, GROUPS - 1)
                before = SLOTS + dve_used(m, h) if m >= 0 else 0
                nc.gpsimd.tensor_copy(cur[:, :], IDX[:, tt, bass.ds(i * SLOTS + g * SLOTS, SLOTS)]).then_inc(cur_ready, 1)
                G.wait_ge(cur_ready, i + (n * GROUPS + g + 1))
                G.sem_inc(pick_go, 1)
                for s in range(SLOTS):
                    if s % 2 == 0 and m >= 0 and by_pe(m, h) and s >= SLOTS - PE_SLOTS:
                        G.wait_ge(pe_used, i * pe_step + (tensor_used(m, h) + s + 2 - (SLOTS - PE_SLOTS)))
                        G.sem_inc(pick_go, 1)
                    elif s % 2 == 0:
                        G.wait_ge(row_used, i * step + (before + s + 2))
                        G.sem_inc(pick_go, 1)
                    nc.gpsimd.indirect_dma_start(ROWBUF[s][:, :], None, tables[table],
                                                 bass.IndirectOffsetOnAxis(cur[:, s:s + 1], axis=0)).then_inc(row_in[s], 16)

            @block.gpsimd
            def _(pool):
                for n, (l, tt, table) in enumerate(passes):
                    if table == "u":
                        pool.wait_ge(picks_ready, 2 * (TT * l + tt) + 1)
                    if n == 0:
                        load_rows(0, [a["ln_g"][1, 0], a["ln_b"][1, 0], a["mix_norm_g_2"][0]])
                        load_rows(1, [a["ln_g"][0, 1], a["ln_b"][0, 1]])
                    if (l, tt, table) == (1, 0, "v"):
                        pool.wait_ge(S("tile_done"), TT)
                        load_rows(1, [a["ln_g"][1, 1], a["ln_b"][1, 1]])
                    for g in range(2):
                        issue(n, g, 0, 0, 0, CUR[g])

                    def stretch(g0, g1, step, pe_step):
                        with pool.Fori(0, (g1 - g0) // 2) as j:
                            for half in range(2):
                                issue(n, g0 + half, j * 2, step, pe_step, CUR[half])

                    if table == "u":
                        stretch(2, GROUPS // 2, SLOTS, 0)
                        pool.wait_ge(picks_ready, 2 * (TT * l + tt) + 2)
                        stretch(GROUPS // 2, GROUPS, SLOTS, 0)
                    elif shared[n]:
                        stretch(2, SHARE_FROM + 1, SLOTS, 0)
                        stretch(SHARE_FROM + 1, GROUPS, SLOTS - PE_SLOTS, PE_SLOTS)
                    else:
                        stretch(2, GROUPS, SLOTS, 0)

        under_way = {"pass": None, "group": GROUPS}

        def gather_begin(n):
            under_way.update({"pass": n, "group": 0})

        def gather_some(k):
            n, g0 = under_way["pass"], under_way["group"]
            g1 = min(g0 + k, GROUPS)
            if g0 < g1:
                under_way["group"] = g1
                split = min(max(g0, SHARE_FROM), g1) if shared[n] else g1
                for lo, hi, slots in ((g0, split, SLOTS), (split, g1, SLOTS - PE_SLOTS)):
                    if lo < hi:
                        use_rows(n, lo, hi, slots)

        def use_rows(n, lo, hi, slots):
            l, tt, table = passes[n]
            used0 = SLOTS + dve_used(n, lo)
            in0 = n * GROUPS + lo
            with V.Fori(0, hi - lo) as i:
                for s in range(slots):
                    if table == "u":
                        V.wait_ge(row_in[s], i * 16 + 16 * (in0 + 1))
                        V.scalar_tensor_tensor(ROWBUF[s][:, :], ROWBUF[s][:, :], 1.0, X[:, tt, :], ALU.mult, ALU.mult,
                                               accum_out=ACTV[:, tt, bass.ds(i * SLOTS + (lo * SLOTS + s), 1)]).then_inc(row_used, 1)
                    else:
                        total = ODD[:, :] if s % 2 else Y[:, tt, :]
                        V.wait_ge(row_used, i * slots + (used0 + s - 1))
                        V.wait_ge(row_in[s], i * 16 + 16 * (in0 + 1))
                        V.scalar_tensor_tensor(total, ROWBUF[s][:, :], GATE[:, tt, bass.ds(i * SLOTS + (lo * SLOTS + s), 1)], total,
                                               ALU.mult, ALU.add).then_inc(row_used, 1)

        def gather_rest():
            gather_some(GROUPS)
            V.wait_ge(row_used, SLOTS + dve_used(under_way["pass"] + 1, 0))

        share = [(g, s) for g in range(SHARE_FROM, GROUPS) for s in range(SLOTS - PE_SLOTS, SLOTS)]

        def pe_share(n, DG):
            for name in ("accA", "accB"):
                job(name)
                if turn(name) > 1:
                    PE.wait_ge(bank_free(name), turn(name) - 1)
            accs = result("accA"), result("accB")
            for x, (g, s) in enumerate(share):
                PE.wait_ge(row_in[s], 16 * (n * GROUPS + g + 1))
                PE.wait_ge(diag_ready, tensor_used(n, SHARE_FROM) + x + 1)
                end = x == len(share) - 1
                d, row = DG[s % PE_SLOTS], ROWBUF[s]
                last = mul(accs[0][:, :], d[:, :], row[:, 0:512], x == 0, end)
                if end:
                    last.then_inc(bank_ready("accA"), 1)
                    mul(accs[1][:, 0:256], d[:, :], row[:, 512:768], False, True).then_inc(bank_ready("accB"), 1)
                    mul(accs[1][:, 256:512], d[:, :], row[:, 768:1024], False, True).then_inc(pe_used, 1)
                else:
                    mul(accs[1][:, :], d[:, :], row[:, 512:1024], x == 0, False).then_inc(pe_used, 1)

        def act_share(n, DG):
            tt = passes[n][1]
            for x, (g, s) in enumerate(share):
                if x >= PE_SLOTS:
                    A.wait_ge(pe_used, tensor_used(n, SHARE_FROM) + x + 1 - PE_SLOTS)
                A.activation(DG[s % PE_SLOTS][:, :], ident, ACT.Copy, scale=GATE[:, tt, g * SLOTS + s:g * SLOTS + s + 1]).then_inc(diag_ready, 1)

        def dve_share(n):
            tt = passes[n][1]
            gather_rest()
            V.wait_ge(pe_used, tensor_used(n + 1, 0))
            for i, name in enumerate(("accA", "accB")):
                V.wait_ge(bank_ready(name), turn(name))
                y = Y[:, tt, i * 512:(i + 1) * 512]
                V.tensor_tensor(y, y, result(name)[:, :], ALU.add).then_inc(bank_free(name), 1)
            for name in ("accA", "accB"):
                V.wait_ge(bank_free(name), turn(name))

        def weigh(block, st, n):
            l, tt, _ = passes[n]

            SUM = sb("SUM", [P, PH], F32, st)
            g3 = GATE[:, tt, :].rearrange("p (h k) -> p h k", h=PH)

            @block.scalar
            def _(act):
                A.activation(GATE[:, tt, :], GATE[:, tt, :], ACT.Exp).then_inc(*tick("gate_exp"))
                A.wait_ge(*nth("dots_done", 1))
                A.activation(ACTV[:, tt, :], ACTV[:, tt, :], ACT.Gelu).then_inc(*tick("gelu_done"))
                A.activation(Y[:, tt, :], X[:, tt, :], ACT.Copy, scale=ALPHA).then_inc(*tick("gelu_done"))
                A.wait_ge(*now("gelu_done"))

            @block.vector
            def _(dve):
                V.wait_ge(*nth("gate_exp", 1))
                V.tensor_reduce(SUM[:, :], g3, AX.X, ALU.add).then_inc(*tick("dve_step"))
                V.wait_ge(*now("dve_step"))
                V.reciprocal(SUM[:, :], SUM[:, :]).then_inc(*tick("dve_step"))
                V.wait_ge(*now("dve_step"))
                V.tensor_tensor(g3, g3, SUM[:, :].unsqueeze(2).broadcast_to([P, PH, TOPK]), ALU.mult).then_inc(*tick("dve_step"))
                V.wait_ge(*now("dve_step"))
                V.memset(ODD[:, :], 0.0).then_inc(*tick("dve_step"))
                gather_rest()
                V.memset(stat[:, 62:63], 0.0).then_inc(*tick("dots_done"))
                V.wait_ge(*now("dots_done"))
                V.wait_ge(*nth("gelu_done", 2))
                V.tensor_tensor(GATE[:, tt, :], GATE[:, tt, :], ACTV[:, tt, :], ALU.mult).then_inc(*tick("dve_step"))
                V.wait_ge(*now("dve_step"))
                gather_begin(n + 1)

        def peer_done(block, st, n, more):
            l, tt, _ = passes[n]
            block.scalar(lambda act: act_root("p_ln_var", 1, "p_ln_root", stat[:, 8 + tt:9 + tt], stat[:, 48 + tt:49 + tt]))

            @block.vector
            def _(dve):
                if n == 1:
                    later["pairs"]()
                if not shared[n]:
                    gather_rest()
                V.tensor_tensor(Y[:, tt, :], Y[:, tt, :], ODD[:, :], ALU.add).then_inc(*tick("dve_step"))
                V.wait_ge(*now("dve_step"))
                rows_here(1, 2 if tt == 0 else 0)
                dve_layer_norm(Y, X, rows[1][:, 0, :], rows[1][:, 1, :], EPS1, "p_ln", "x_ready", tiles=(tt,), root=True)
                dve.sem_inc(S("tile_done"), 1)
                if more:
                    gather_begin(n + 1)

        later = {}

        def peer_route(block, st, l, tiles, tag):
            KEYT = sb("KEYT", [P, 2 * PH, NK], F32, st)
            QP = {tt: sb(f"QP{tt}", [P, 2 * PH, P], F32, st) for tt in tiles}
            SC = sb("SC", [P, 2 * PH, NK], F32, st)
            CAND = SC[:, :, :].rearrange("p a b -> p (a b)")[:, 0:PH * NCAND].rearrange("p (h n) -> p h n", h=PH)
            TV = sb("TV", [P, 2 * PH, TOPK], F32, st)
            TI = sb("TI", [P, 2 * PH, TOPK], U32, st)
            TF = sb("TF", [P, 2 * PH, TOPK], F32, st)
            BV = sb("BV", [P, PH, TOPK], F32, st)
            BI = sb("BI", [P, PH, TOPK], U32, st)
            HALF = sb("HALF", [P, 4, PICKS // 2], U32, st)
            HALFF = sb("HALFF", [P, 4, PICKS // 2], F32, st)
            EX = sb("EX", [P, 2, PICKS // 2], F32, st)
            DG = [sb(f"DG{i}", [P, P], F32, st) for i in range(PE_SLOTS)]
            beside = 2 * tiles[0] + 3
            per = 4 // len(tiles)
            t = slice(tiles[0] * P, (tiles[-1] + 1) * P)

            def best8(source, vals, idxs, at, ks):
                for k in ks:
                    V.max(vals[:, k, at:at + 8], source(k)).then_inc(*tick("dve_step"))
                V.wait_ge(*now("dve_step"))
                for k in ks:
                    V.max_index(idxs[:, k, at:at + 8], vals[:, k, at:at + 8], source(k)).then_inc(*tick("dve_step"))
                V.wait_ge(*now("dve_step"))

            def best_pairs(tt, half):
                some = 2 if (l, tt) == (0, 1) else 1
                HH = PH // 2
                NP = HH * TOPK
                hs, ks = slice(half * HH, (half + 1) * HH), slice(half * NP, (half + 1) * NP)
                tv = TV[:, :, :].rearrange("p (h c) k -> p h c k", c=2)
                for c, i0, i1, nj in ((slice(0, 64), 0, 4, TOPK), (slice(64, NCAND), 4, TOPK, 4)):
                    V.tensor_tensor(CAND[:, hs, c].rearrange("p h (i j) -> p h i j", j=nj),
                                    tv[:, hs, 0, i0:i1].unsqueeze(3).broadcast_to([P, HH, i1 - i0, nj]),
                                    tv[:, hs, 1, 0:nj].unsqueeze(2).broadcast_to([P, HH, i1 - i0, nj]), ALU.add).then_inc(*tick("dve_step"))
                V.wait_ge(*now("dve_step"))
                sums = lambda h: CAND[:, h, :]
                best8(sums, BV, BI, 0, range(hs.start, hs.stop))
                gather_some(some)
                for h in range(hs.start, hs.stop):
                    V.match_replace(sums(h), BV[:, h, 0:8], sums(h), FLOOR).then_inc(*tick("dve_step"))
                V.wait_ge(*now("dve_step"))
                gather_some(some)
                best8(sums, BV, BI, 8, range(hs.start, hs.stop))
                g3 = GATE[:, tt, ks].rearrange("p (h k) -> p h k", h=HH)
                V.tensor_tensor(g3, BV[:, hs, :], BV[:, hs, 0:1].broadcast_to([P, HH, TOPK]), ALU.subtract).then_inc(*tick("dve_step"))
                V.wait_ge(*now("dve_step"))
                bi = BI[:, hs, :].rearrange("p h k -> p (h k)")
                V.tensor_scalar(HALF[:, 0, :], bi, 4, None, ALU.logical_shift_right).then_inc(*tick("dve_step"))
                V.tensor_scalar(HALF[:, 1, :], bi, TOPK - 1, None, ALU.bitwise_and).then_inc(*tick("dve_step"))
                V.tensor_scalar(HALF[:, 2, :], bi, 2, None, ALU.logical_shift_right).then_inc(*tick("dve_step"))
                V.tensor_scalar(HALF[:, 3, :], bi, 3, None, ALU.bitwise_and).then_inc(*tick("dve_step"))
                V.wait_ge(*now("dve_step"))
                V.tensor_copy(HALFF[:, :, :], HALF[:, :, :]).then_inc(*tick("dve_step"))
                V.wait_ge(*now("dve_step"))
                first, second, quarter, rest = (HALFF[:, x, :] for x in range(4))
                V.scalar_tensor_tensor(first, quarter, -12.0, first, ALU.add, ALU.max).then_inc(*tick("dve_step"))
                V.tensor_tensor(second, second, rest, ALU.subtract).then_inc(*tick("dve_step"))
                V.wait_ge(*now("dve_step"))
                V.scalar_tensor_tensor(second, first, 4.0, second, ALU.is_lt, ALU.mult).then_inc(*tick("dve_step"))
                V.wait_ge(*now("dve_step"))
                V.tensor_tensor(second, second, rest, ALU.add).then_inc(*tick("dve_step"))
                V.wait_ge(*now("dve_step"))
                tf = TF[:, :, :].rearrange("p (h c) k -> p h c k", c=2)
                hot = QP[tt][:, :, :].rearrange("p a b -> p (a b)").rearrange("p (k j) -> p k j", j=TOPK)[:, 0:NP, :]
                at16, _ = cwhere["i16"]
                for c in range(2):
                    V.tensor_tensor(hot, HALFF[:, c, :].unsqueeze(2).broadcast_to([P, NP, TOPK]),
                                    CN[:, at16:at16 + TOPK].unsqueeze(1).broadcast_to([P, NP, TOPK]), ALU.is_equal).then_inc(*tick("dve_step"))
                    V.wait_ge(*now("dve_step"))
                    if c == 0 or some == 2:
                        gather_some(some)
                    hot4 = hot.rearrange("p (h k) j -> p h k j", h=HH)
                    V.tensor_tensor(hot4, hot4, tf[:, hs, c, :].unsqueeze(2).broadcast_to([P, HH, TOPK, TOPK]), ALU.mult).then_inc(*tick("dve_step"))
                    V.wait_ge(*now("dve_step"))
                    V.tensor_reduce(EX[:, c, :], hot, AX.X, ALU.add).then_inc(*tick("dve_step"))
                    V.wait_ge(*now("dve_step"))
                V.scalar_tensor_tensor(EX[:, 0, :], EX[:, 0, :], float(NK), EX[:, 1, :], ALU.mult, ALU.add).then_inc(*tick("dve_step"))
                V.wait_ge(*now("dve_step"))
                V.tensor_scalar(IDX[:, tt, ks], EX[:, 0, :], float(l * NEXP), None, ALU.add).then_inc(picks_ready, 1)
                V.wait_ge(picks_ready, 2 * (TT * l + tt) + half + 1)

            if l == 0:
                later["pairs"] = lambda: (best_pairs(1, 0), best_pairs(1, 1))

            @block.tensor
            def _(pe):
                pe.wait_ge(*landed(f"keys{tag}"))
                w = slot_of(f"keys{tag}")
                for g in range(4):
                    b = job(f"kt{g}")
                    if turn(f"kt{g}") > 1:
                        PE.wait_ge(bank_free(f"kt{g}"), turn(f"kt{g}") - 1)
                    for j in range(4):
                        last = tr(b[:, j * P:(j + 1) * P], w[:, 4 * g + j, :], ident)
                    last.then_inc(bank_ready(f"kt{g}"), 1)
                weight_read(f"keys{tag}", "kt3")
                pe_turn(PE, "xt", X, None, tiles=tiles)
                for name in [f"xt{tt}{g}" for tt in tiles for g in range(2)]:
                    pe.wait_ge(bank_free(name), turn(name))

                def scores(tt, g):
                    b = job(f"s{tt}{g}")
                    if turn(f"s{tt}{g}") > 1:
                        PE.wait_ge(bank_free(f"s{tt}{g}"), turn(f"s{tt}{g}") - 1)
                    for j in range(4):
                        last = mul(b[:, j * P:(j + 1) * P], QP[tt][:, 4 * g + j, :], KEYT[:, 4 * g + j, :], True, True)
                    last.then_inc(bank_ready(f"s{tt}{g}"), 1)

                for e in range(5):
                    if e < 4:
                        pe.wait_ge(*landed(f"peer_q{tag}_{e}"))
                        w = slot_of(f"peer_q{tag}_{e}")
                        for i in range(len(tiles)):
                            pe_colpair(PE, w, f"q{e}{i}", XT, [P * (per * i + s) for s in range(per)], t=t)
                        weight_read(f"peer_q{tag}_{e}", f"q{e}{len(tiles) - 1}")
                    if e > 0:
                        g = e - 1
                        pe.wait_ge(bank_free(f"kt{g}"), turn(f"kt{g}"))
                        for i in range(len(tiles)):
                            pe.wait_ge(bank_free(f"q{g}{i}"), turn(f"q{g}{i}"))
                        scores(tiles[0], g)
                for tt in tiles[1:]:
                    for g in range(4):
                        scores(tt, g)
                if l == 1:
                    pe_share(beside, DG)

            @block.scalar
            def _(act):
                for g in range(4):
                    A.wait_ge(bank_ready(f"kt{g}"), turn(f"kt{g}"))
                    b = result(f"kt{g}")
                    copy(A, KEYT[:, 4 * g:4 * g + 4, :], b[:, :].rearrange("p (k n) -> p k n", k=4)).then_inc(bank_free(f"kt{g}"), 1)
                take_turn(A, "xt", XT, [(tt, g) for tt in tiles for g in range(2)])
                for e in range(4):
                    for i in range(len(tiles)):
                        A.wait_ge(bank_ready(f"q{e}{i}"), turn(f"q{e}{i}"))
                        b = result(f"q{e}{i}")[:, :].rearrange("p (k t) -> p k t", k=per)
                        c = slice(4 * e + per * i, 4 * e + per * i + per)
                        for x, tt in enumerate(tiles[:-1]):
                            copy(A, QP[tt][:, c, :], b[:, :, x * P:(x + 1) * P]).then_inc(*tick("act_step"))
                        copy(A, QP[tiles[-1]][:, c, :], b[:, :, (len(tiles) - 1) * P:]).then_inc(bank_free(f"q{e}{i}"), 1)
                if l == 1:
                    act_share(beside, DG)

            @block.vector
            def _(dve):
                if tiles[0] == 0 and l == 0:
                    dve.sem_inc(row_used, SLOTS)
                gather_some(3)
                for tt in tiles:
                    for g in range(4):
                        name = f"s{tt}{g}"
                        gather_some(1)
                        V.wait_ge(bank_ready(name), turn(name))
                        score = lambda k: result(name)[:, (k - 4 * g) * P:(k - 4 * g + 1) * P]
                        lists = range(4 * g, 4 * g + 4)
                        best8(score, TV, TI, 0, lists)
                        for k in lists[:-1]:
                            V.match_replace(SC[:, k, :], TV[:, k, 0:8], score(k), FLOOR).then_inc(*tick("dve_step"))
                        k = lists[-1]
                        V.match_replace(SC[:, k, :], TV[:, k, 0:8], score(k), FLOOR).then_inc(bank_free(name), 1)
                        V.wait_ge(bank_free(name), turn(name))
                        gather_some(1)
                        best8(lambda k: SC[:, k, :], TV, TI, 8, lists)
                    V.tensor_copy(TF[:, :, :], TI[:, :, :]).then_inc(*tick("dve_step"))
                    V.wait_ge(*now("dve_step"))
                    if (l, tt) != (0, 1):
                        best_pairs(tt, 0)
                        best_pairs(tt, 1)
                    if l == 0 and tt == 0:
                        gather_begin(0)
                if l == 1:
                    dve_share(beside)

        def embed(block, st, src, gate_key, proj_key, which, before=None, tiles=BOTH):
            both = len(tiles) == TT
            turns = ([(tt, 0) for tt in tiles], [(tt, 1) for tt in tiles]) if both else ([(tt, g) for tt in tiles for g in range(2)], [])
            SG = sb("SG", [P, TT, D], F32, st)
            PW = sb("PW", [P, TT, D], F32, st)
            PTT = sb("PTT", [P, 2, T], F32, st)

            @block.tensor
            def _(pe):
                params_here(pe)
                for tt in tiles:
                    b = job(f"pt{tt}")
                    if turn(f"pt{tt}") > 1:
                        PE.wait_ge(bank_free(f"pt{tt}"), turn(f"pt{tt}") - 1)
                    for j in range(2):
                        last = tr(b[:, j * P:(j + 1) * P], PIN[:, which, tt, j * P:(j + 1) * P], ident)
                    last.then_inc(bank_ready(f"pt{tt}"), 1)
                for tt in tiles:
                    pe.wait_ge(bank_free(f"pt{tt}"), turn(f"pt{tt}"))
                pe.wait_ge(*landed(proj_key))
                w = slot_of(proj_key)
                for cb in range(2):
                    for tt in tiles:
                        pe_rows(PE, w, f"p{cb}{tt}", PTT, tt, cb * 512, 512)
                weight_read(proj_key, f"p1{tiles[-1]}")
                pe_turn(PE, "xt", src, "h_ready" if before else None, tiles=tiles)
                for name in [f"xt{tt}{g}" for tt in tiles for g in range(2)]:
                    pe.wait_ge(bank_free(name), turn(name))
                for cb in range(2):
                    pe.wait_ge(*landed(f"{gate_key}{cb}"))
                    w = slot_of(f"{gate_key}{cb}")
                    for tt in tiles:
                        pe_rows(PE, w, f"g{cb}{tt}", XT, tt, 0, 512)
                    weight_read(f"{gate_key}{cb}", f"g{cb}{tiles[-1]}")

            @block.scalar
            def _(act):
                for tt in tiles:
                    A.wait_ge(bank_ready(f"pt{tt}"), turn(f"pt{tt}"))
                    b = result(f"pt{tt}")
                    copy(A, PTT[:, :, tt * P:(tt + 1) * P], b[:, 0:T].rearrange("p (k t) -> p k t", k=2)).then_inc(bank_free(f"pt{tt}"), 1)
                if before:
                    before[0]()
                for cb in range(2):
                    for tt in tiles:
                        A.wait_ge(bank_ready(f"p{cb}{tt}"), turn(f"p{cb}{tt}"))
                        copy(A, PW[:, tt, cb * 512:cb * 512 + 512], result(f"p{cb}{tt}")[:, :]).then_inc(bank_free(f"p{cb}{tt}"), 1)
                take_turn(A, "xt", XT, turns[0])
                for cb in range(2):
                    for tt in tiles:
                        A.wait_ge(bank_ready(f"g{cb}{tt}"), turn(f"g{cb}{tt}"))
                        b = result(f"g{cb}{tt}")
                        A.activation(SG[:, tt, cb * 512:cb * 512 + 512], b[:, :], ACT.Sigmoid).then_inc(bank_free(f"g{cb}{tt}"), 1)

            @block.vector
            def _(dve):
                if before:
                    before[1]()
                gather_some(2)
                take_turn(V, "xt", XT, turns[1])
                gather_some(2)
                for cb in range(2):
                    for tt in tiles:
                        s = slice(cb * 512, cb * 512 + 512)
                        V.wait_ge(bank_free(f"g{cb}{tt}"), turn(f"g{cb}{tt}"))
                        V.wait_ge(bank_free(f"p{cb}{tt}"), turn(f"p{cb}{tt}"))
                        V.tensor_tensor(PW[:, tt, s], PW[:, tt, s], SG[:, tt, s], ALU.mult).then_inc(*tick("dve_step"))
                V.wait_ge(*now("dve_step"))
                for tt in tiles:
                    V.tensor_tensor(X[:, tt, :], X[:, tt, :], PW[:, tt, :], ALU.add).then_inc(*tick("x_ready"))
                    V.wait_ge(*now("x_ready"))

        def mla(block, st, tt, KNT, VM, KRT):
            CK = sb("CK", [P, KVR + ROPE], F32, st)
            CQ = sb("CQ", [P, QR], F32, st)
            MS = sb("MS", [P, 4], F32, st)
            CKT = sb("CKT", [P, KVR // P, P], F32, st)
            CQT = sb("CQT", [P, QR // P, P], F32, st)
            QNT = sb("QNT", [P, AH, P], F32, st)
            QRR = sb("QRR", [P, AH, ROPE], F32, st)
            QRT = sb("QRT", [ROPE, AH, P], F32, st)
            KRR = sb("KRR", [P, 1, ROPE], F32, st)
            HR = ROPE // 2
            ANG = sb("ANG", [P, 2, HR], F32, st)
            TURN = sb("TURN", [P, HR], F32, st)
            TRIG = sb("TRIG", [P, 2, HR], F32, st)
            RT = sb("RT", [P, 4, AH, HR], F32, st)
            n = (tt + 1) * P
            PR = [sb(f"PR{i}", [P, n], F32, st) for i in range(2)]
            PRT = [sb(f"PRT{i}", [P, n], F32, st) for i in range(2)]
            MX = sb("MX", [P, AH], F32, st)
            SM = sb("SM", [P, AH], F32, st)
            RS = sb("RS", [P, AH], F32, st)
            POSF = sb("POSF", [P, 1], F32, st)
            t = slice(tt * P, (tt + 1) * P)
            JUNK = Y[:, tt, :]
            scale = (NOPE + ROPE) ** -0.5

            @block.tensor
            def _(pe):
                pe_turn(PE, "xt", X, None, tiles=(tt,))
                for g in range(2):
                    pe.wait_ge(bank_free(f"xt{tt}{g}"), turn(f"xt{tt}{g}"))
                for key, name, c in ((f"kv_down{tt}", "ck", KVR + ROPE), (f"dq{tt}", "cq", QR)):
                    pe.wait_ge(*landed(key))
                    w = slot_of(key)
                    pe_rows(PE, w, name, XT, tt, 0, c)
                    weight_read(key, name)
                pe.wait_ge(*nth("latents_ready", 1))
                b = job("ckt")
                if turn("ckt") > 1:
                    PE.wait_ge(bank_free("ckt"), turn("ckt") - 1)
                for j in range(KVR // P):
                    tr(b[:, j * P:(j + 1) * P], CK[:, j * P:(j + 1) * P], ident)
                tr(b[0:ROPE, KVR:KVR + P], KRR[:, 0, :], ident).then_inc(bank_ready("ckt"), 1)
                b = job("cqt")
                if turn("cqt") > 1:
                    PE.wait_ge(bank_free("cqt"), turn("cqt") - 1)
                for j in range(QR // P):
                    last = tr(b[:, j * P:(j + 1) * P], CQ[:, j * P:(j + 1) * P], ident)
                last.then_inc(bank_ready("cqt"), 1)
                pe.wait_ge(bank_free("ckt"), turn("ckt"))
                pe.wait_ge(bank_free("cqt"), turn("cqt"))
                pe.wait_ge(*landed(f"kv_up{tt}"))
                w = slot_of(f"kv_up{tt}")
                one = slice(0, P)
                for i in range(AH // 4):
                    pe_colpair(PE, w, f"kn{i}", CKT, [256 * (4 * i + j) for j in range(4)], t=one)
                wh = w.rearrange("p k (h c) -> p k h c", h=AH)
                for hb in range(2):
                    b = job(f"vv{hb}")
                    if turn(f"vv{hb}") > 1:
                        PE.wait_ge(bank_free(f"vv{hb}"), turn(f"vv{hb}") - 1)
                    for k in range(KVR // P):
                        last = mul(b[:, :], CKT[:, k, :], wh[:, k, 4 * hb:4 * hb + 4, NOPE:NOPE + AV], k == 0, k == 1)
                    last.then_inc(bank_ready(f"vv{hb}"), 1)
                weight_read(f"kv_up{tt}", "vv1")
                for e in range(2):
                    pe.wait_ge(*landed(f"uq{tt}{e}"))
                    w = slot_of(f"uq{tt}{e}")
                    wh = w.rearrange("p k (h c) -> p k h c", h=4)
                    b = job(f"qr{e}")
                    if turn(f"qr{e}") > 1:
                        PE.wait_ge(bank_free(f"qr{e}"), turn(f"qr{e}") - 1)
                    for k in range(QR // P):
                        last = mul(b[:, 0:4 * ROPE], CQT[:, k, :], wh[:, k, :, NOPE:NOPE + ROPE], k == 0, k == 2)
                    last.then_inc(bank_ready(f"qr{e}"), 1)
                    pe_colpair(PE, w, f"qn{e}", CQT, [192 * j for j in range(4)], t=one)
                    weight_read(f"uq{tt}{e}", f"qn{e}")
                for e in range(2):
                    pe.wait_ge(*nth("q_rotated", e + 1))
                    b = job(f"qrt{e}")
                    if turn(f"qrt{e}") > 1:
                        PE.wait_ge(bank_free(f"qrt{e}"), turn(f"qrt{e}") - 1)
                    for j in range(4):
                        last = tr(b[0:ROPE, j * P:(j + 1) * P], QRR[:, 4 * e + j, :], ident)
                    last.then_inc(bank_ready(f"qrt{e}"), 1)
                for name in ["kn0", "kn1", "vv0", "vv1", "qn0", "qn1", "qrt0", "qrt1"]:
                    pe.wait_ge(bank_free(name), turn(name))
                for i in range(AH + 2):
                    if i < AH:
                        h = i
                        b = job(f"s{h}")
                        if turn(f"s{h}") > 1:
                            PE.wait_ge(bank_free(f"s{h}"), turn(f"s{h}") - 1)
                        mul(b[:, 0:n], QNT[:, h, :], KNT[:, h, 0:n], True, False)
                        mul(b[:, 0:n], QRT[:, h, :], KRT[:, 0:n], False, False)
                        mul(b[:, n - P:n], ident, con("mask_q"), False, True).then_inc(bank_ready(f"s{h}"), 1)
                    if 1 <= i <= AH:
                        h = i - 1
                        pe.wait_ge(bank_free(f"s{h}"), turn(f"s{h}"))
                        b = job(f"t{h}")
                        if turn(f"t{h}") > 1:
                            PE.wait_ge(bank_free(f"t{h}"), turn(f"t{h}") - 1)
                        for j in range(tt + 1):
                            last = tr(b[:, j * P:(j + 1) * P], PR[h % 2][:, j * P:(j + 1) * P], ident)
                        last.then_inc(bank_ready(f"t{h}"), 1)
                    if i >= 2:
                        h = i - 2
                        pe.wait_ge(bank_free(f"t{h}"), turn(f"t{h}"))
                        b = job(f"o{h}")
                        if turn(f"o{h}") > 1:
                            PE.wait_ge(bank_free(f"o{h}"), turn(f"o{h}") - 1)
                        v = slice(h * AV, (h + 1) * AV)
                        for j in range(tt + 1):
                            last = mul(b[:, 0:AV], PRT[h % 2][:, j * P:(j + 1) * P], VM[:, j, v], j == 0, j == tt)
                        last.then_inc(bank_ready(f"o{h}"), 1)
                pe.wait_ge(bank_free(f"o{AH - 1}"), turn(f"o{AH - 1}"))
                pe_turn(PE, "yt", Y, None, tiles=(tt,))
                for g in range(2):
                    pe.wait_ge(bank_free(f"yt{tt}{g}"), turn(f"yt{tt}{g}"))
                for cb in range(2):
                    pe.wait_ge(*landed(f"b_out{tt}{cb}"))
                    w = slot_of(f"b_out{tt}{cb}")
                    pe_rows(PE, w, f"m{cb}{tt}", XT, tt, 0, 512)
                    weight_read(f"b_out{tt}{cb}", f"m{cb}{tt}")

            @block.scalar
            def _(act):
                take_turn(A, "xt", XT, [(tt, 0), (tt, 1)])
                A.wait_ge(*nth("angles", 1))
                A.activation(TRIG[:, :, :], ANG[:, :, :], ACT.Sin).then_inc(*tick("trig"))
                A.wait_ge(*now("trig"))
                for i, (name, c, dst) in enumerate((("ck", KVR + ROPE, CK), ("cq", QR, CQ))):
                    A.wait_ge(bank_ready(name), turn(name))
                    copy(A, dst[:, :], result(name)[:, 0:c]).then_inc(bank_free(name), 1)
                    A.wait_ge(bank_free(name), turn(name))
                for i, (src, c) in enumerate(((CK, KVR), (CQ, QR))):
                    A.activation(JUNK[:, 0:c], src[:, 0:c], ACT.Square, accum_out=MS[:, i:i + 1]).then_inc(*tick("latent_sq"))
                    A.wait_ge(*now("latent_sq"))
                act_root("latent_var", 1, "latent_root", MS[:, 0:2], MS[:, 2:4])
                A.wait_ge(bank_ready("ckt"), turn("ckt"))
                b = result("ckt")
                copy(A, CKT[:, :, :], b[:, 0:KVR].rearrange("p (k t) -> p k t", k=2)).then_inc(*tick("act_step"))
                copy(A, KRT[:, t], b[0:ROPE, KVR:KVR + P]).then_inc(bank_free("ckt"), 1)
                A.wait_ge(bank_ready("cqt"), turn("cqt"))
                copy(A, CQT[:, :, :], result("cqt")[:, 0:QR].rearrange("p (k t) -> p k t", k=3)).then_inc(bank_free("cqt"), 1)
                quad = lambda b: b[:, :].rearrange("p (k t) -> p k t", k=4)
                for i in range(2):
                    A.wait_ge(bank_ready(f"kn{i}"), turn(f"kn{i}"))
                    copy(A, KNT[:, 4 * i:4 * i + 4, t], quad(result(f"kn{i}"))).then_inc(bank_free(f"kn{i}"), 1)
                for hb in range(2):
                    A.wait_ge(bank_ready(f"vv{hb}"), turn(f"vv{hb}"))
                    copy(A, VM[:, tt, hb * 512:hb * 512 + 512], result(f"vv{hb}")[:, :]).then_inc(bank_free(f"vv{hb}"), 1)
                for e in range(2):
                    A.wait_ge(bank_ready(f"qn{e}"), turn(f"qn{e}"))
                    copy(A, QNT[:, 4 * e:4 * e + 4, :], quad(result(f"qn{e}"))).then_inc(bank_free(f"qn{e}"), 1)
                for e in range(2):
                    A.wait_ge(bank_ready(f"qrt{e}"), turn(f"qrt{e}"))
                    copy(A, QRT[:, 4 * e:4 * e + 4, :], quad(result(f"qrt{e}"))[0:ROPE]).then_inc(bank_free(f"qrt{e}"), 1)
                for h in range(AH):
                    A.wait_ge(bank_ready(f"s{h}"), turn(f"s{h}"))
                    b = result(f"s{h}")
                    A.wait_ge(*nth("max_ready", h + 1))
                    if h >= 2:
                        A.wait_ge(bank_ready(f"t{h - 2}"), turn(f"t{h - 2}"))
                    A.activation(PR[h % 2][:, :], b[:, 0:n], ACT.Exp, bias=MX[:, h:h + 1], scale=scale, accum_out=SM[:, h:h + 1]).then_inc(bank_free(f"s{h}"), 1)
                    if h >= 1:
                        g = h - 1
                        A.wait_ge(bank_ready(f"t{g}"), turn(f"t{g}"))
                        if g >= 2:
                            A.wait_ge(bank_ready(f"o{g - 2}"), turn(f"o{g - 2}"))
                        copy(A, PRT[g % 2][:, :], result(f"t{g}")[:, 0:n]).then_inc(bank_free(f"t{g}"), 1)
                g = AH - 1
                A.wait_ge(bank_ready(f"t{g}"), turn(f"t{g}"))
                A.wait_ge(bank_ready(f"o{g - 2}"), turn(f"o{g - 2}"))
                copy(A, PRT[g % 2][:, :], result(f"t{g}")[:, 0:n]).then_inc(bank_free(f"t{g}"), 1)
                take_turn(A, "yt", XT, [(tt, 0), (tt, 1)])
                act_root("b_ln_var", 1, "b_ln_root", stat[:, 8 + tt:9 + tt], stat[:, 48 + tt:49 + tt])

            @block.vector
            def _(dve):
                params_here(dve)
                V.tensor_copy(POSF[:, :], POS[:, tt:tt + 1]).then_inc(*tick("dve_step"))
                V.wait_ge(*now("dve_step"))
                V.tensor_scalar(ANG[:, 0, :], con("freq"), POSF[:, 0:1], None, ALU.mult).then_inc(*tick("dve_step"))
                V.wait_ge(*now("dve_step"))
                magic, tau = 1.5 * 2.0 ** 23, 2.0 * math.pi
                hi = 6.28125
                mid = math.floor((tau - hi) * 2.0 ** 20) / 2.0 ** 20
                lo = tau - hi - mid
                V.tensor_scalar(TURN[:, :], ANG[:, 0, :], 1.0 / tau, magic, ALU.mult, ALU.add).then_inc(*tick("dve_step"))
                V.wait_ge(*now("dve_step"))
                V.tensor_scalar(TURN[:, :], TURN[:, :], magic, None, ALU.subtract).then_inc(*tick("dve_step"))
                V.wait_ge(*now("dve_step"))
                for part in (hi, mid, lo):
                    V.scalar_tensor_tensor(ANG[:, 0, :], TURN[:, :], -part, ANG[:, 0, :], ALU.mult, ALU.add).then_inc(*tick("dve_step"))
                    V.wait_ge(*now("dve_step"))
                V.tensor_scalar(ANG[:, 1, :], ANG[:, 0, :], 0.5 * math.pi, None, ALU.add).then_inc(*tick("dve_step"))
                V.wait_ge(*now("dve_step"))
                V.tensor_scalar(TURN[:, :], ANG[:, 1, :], math.pi, -tau, ALU.is_gt, ALU.mult).then_inc(*tick("dve_step"))
                V.wait_ge(*now("dve_step"))
                V.tensor_tensor(ANG[:, 1, :], ANG[:, 1, :], TURN[:, :], ALU.add).then_inc(*tick("dve_step"))
                V.wait_ge(*now("dve_step"))
                V.tensor_scalar(ANG[:, :, :], ANG[:, :, :], 3.1415925, -3.1415925, ALU.min, ALU.max).then_inc(*tick("angles"))
                V.wait_ge(*now("angles"))
                gather_some(1)

                def rotate_products(src):
                    k = src.shape[1]
                    sin, cos = (TRIG[:, f, :].unsqueeze(1).broadcast_to([P, k, HR]) for f in range(2))
                    x1, x2 = src[:, :, 0:HR], src[:, :, HR:ROPE]
                    V.tensor_tensor(RT[:, 0, 0:k], x1, cos, ALU.mult).then_inc(*tick("dve_step"))
                    V.tensor_tensor(RT[:, 1, 0:k], x2, sin, ALU.mult).then_inc(*tick("dve_step"))
                    V.tensor_tensor(RT[:, 2, 0:k], x1, sin, ALU.mult).then_inc(*tick("dve_step"))
                    return V.tensor_tensor(RT[:, 3, 0:k], x2, cos, ALU.mult)

                def rotate_sums(dst):
                    k = dst.shape[1]
                    V.tensor_tensor(dst[:, :, 0:HR], RT[:, 0, 0:k], RT[:, 1, 0:k], ALU.subtract).then_inc(*tick("dve_step"))
                    V.wait_ge(*now("dve_step"))
                    return V.tensor_tensor(dst[:, :, HR:ROPE], RT[:, 2, 0:k], RT[:, 3, 0:k], ALU.add)

                V.wait_ge(*nth("trig", 1))
                V.wait_ge(bank_free("ck"), turn("ck"))
                rotate_products(CK[:, KVR:KVR + ROPE].unsqueeze(1)).then_inc(*tick("dve_step"))
                V.wait_ge(*now("dve_step"))
                rotate_sums(KRR[:, :, :]).then_inc(*tick("dve_step"))
                V.wait_ge(*now("dve_step"))
                V.wait_ge(*nth("latent_sq", 2))
                V.tensor_scalar(MS[:, 0:1], MS[:, 0:1], 1.0 / KVR, EPS1, ALU.mult, ALU.add).then_inc(*tick("dve_step"))
                V.tensor_scalar(MS[:, 1:2], MS[:, 1:2], 1.0 / QR, EPS1, ALU.mult, ALU.add).then_inc(*tick("latent_var"))
                V.wait_ge(*now("dve_step"))
                V.wait_ge(*now("latent_var"))
                gather_some(1)
                V.wait_ge(*nth("latent_root", 1))
                dve_rstd(MS[:, 0:2], MS[:, 2:4])
                V.scalar_tensor_tensor(CK[:, 0:KVR], CK[:, 0:KVR], MS[:, 0:1], small("kv_norm_g"), ALU.mult, ALU.mult).then_inc(*tick("dve_step"))
                V.wait_ge(*now("dve_step"))
                V.scalar_tensor_tensor(CQ[:, :], CQ[:, :], MS[:, 1:2], small("b_q_norm_g"), ALU.mult, ALU.mult).then_inc(*tick("latents_ready"))
                V.wait_ge(*now("latents_ready"))
                gather_some(1)
                for e in range(2):
                    V.wait_ge(bank_ready(f"qr{e}"), turn(f"qr{e}"))
                    src = result(f"qr{e}")[:, 0:4 * ROPE].rearrange("p (h r) -> p h r", h=4)
                    rotate_products(src).then_inc(bank_free(f"qr{e}"), 1)
                    V.wait_ge(bank_free(f"qr{e}"), turn(f"qr{e}"))
                    rotate_sums(QRR[:, 4 * e:4 * e + 4, :]).then_inc(*tick("q_rotated"))
                    V.wait_ge(*now("q_rotated"))
                for i in range(AH + 2):
                    if i % 2 == 0:
                        gather_some(1)
                    if i < AH:
                        h = i
                        V.wait_ge(bank_ready(f"s{h}"), turn(f"s{h}"))
                        V.tensor_reduce(MX[:, h:h + 1], result(f"s{h}")[:, 0:n], AX.X, ALU.max).then_inc(*tick("dve_step"))
                        V.wait_ge(*now("dve_step"))
                        V.tensor_scalar(MX[:, h:h + 1], MX[:, h:h + 1], -scale, None, ALU.mult).then_inc(*tick("max_ready"))
                        V.wait_ge(*now("max_ready"))
                    if i >= 2:
                        h = i - 2
                        V.wait_ge(bank_ready(f"o{h}"), turn(f"o{h}"))
                        V.wait_ge(bank_free(f"s{h}"), turn(f"s{h}"))
                        V.reciprocal(RS[:, h:h + 1], SM[:, h:h + 1]).then_inc(*tick("dve_step"))
                        V.wait_ge(*now("dve_step"))
                        V.tensor_scalar(Y[:, tt, h * AV:(h + 1) * AV], result(f"o{h}")[:, 0:AV], RS[:, h:h + 1], None, ALU.mult).then_inc(bank_free(f"o{h}"), 1)
                V.wait_ge(bank_free(f"o{AH - 1}"), turn(f"o{AH - 1}"))
                gather_some(1)
                dve_residual("m", ALPHA, tiles=(tt,))
                rows_here(0, 3 if tt == 0 else 0)
                dve_layer_norm(Y, X, rows[0][:, 0, :], rows[0][:, 1, :], EPS1, "b_ln", "x_ready", tiles=(tt,), root=True)

        def dve_rms(key, g):
            dve_mean_square(key, D, EPS2)
            for tt in range(TT):
                V.scalar_tensor_tensor(Y[:, tt, :], X[:, tt, :], stat[:, 12 + tt:13 + tt], g, ALU.mult, ALU.mult).then_inc(*tick("h_ready"))
                V.wait_ge(*now("h_ready"))

        def pool_rms(key):
            pool_power(key + "_var", 1, key + "_rstd", stat[:, 12:14])

        def nsa():
            with ExitStack() as st:
                QT = sb("QT2", [P, NH // 2, T], F32, st)
                KS = sb("KS", [P, 2, NKV, T], F32, st)
                VS = sb("VS", [P, 2, TT, NKV * HD], F32, st)
                NG = sb("NG", [P, TT, NH, 3], F32, st)
                KCMP = sb("KCMP", [P, NKV * NCMP], F32, st)
                VCMP = sb("VCMP", [NCMP, NKV, HD], F32, st)
                BIAS = ROWS[:, SLOTS // 2:, :].rearrange("p s d -> p (s d)")[:, 0:NH * STRIP].rearrange("p (h c) -> p h c", h=NH)
                phase(mixers_in, QT, KS, VS, NG, KCMP, VCMP, BIAS, with_pool=True)
                phase(nsa_attention, QT, KS, VS, NG, KCMP, VCMP, BIAS)
            phase(mixers_out)

        def mixers_in(block, st, QT, KS, VS, NG, KCMP, VCMP, BIAS):
            CT = sb("CT", [P, 2, NKV, T], F32, st)
            FLT = sb("FLT", [P, 2, CB // 2, NKV * NCMP], F32, st)
            HID = sb("HID", [P, 2, 2, NKV * NCMP], F32, st)
            POST = sb("POST", [P, 2, CB // 2], F32, st)
            BVEC = sb("BVEC", [NH, 384], F32, st)
            CWT = sb("CWT", [P, 2, 32], F32, st)
            SGC = sb("SGC", [P, 2, T], F32, st)
            CH = sb("CH", [P, 2, CW - 1 + T], F32, st)
            CACC = sb("CACC", [P, 2, T], F32, st)
            CV = sb("CV", [P, TT, CC], F32, st)
            CV2 = SGC
            GAT = sb("GAT", [GR, T], F32, st)
            LX = sb("LX", [P, TT, GK], F32, st)
            LA = sb("LA", [P, TT, GK], F32, st)
            E1 = sb("E1", [P, T], F32, st)
            E2 = sb("E2", [P, T], F32, st)
            E3 = sb("E3", [P, T], F32, st)
            BS = sb("BS", [P, T], F32, st)
            QG = sb("QG", [P, T], F32, st)
            KG = sb("KG", [P, T], F32, st)
            KDC = sb("KDC", [P, T], F32, st)
            KDT = sb("KDT", [P, TT, GK], F32, st)
            QBD = sb("QBD", [P, TT, GH, P], F32, st)
            AM = sb("AM", [P, TT, GH, P], F32, st)
            STB = sb("STB", [P, 3, GV], F32, st)
            GVS = sb("GVS", [P, TT, GV], F32, st)
            GRS = sb("GRS", [P, TT, GV], F32, st)
            GO = sb("GO", [P, TT, GV], F32, st)
            GSQ = CACC
            GST = sb("GST", [P, TT * GH], F32, st)
            DK, DV = GK // GH, GV // GH
            NCH = T // GCH

            @block.tensor
            def _(pe):
                b = job("bvec")
                if turn("bvec") > 1:
                    PE.wait_ge(bank_free("bvec"), turn("bvec") - 1)
                mul(b[0:NH, 0:384], RELB[:, :], con("onehot", BUCKETS), True, True).then_inc(bank_ready("bvec"), 1)
                b = job("post")
                if turn("post") > 1:
                    PE.wait_ge(bank_free("post"), turn("post") - 1)
                for k in range(2):
                    last = tr(b[:, k * 16:(k + 1) * 16], CPOS[:, k, :], ident[0:CB // 2, 0:CB // 2])
                last.then_inc(bank_ready("post"), 1)
                b = job("cwt")
                if turn("cwt") > 1:
                    PE.wait_ge(bank_free("cwt"), turn("cwt") - 1)
                for k in range(2):
                    last = tr(b[:, k * 32:k * 32 + CW], CONVW[:, k * P:(k + 1) * P], ident[0:CW, 0:CW])
                last.then_inc(bank_ready("cwt"), 1)
                pe_turn(PE, "xt", Y, "h_ready")
                pe.wait_ge(bank_free("xt00"), turn("xt00"))
                pe.wait_ge(bank_free("xt01"), turn("xt01"))
                pe.wait_ge(bank_free("xt10"), turn("xt10"))
                pe.wait_ge(bank_free("xt11"), turn("xt11"))
                pe.wait_ge(*landed("n_in0"))
                w = slot_of("n_in0")
                for i in range(2):
                    pe_colpair(PE, w, f"nq{i}", XT, [256 * i, 256 * i + 128])
                weight_read("n_in0", "nq1")
                pe.wait_ge(*landed("n_in1"))
                w = slot_of("n_in1")
                pe_colpair(PE, w, "ck", XT, [0, 128])
                pe_colpair(PE, w, "ks0", XT, [256])
                for tt in range(TT):
                    pe_rows(PE, w, f"vs0{tt}", XT, tt, 384, 128)
                weight_read("n_in1", "vs01")
                pe.wait_ge(*landed("n_in2"))
                w = slot_of("n_in2")
                pe_colpair(PE, w, "ks1", XT, [0])
                for tt in range(TT):
                    pe_rows(PE, w, f"vs1{tt}", XT, tt, 128, 128 + 24)
                weight_read("n_in2", "vs11")
                pe.wait_ge(*landed("n_in3"))
                w = slot_of("n_in3")
                pe_colpair(PE, w, "ca", XT, [0, 128])
                pe_colpair(PE, w, "cg", XT, [256, 384])
                weight_read("n_in3", "cg")
                pe.wait_ge(*landed("n_in4"))
                w = slot_of("n_in4")
                pe_colpair(PE, w, "gqk", XT, [0, 128])
                for tt in range(TT):
                    pe_rows(PE, w, f"gv{tt}", XT, tt, 256, 256)
                weight_read("n_in4", "gv1")
                pe.wait_ge(*landed("n_in5"))
                w = slot_of("n_in5")
                pe_colpair(PE, w, "ga", XT, [0], GR)
                for tt in range(TT):
                    pe_rows(PE, w, f"gr{tt}", XT, tt, GR, 256)
                weight_read("n_in5", "gr1")
                pe.wait_ge(bank_free("ga"), turn("ga"))
                for tt in range(TT):
                    b = job(f"la{tt}")
                    if turn(f"la{tt}") > 1:
                        PE.wait_ge(bank_free(f"la{tt}"), turn(f"la{tt}") - 1)
                    mul(b[:, 0:GK], GAT[:, tt * P:(tt + 1) * P], WAL[:, :], True, True).then_inc(bank_ready(f"la{tt}"), 1)
                def hidden(k):
                    pe.wait_ge(*landed(f"w1{'kv'[k]}"))
                    w = slot_of(f"w1{'kv'[k]}")
                    pe.wait_ge(*nth("blocks_ready", 4 * (k + 1)))
                    b = job(f"hid{k}")
                    if turn(f"hid{k}") > 1:
                        PE.wait_ge(bank_free(f"hid{k}"), turn(f"hid{k}") - 1)
                    for t2 in range(2):
                        for j in range(CB // 2):
                            last = mul(b[:, t2 * 32:t2 * 32 + NKV * NCMP], w[:, j, t2 * P:(t2 + 1) * P], FLT[:, k, j, :], j == 0, j == 15)
                    last.then_inc(bank_ready(f"hid{k}"), 1)
                    weight_read(f"w1{'kv'[k]}", f"hid{k}")

                hidden(0)
                pe.wait_ge(*nth("decay_ready", 1))
                b = job("gb")
                if turn("gb") > 1:
                    PE.wait_ge(bank_free("gb"), turn("gb") - 1)
                for tt in range(TT):
                    last = mul(b[:, tt * P:(tt + 1) * P], LA[:, tt, :], con("tri"), True, True)
                last.then_inc(bank_ready("gb"), 1)
                pe.wait_ge(*nth("conv_ready", 1))
                b = job("cvt")
                if turn("cvt") > 1:
                    PE.wait_ge(bank_free("cvt"), turn("cvt") - 1)
                for tt in range(TT):
                    for c in range(2):
                        last = tr(b[:, (2 * tt + c) * P:(2 * tt + c + 1) * P], CACC[:, c, tt * P:(tt + 1) * P], ident)
                last.then_inc(bank_ready("cvt"), 1)
                pe.wait_ge(*nth("k_decayed", 1))
                b = job("kdt")
                if turn("kdt") > 1:
                    PE.wait_ge(bank_free("kdt"), turn("kdt") - 1)
                for tt in range(TT):
                    last = tr(b[:, tt * P:(tt + 1) * P], KDC[:, tt * P:(tt + 1) * P], ident)
                last.then_inc(bank_ready("kdt"), 1)
                pe.wait_ge(*nth("q_spread", 1))
                for tt in range(TT):
                    b = job(f"at{tt}")
                    if turn(f"at{tt}") > 1:
                        PE.wait_ge(bank_free(f"at{tt}"), turn(f"at{tt}") - 1)
                    mul(b[:, :], KG[:, tt * P:(tt + 1) * P], QBD[:, tt, :, :], True, True).then_inc(bank_ready(f"at{tt}"), 1)
                pe.wait_ge(bank_free("kdt"), turn("kdt"))
                pe.wait_ge(bank_free("gv0"), turn("gv0"))
                pe.wait_ge(bank_free("gv1"), turn("gv1"))
                for c in range(NCH - 1):
                    r = slice(GCH * (c % 2), GCH * (c % 2) + GCH)
                    b = job(f"sd{c}")
                    if turn(f"sd{c}") > 1:
                        PE.wait_ge(bank_free(f"sd{c}"), turn(f"sd{c}") - 1)
                    mul(b[:, 0:GV], KDT[r, c // 2, :], GVS[r, c // 2, :], True, True).then_inc(bank_ready(f"sd{c}"), 1)
                hidden(1)
                for tt in range(TT):
                    pe.wait_ge(bank_free(f"at{tt}"), turn(f"at{tt}"))
                    pe.wait_ge(*nth("state_ready", 2 * tt + 1))
                    b = job(f"go{tt}")
                    if turn(f"go{tt}") > 1:
                        PE.wait_ge(bank_free(f"go{tt}"), turn(f"go{tt}") - 1)
                    for h in range(GH):
                        mul(b[:, h * DV:(h + 1) * DV], AM[:, tt, h, :], GVS[:, tt, h * DV:(h + 1) * DV], h == 0, False)
                    for c in range(2 * tt, 2 * tt + 2):
                        if c:
                            r = GCH * (c % 2)
                            last = mul(b[r:r + GCH, 0:GV], QG[:, c * GCH:(c + 1) * GCH], STB[:, c - 1, :], False, True)
                    last.then_inc(bank_ready(f"go{tt}"), 1)
                pe.wait_ge(bank_free("hid0"), turn("hid0"))
                pe.wait_ge(bank_free("hid1"), turn("hid1"))
                b = job("kcmp")
                if turn("kcmp") > 1:
                    PE.wait_ge(bank_free("kcmp"), turn("kcmp") - 1)
                for t2 in range(2):
                    last = mul(b[0:HD, 0:NKV * NCMP], W2[:, 0, t2, :], HID[:, 0, t2, :], t2 == 0, t2 == 1)
                last.then_inc(bank_ready("kcmp"), 1)
                b = job("vcmp")
                if turn("vcmp") > 1:
                    PE.wait_ge(bank_free("vcmp"), turn("vcmp") - 1)
                for g in range(NKV):
                    for t2 in range(2):
                        last = mul(b[0:NCMP, g * HD:(g + 1) * HD], HID[:, 1, t2, g * NCMP:(g + 1) * NCMP], W2[:, 1, t2, :], t2 == 0, t2 == 1)
                last.then_inc(bank_ready("vcmp"), 1)

            @block.scalar
            def _(act):
                act_squares(X, Y, "mix_sq", D)
                A.wait_ge(bank_ready("post"), turn("post"))
                b = result("post")
                copy(A, POST[:, :, :], b[:, 0:32].rearrange("p (k j) -> p k j", k=2)).then_inc(bank_free("post"), 1)
                A.wait_ge(bank_ready("cwt"), turn("cwt"))
                b = result("cwt")
                copy(A, CWT[:, :, 0:CW], b[:, 0:64].rearrange("p (k j) -> p k j", k=2)[:, :, 0:CW]).then_inc(bank_free("cwt"), 1)
                take_turn(A, "xt", XT, [(0, 0), (1, 0)])
                for i in range(2):
                    A.wait_ge(bank_ready(f"nq{i}"), turn(f"nq{i}"))
                    b = result(f"nq{i}")
                    copy(A, QT[:, 2 * i:2 * i + 2, :], pair(b), HD ** -0.5).then_inc(bank_free(f"nq{i}"), 1)

                def spread(dst, src, name):
                    for head in range(NKV):
                        for half in range(2):
                            ins = copy(A, dst(slice(HD * half, HD * half + HD), head), src(slice(HD * head, HD * head + HD)))
                            if (head, half) == (1, 1):
                                ins.then_inc(bank_free(name), 1)
                            else:
                                ins.then_inc(*tick("act_step"))

                A.wait_ge(bank_ready("ck"), turn("ck"))
                b = result("ck")
                spread(lambda r, g: CT[r, :, g, :], lambda r: b[r, 0:2 * T].rearrange("p (k t) -> p k t", k=2), "ck")
                for s in range(2):
                    A.wait_ge(bank_ready(f"ks{s}"), turn(f"ks{s}"))
                    b = result(f"ks{s}")
                    spread(lambda r, g: KS[r, s, g, :], lambda r: b[r, 0:T], f"ks{s}")
                    for tt in range(TT):
                        A.wait_ge(bank_ready(f"vs{s}{tt}"), turn(f"vs{s}{tt}"))
                        b = result(f"vs{s}{tt}")
                        if s == 1:
                            A.activation(NG[:, tt, :, :].rearrange("p h n -> p (h n)"), b[:, 128:152], ACT.Sigmoid).then_inc(*tick("act_step"))
                            A.wait_ge(*now("act_step"))
                        copy(A, VS[:, s, tt, :], b[:, 0:128]).then_inc(bank_free(f"vs{s}{tt}"), 1)
                A.wait_ge(bank_ready("cg"), turn("cg"))
                b = result("cg")
                A.activation(SGC[:, :, :], pair(b), ACT.Sigmoid).then_inc(bank_free("cg"), 1)
                A.wait_ge(bank_ready("gqk"), turn("gqk"))
                b = result("gqk")
                copy(A, QG[:, :], b[:, 0:T], DK ** -0.5).then_inc(*tick("act_step"))
                copy(A, KG[:, :], b[:, T:2 * T]).then_inc(bank_free("gqk"), 1)
                for tt in range(TT):
                    A.wait_ge(bank_ready(f"gv{tt}"), turn(f"gv{tt}"))
                    b = result(f"gv{tt}")
                    copy(A, GVS[:, tt, :], b[:, 0:GV]).then_inc(bank_free(f"gv{tt}"), 1)
                A.wait_ge(bank_ready("ga"), turn("ga"))
                b = result("ga")
                copy(A, GAT[:, :], b[0:GR, 0:T]).then_inc(bank_free("ga"), 1)
                for tt in range(TT):
                    A.wait_ge(bank_ready(f"gr{tt}"), turn(f"gr{tt}"))
                    b = result(f"gr{tt}")
                    A.activation(GRS[:, tt, :], b[:, 0:GV], ACT.Silu).then_inc(bank_free(f"gr{tt}"), 1)
                logsig_steps(LA[:, :, :], "decay")
                A.wait_ge(bank_ready("gb"), turn("gb"))
                b = result("gb")
                copy(A, BS[:, :], b[:, 0:T]).then_inc(*tick("decay_sums"))
                A.wait_ge(*now("decay_sums"))
                A.activation(E1[:, :], b[:, 0:T], ACT.Exp).then_inc(*tick("act_step"))
                A.activation(E2[:, :], b[:, 0:T], ACT.Exp, scale=-1.0).then_inc(*tick("act_step"))
                for c in range(NCH):
                    s = slice(c * GCH, (c + 1) * GCH)
                    ins = A.activation(E3[:, s], b[:, s], ACT.Exp, scale=-1.0, bias=BS[:, (c + 1) * GCH - 1:(c + 1) * GCH])
                    if c < NCH - 1:
                        ins.then_inc(*tick("act_step"))
                    else:
                        ins.then_inc(bank_free("gb"), 1)
                A.wait_ge(bank_ready("kdt"), turn("kdt"))
                b = result("kdt")
                copy(A, KDT[:, :, :], b[:, 0:T].rearrange("p (t d) -> p t d", t=TT)).then_inc(bank_free("kdt"), 1)
                for k in range(2):
                    A.wait_ge(bank_ready(f"hid{k}"), turn(f"hid{k}"))
                    b = result(f"hid{k}")
                    for t2 in range(2):
                        ins = A.activation(HID[:, k, t2, :], b[:, t2 * 32:t2 * 32 + NKV * NCMP], ACT.Silu, bias=B1[:, k, t2:t2 + 1])
                        if t2 == 0:
                            ins.then_inc(*tick("act_step"))
                        else:
                            ins.then_inc(bank_free(f"hid{k}"), 1)
                A.wait_ge(*nth("conv_normed", TT))
                for tt in range(TT):
                    A.activation(Y[:, tt, 512:512 + CC], CV2[:, tt, :], ACT.Silu).then_inc(*tick("act_step"))
                    A.wait_ge(*now("act_step"))
                A.wait_ge(bank_ready("kcmp"), turn("kcmp"))
                b = result("kcmp")
                copy(A, KCMP[0:HD, :], b[0:HD, 0:NKV * NCMP]).then_inc(*tick("act_step"))
                copy(A, KCMP[HD:P, :], b[0:HD, 0:NKV * NCMP]).then_inc(bank_free("kcmp"), 1)
                A.wait_ge(bank_ready("vcmp"), turn("vcmp"))
                b = result("vcmp")
                copy(A, VCMP[:, :, :], b[0:NCMP, 0:NKV * HD].rearrange("p (g d) -> p g d", g=NKV)).then_inc(bank_free("vcmp"), 1)
                A.wait_ge(bank_free("kcmp"), turn("kcmp"))
                A.wait_ge(bank_free("vcmp"), turn("vcmp"))

            @block.vector
            def _(dve):
                params_here(dve)
                for c in range(2):
                    V.memset(CH[:, c, 0:CW - 1], 0.0).then_inc(*tick("dve_step"))
                dve_rms("mix", rows[0][:, 2, :])
                V.wait_ge(bank_ready("bvec"), turn("bvec"))
                b = result("bvec")
                V.tensor_tensor(BVEC[:, :], b[0:NH, 0:384], con("future", NH), ALU.add).then_inc(bank_free("bvec"), 1)
                take_turn(V, "xt", XT, [(0, 1), (1, 1)])
                V.wait_ge(bank_free("ck"), turn("ck"))
                V.wait_ge(bank_free("post"), turn("post"))
                for k in range(2):
                    for g in range(NKV):
                        for half in range(2):
                            r = slice(HD * half, HD * half + HD)
                            row = CT[r, k, g, half:half + 1]
                            blocks = bass.AP(row.tensor, row.offset, [list(row.ap[0]), [2, CB // 2], [CS, NCMP]])
                            pos = POST[r, k, :].unsqueeze(2).broadcast_to([HD, CB // 2, NCMP])
                            V.tensor_tensor(FLT[r, k, :, g * NCMP:(g + 1) * NCMP], blocks, pos, ALU.add).then_inc(*tick("blocks_ready"))
                            V.wait_ge(*now("blocks_ready"))
                V.wait_ge(bank_ready("ca"), turn("ca"))
                b = result("ca")
                V.wait_ge(bank_free("cg"), turn("cg"))
                V.wait_ge(bank_free("cwt"), turn("cwt"))
                V.tensor_tensor(CH[:, :, CW - 1:], pair(b), SGC[:, :, :], ALU.mult).then_inc(bank_free("ca"), 1)
                V.wait_ge(bank_free("ca"), turn("ca"))
                for j in range(CW):
                    for c in range(2):
                        x = CH[:, c, j:j + T]
                        if j == 0:
                            ins = V.tensor_scalar(CACC[:, c, :], x, CWT[:, c, 0:1], CONVB[:, c:c + 1], ALU.mult, ALU.add)
                        else:
                            dve.wait_ge(S("dve_step"), count["dve_step"] - 1)
                            ins = V.scalar_tensor_tensor(CACC[:, c, :], x, CWT[:, c, j:j + 1], CACC[:, c, :], ALU.mult, ALU.add)
                        if (j, c) == (CW - 1, 1):
                            ins.then_inc(*tick("conv_ready"))
                            V.wait_ge(*now("conv_ready"))
                        else:
                            ins.then_inc(*tick("dve_step"))
                for tt in range(TT):
                    V.wait_ge(bank_ready(f"la{tt}"), turn(f"la{tt}"))
                    b = result(f"la{tt}")
                    V.tensor_tensor(LX[:, tt, :], b[:, 0:GK], small("gla_b_alpha_2"), ALU.add).then_inc(bank_free(f"la{tt}"), 1)
                V.wait_ge(bank_free("la0"), turn("la0"))
                V.wait_ge(bank_free("la1"), turn("la1"))
                V.scalar_tensor_tensor(LA[:, :, :], LX[:, :, :], -1.0, LX[:, :, :], ALU.mult, ALU.max).then_inc(*tick("decay_abs"))
                V.wait_ge(*now("decay_abs"))
                V.wait_ge(*nth("decay_ln", 1))
                V.scalar_tensor_tensor(LA[:, :, :], LX[:, :, :], 0.0, LA[:, :, :], ALU.min, ALU.subtract).then_inc(*tick("dve_step"))
                V.wait_ge(*now("dve_step"))
                V.tensor_scalar(LA[:, :, :], LA[:, :, :], 1.0 / 16.0, None, ALU.mult).then_inc(*tick("decay_ready"))
                V.wait_ge(*now("decay_ready"))
                V.wait_ge(bank_free("gb"), turn("gb"))
                V.wait_ge(bank_free("gqk"), turn("gqk"))
                V.tensor_tensor(KDC[:, :], KG[:, :], E3[:, :], ALU.mult).then_inc(*tick("k_decayed"))
                V.wait_ge(*now("k_decayed"))
                V.tensor_tensor(KG[:, :], KG[:, :], E2[:, :], ALU.mult).then_inc(*tick("dve_step"))
                V.tensor_tensor(QG[:, :], QG[:, :], E1[:, :], ALU.mult).then_inc(*tick("dve_step"))
                V.wait_ge(*now("dve_step"))
                V.wait_ge(*nth("cleared", 3))
                for h in range(GH):
                    r = slice(DK * h, DK * h + DK)
                    ins = V.tensor_copy(QBD[r, :, h, :], QG[r, :].rearrange("p (t q) -> p t q", t=TT))
                    if h < GH - 1:
                        ins.then_inc(*tick("dve_step"))
                    else:
                        ins.then_inc(*tick("q_spread"))
                        V.wait_ge(*now("q_spread"))
                V.wait_ge(bank_ready("cvt"), turn("cvt"))
                b = result("cvt")
                copy(V, CV[:, :, :], b[:, :].rearrange("p (t c) -> p t c", t=TT)).then_inc(bank_free("cvt"), 1)
                V.wait_ge(bank_free("cvt"), turn("cvt"))
                dve_layer_norm(CV, CV2, small("conv_ln_g_2"), small("conv_ln_b_2"), EPS2, "conv", "conv_normed")
                mask = con("tri").bitcast(I32).unsqueeze(1).broadcast_to([P, GH, P])
                for tt in range(TT):
                    V.wait_ge(bank_ready(f"at{tt}"), turn(f"at{tt}"))
                    b = result(f"at{tt}")
                    V.copy_predicated(AM[:, tt, :, :], mask, b[:, :].rearrange("p (h t) -> p h t", h=GH)).then_inc(bank_free(f"at{tt}"), 1)
                for c in range(NCH - 1):
                    V.wait_ge(bank_ready(f"sd{c}"), turn(f"sd{c}"))
                    b = result(f"sd{c}")
                    end = (c + 1) * GCH - 1
                    for h in range(GH):
                        r, s = slice(DK * h, DK * h + DK), slice(h * DV, (h + 1) * DV)
                        if c == 0:
                            ins = V.tensor_copy(STB[r, 0, s], b[r, s])
                        else:
                            ins = V.scalar_tensor_tensor(STB[r, c, s], STB[r, c - 1, s], E1[r, end:end + 1], b[r, s], ALU.mult, ALU.add)
                        if h == GH - 1:
                            ins.then_inc(bank_free(f"sd{c}"), 1)
                            V.wait_ge(bank_free(f"sd{c}"), turn(f"sd{c}"))
                        else:
                            ins.then_inc(*tick("dve_step"))
                    V.memset(stat[:, 48 + c:49 + c], 0.0).then_inc(*tick("state_ready"))
                    V.wait_ge(*now("state_ready"))
                for tt in range(TT):
                    V.wait_ge(bank_ready(f"go{tt}"), turn(f"go{tt}"))
                    b = result(f"go{tt}")
                    copy(V, GO[:, tt, :], b[:, 0:GV]).then_inc(bank_free(f"go{tt}"), 1)
                V.wait_ge(bank_free("go0"), turn("go0"))
                V.wait_ge(bank_free("go1"), turn("go1"))
                V.tensor_tensor(GSQ[:, :, :], GO[:, :, :], GO[:, :, :], ALU.mult).then_inc(*tick("dve_step"))
                V.wait_ge(*now("dve_step"))
                heads = lambda x: x[:, :, :].rearrange("p t (h v) -> p (t h) v", v=DV)
                V.tensor_reduce(GST[:, :], heads(GSQ), AX.X, ALU.add).then_inc(*tick("dve_step"))
                V.wait_ge(*now("dve_step"))
                V.tensor_scalar(GST[:, :], GST[:, :], 1.0 / DV, EPS2, ALU.mult, ALU.add).then_inc(*tick("gla_var"))
                V.wait_ge(*now("gla_var"))
                V.wait_ge(*nth("gla_rstd", 1))
                V.tensor_tensor(heads(GO), heads(GO), GST[:, :].unsqueeze(2).broadcast_to([P, TT * GH, DV]), ALU.mult).then_inc(*tick("dve_step"))
                V.wait_ge(*now("dve_step"))
                V.tensor_tensor(GO[:, :, :], GO[:, :, :], small("gla_norm_g_2").unsqueeze(1).broadcast_to([P, TT, GV]), ALU.mult).then_inc(*tick("dve_step"))
                V.wait_ge(*now("dve_step"))
                V.wait_ge(bank_free("gr0"), turn("gr0"))
                V.wait_ge(bank_free("gr1"), turn("gr1"))
                V.tensor_tensor(Y[:, :, 768:1024], GO[:, :, :], GRS[:, :, :], ALU.mult).then_inc(*tick("dve_step"))
                V.wait_ge(*now("dve_step"))
                V.wait_ge(*nth("bias_here", 1))
                V.tensor_copy(BIAS[:, :, 384:384 + NCMP], BIAS[:, :, CB - 1:T:CS]).then_inc(*tick("dve_step"))
                V.tensor_copy(BIAS[:, :, 384 + NCMP:STRIP], BIAS[:, :, P + CB - 1:T:CS]).then_inc(*tick("dve_step"))
                V.wait_ge(*now("dve_step"))
                at, _ = cwhere["seen"]
                for tt in range(TT):
                    V.tensor_scalar(NG[:, tt, :, 0], NG[:, tt, :, 0], CN[:, at + tt:at + tt + 1], None, ALU.mult).then_inc(*tick("dve_step"))
                    V.wait_ge(*now("dve_step"))

            @block.gpsimd
            def _(pool):
                pool_rms("mix")
                load_rows(0, [a["ffn_norm_g_2"][0]])
                load_rows(1, [a["ple_norm_g_2"][0], a["final_norm_g_2"]])
                for t in (QBD, AM, STB):
                    G.memset(t[:], 0.0).then_inc(*tick("cleared"))
                    G.wait_ge(*now("cleared"))
                pool.wait_ge(bank_free("bvec"), turn("bvec"))
                n = BVEC.shape[1]
                pool.dma_start(scratch, BVEC[:, :].unsqueeze(1).broadcast_to([NH, P, n])).then_inc(S("bias_out"), 16)
                pool.wait_ge(S("bias_out"), 16)
                t1 = bass.AP(scratch.tensor, P - 1, [[n - 1, P], [P * n, NH], [1, T]])
                t0 = bass.AP(scratch.tensor, 2 * P - 1, [[n - 1, P], [P * n, NH], [1, P]])
                pool.dma_start(BIAS[:, :, 0:T], t1).then_inc(S("bias_in"), 16)
                pool.dma_start(BIAS[:, :, T:T + P], t0).then_inc(S("bias_in"), 16)
                pool.wait_ge(S("bias_in"), 32)
                G.memset(stat[:, 56:57], 0.0).then_inc(*tick("bias_here"))
                G.wait_ge(*now("bias_here"))
                pool_layer_norm("conv")
                pool_power("gla_var", 1, "gla_rstd", GST[:, :])

        def nsa_attention(block, st, QT, KS, VS, NG, KCMP, VCMP, BIAS):
            N0 = 7
            WIN = 384 + NCMP + N0
            groups = [(0, T), (T, P), (384, NCMP), (384 + NCMP, N0), (WIN, T), (WIN + T, P)]
            branch = [1, 1, 0, 0, 2, 2]
            PR = [sb(f"NP{i}", [P, WIN + 384], F32, st) for i in range(2)]
            PTS = [sb(f"NPT{i}", [P, 2, 384], F32, st) for i in range(2)]
            PTC = [sb(f"NPC{i}", [NCMP, 2, P], F32, st) for i in range(2)]
            MX = sb("NMX", [P, NH, 6], F32, st)
            SM = sb("NSM", [P, NH, 6], F32, st)
            FC = sb("NFC", [P, NH, 6], F32, st)
            G6 = sb("G6", [P, NH, 6], F32, st)
            MIXO = [sb(f"MIXO{i}", [P, 6, HD], F32, st) for i in range(2)]

            @block.tensor
            def _(pe):
                for i in range(NH + 2):
                    if i < NH:
                        h, g = i, i // (NH // NKV)
                        r = slice(HD * (h % 2), HD * (h % 2) + HD)
                        q = QT[r, h // 2, :]
                        b = job(f"s{h}")
                        if turn(f"s{h}") > 1:
                            PE.wait_ge(bank_free(f"s{h}"), turn(f"s{h}") - 1)
                        mul(b[:, 0:T], q[:, P:T], KS[r, 0, g, :], True, True)
                        mul(b[:, T:T + P], q[:, 0:P], KS[r, 0, g, 0:P], True, True)
                        mul(b[:, 384:384 + NCMP], q[:, P:T], KCMP[r, g * NCMP:(g + 1) * NCMP], True, True)
                        mul(b[:, 384 + NCMP:WIN], q[:, 0:P], KCMP[r, g * NCMP:g * NCMP + N0], True, True).then_inc(bank_ready(f"s{h}"), 1)
                        b = job(f"w{h}")
                        if turn(f"w{h}") > 1:
                            PE.wait_ge(bank_free(f"w{h}"), turn(f"w{h}") - 1)
                        mul(b[:, 0:T], q[:, P:T], KS[r, 1, g, :], True, True)
                        mul(b[:, T:T + P], q[:, 0:P], KS[r, 1, g, 0:P], True, True).then_inc(bank_ready(f"w{h}"), 1)
                    if 1 <= i <= NH:
                        h = i - 1
                        pe.wait_ge(*nth("probs_ready", h + 1))
                        p = PR[h % 2]
                        b = job(f"ts{h}")
                        if turn(f"ts{h}") > 1:
                            PE.wait_ge(bank_free(f"ts{h}"), turn(f"ts{h}") - 1)
                        for j in range(3):
                            tr(b[:, j * P:(j + 1) * P], p[:, j * P:(j + 1) * P], ident)
                        tr(b[0:NCMP, 384:512], p[:, 384:384 + NCMP], ident).then_inc(bank_ready(f"ts{h}"), 1)
                        b = job(f"tw{h}")
                        if turn(f"tw{h}") > 1:
                            PE.wait_ge(bank_free(f"tw{h}"), turn(f"tw{h}") - 1)
                        for j in range(3):
                            tr(b[:, j * P:(j + 1) * P], p[:, WIN + j * P:WIN + (j + 1) * P], ident)
                        tr(b[0:N0, 384:512], p[:, 384 + NCMP:WIN], ident).then_inc(bank_ready(f"tw{h}"), 1)
                    if i >= 2:
                        h = i - 2
                        g = h // (NH // NKV)
                        v = slice(g * HD, (g + 1) * HD)
                        pe.wait_ge(bank_free(f"ts{h}"), turn(f"ts{h}"))
                        pe.wait_ge(bank_free(f"tw{h}"), turn(f"tw{h}"))
                        b = job(f"o{h}")
                        if turn(f"o{h}") > 1:
                            PE.wait_ge(bank_free(f"o{h}"), turn(f"o{h}") - 1)
                        o = lambda n: b[:, n * HD:(n + 1) * HD]
                        for s, n in ((0, 0), (1, 4)):
                            mul(o(n), PTS[h % 2][:, s, 0:P], VS[:, s, 0, v], True, False)
                            mul(o(n), PTS[h % 2][:, s, P:2 * P], VS[:, s, 1, v], False, True)
                            mul(o(n + 1), PTS[h % 2][:, s, 2 * P:3 * P], VS[:, s, 0, v], True, True)
                        mul(o(2), PTC[h % 2][:, 0, :], VCMP[:, g, :], True, True)
                        mul(o(3), PTC[h % 2][0:N0, 1, :], VCMP[0:N0, g, :], True, True).then_inc(bank_ready(f"o{h}"), 1)

            @block.scalar
            def _(act):
                for i in range(NH + 1):
                    if i < NH:
                        h = i
                        A.wait_ge(*nth("max_ready", h + 1))
                        for n, (c, w) in enumerate(groups):
                            ins = A.activation(PR[h % 2][:, c:c + w], PR[h % 2][:, c:c + w], ACT.Exp, bias=MX[:, h, n:n + 1], accum_out=SM[:, h, n:n + 1])
                            if n < 5:
                                ins.then_inc(*tick("act_step"))
                            else:
                                ins.then_inc(*tick("probs_ready"))
                                A.wait_ge(*now("probs_ready"))
                    if i >= 1:
                        h = i - 1
                        if h >= 2:
                            A.wait_ge(bank_ready(f"o{h - 2}"), turn(f"o{h - 2}"))
                        A.wait_ge(bank_ready(f"ts{h}"), turn(f"ts{h}"))
                        b = result(f"ts{h}")
                        copy(A, PTS[h % 2][:, 0, :], b[:, 0:384]).then_inc(*tick("act_step"))
                        copy(A, PTC[h % 2][:, 0, :], b[0:NCMP, 384:512]).then_inc(bank_free(f"ts{h}"), 1)

            @block.vector
            def _(dve):
                for n in range(6):
                    V.tensor_copy(G6[:, :, n], NG[:, 1 - n % 2, :, branch[n]]).then_inc(*tick("dve_step"))
                for i in range(NH + 2):
                    if i < NH:
                        h = i
                        if h >= 2:
                            V.wait_ge(bank_ready(f"tw{h - 2}"), turn(f"tw{h - 2}"))
                        for n, (c, w) in enumerate(groups):
                            name = f"s{h}" if n < 4 else f"w{h}"
                            if n in (0, 4):
                                V.wait_ge(bank_ready(name), turn(name))
                                b = result(name)
                            bc = c if n < 4 else c - WIN
                            ins = V.tensor_tensor_reduce(out=PR[h % 2][:, c:c + w], in0=b[:, bc:bc + w], in1=BIAS[:, h, bc:bc + w], scale=1.0,
                                                         scalar=FLOOR, op0=ALU.add, op1=ALU.max, accum_out=MX[:, h, n:n + 1])
                            if n in (3, 5):
                                ins.then_inc(bank_free(name), 1)
                            else:
                                ins.then_inc(*tick("dve_step"))
                        V.wait_ge(bank_free(f"s{h}"), turn(f"s{h}"))
                        V.wait_ge(bank_free(f"w{h}"), turn(f"w{h}"))
                        V.tensor_scalar(MX[:, h, :], MX[:, h, :], -1.0, None, ALU.mult).then_inc(*tick("max_ready"))
                        V.wait_ge(*now("max_ready"))
                    if 1 <= i <= NH:
                        h = i - 1
                        if h >= 2:
                            V.wait_ge(bank_ready(f"o{h - 2}"), turn(f"o{h - 2}"))
                        V.wait_ge(bank_ready(f"tw{h}"), turn(f"tw{h}"))
                        b = result(f"tw{h}")
                        copy(V, PTS[h % 2][:, 1, :], b[:, 0:384]).then_inc(*tick("dve_step"))
                        copy(V, PTC[h % 2][0:N0, 1, :], b[0:N0, 384:512]).then_inc(bank_free(f"tw{h}"), 1)
                        V.wait_ge(*nth("probs_ready", h + 1))
                        V.reciprocal(FC[:, h, :], SM[:, h, :]).then_inc(*tick("dve_step"))
                        V.wait_ge(*now("dve_step"))
                        V.tensor_tensor(FC[:, h, :], FC[:, h, :], G6[:, h, :], ALU.mult).then_inc(*tick("dve_step"))
                        V.wait_ge(*now("dve_step"))
                    if i >= 2:
                        h = i - 2
                        V.wait_ge(bank_ready(f"o{h}"), turn(f"o{h}"))
                        b = result(f"o{h}")
                        m = MIXO[h % 2]
                        V.tensor_tensor(m[:, :, :], b[:, 0:384].rearrange("p (n d) -> p n d", n=6),
                                             FC[:, h, :].unsqueeze(2).broadcast_to([P, 6, HD]), ALU.mult).then_inc(bank_free(f"o{h}"), 1)
                        V.wait_ge(bank_free(f"o{h}"), turn(f"o{h}"))
                        for tt in range(TT):
                            V.tensor_reduce(Y[:, tt, h * HD:(h + 1) * HD], m[:, 1 - tt::2, :].rearrange("p n d -> p d n"), AX.X, ALU.add).then_inc(*tick("dve_step"))
                        V.wait_ge(*now("dve_step"))

        def mixers_out(block, st):
            @block.tensor
            def _(pe):
                pe_turn(PE, "yt", Y, None)
                pe.wait_ge(bank_free("yt00"), turn("yt00"))
                pe.wait_ge(bank_free("yt01"), turn("yt01"))
                pe.wait_ge(bank_free("yt10"), turn("yt10"))
                pe.wait_ge(bank_free("yt11"), turn("yt11"))
                for cb in range(2):
                    pe.wait_ge(*landed(f"n_out{cb}"))
                    w = slot_of(f"n_out{cb}")
                    for tt in range(TT):
                        pe_rows(PE, w, f"o{cb}{tt}", XT, tt, 0, 512)
                    weight_read(f"n_out{cb}", f"o{cb}1")

            block.scalar(lambda act: take_turn(A, "yt", XT, [(0, 0), (1, 0)]))

            @block.vector
            def _(dve):
                take_turn(V, "yt", XT, [(0, 1), (1, 1)])
                for cb in range(2):
                    for tt in range(TT):
                        s = slice(cb * 512, cb * 512 + 512)
                        V.wait_ge(bank_ready(f"o{cb}{tt}"), turn(f"o{cb}{tt}"))
                        b = result(f"o{cb}{tt}")
                        V.tensor_tensor(X[:, tt, s], X[:, tt, s], b[:, :], ALU.add).then_inc(bank_free(f"o{cb}{tt}"), 1)
                V.wait_ge(bank_free("o00"), turn("o00"))
                V.wait_ge(bank_free("o01"), turn("o01"))
                V.wait_ge(bank_free("o10"), turn("o10"))
                V.wait_ge(bank_free("o11"), turn("o11"))

        def ffn(block, st):
            FT = sb("FT", [P, FF // P, T], F32, st)
            SG = [sb(f"SGF{i}", [P, T], F32, st) for i in range(2)]

            @block.tensor
            def _(pe):
                pe_turn(PE, "xt", Y, "h_ready")
                pe.wait_ge(bank_free("xt00"), turn("xt00"))
                pe.wait_ge(bank_free("xt01"), turn("xt01"))
                pe.wait_ge(bank_free("xt10"), turn("xt10"))
                pe.wait_ge(bank_free("xt11"), turn("xt11"))
                for e in range(len(ffe) - 1):
                    pe.wait_ge(*landed(f"ffg{e}"))
                    pe.wait_ge(*landed(f"ffu{e}"))
                    wg, wu = slot_of(f"ffg{e}"), slot_of(f"ffu{e}")
                    for i in range((ffe[e + 1] - ffe[e]) // P):
                        f = 4 * e + i
                        b = job(f"gu{f}")
                        if turn(f"gu{f}") > 1:
                            PE.wait_ge(bank_free(f"gu{f}"), turn(f"gu{f}") - 1)
                        for s, w in enumerate((wg, wu)):
                            for k in range(KD):
                                last = mul(b[:, s * T:(s + 1) * T], w[:, k, i * P:(i + 1) * P], XT[:, k, :], k == 0, k == KD - 1)
                        last.then_inc(bank_ready(f"gu{f}"), 1)
                    weight_read(f"ffg{e}", f"gu{f}")
                    weight_read(f"ffu{e}", f"gu{f}")
                for cb in range(2):
                    bs = [job(f"d{cb}{tt}") for tt in range(TT)]
                    for tt in range(TT):
                        pe.wait_ge(bank_free(f"d{cb}{tt}"), turn(f"d{cb}{tt}") - 1)
                    for e, (k0, k1) in enumerate(((0, 8), (8, 16), (16, 22))):
                        pe.wait_ge(*landed(f"ffd{cb}{e}"))
                        w = slot_of(f"ffd{cb}{e}")
                        for tt in range(TT):
                            for k in range(k0, k1):
                                if cb == 0 and tt == 0:
                                    pe.wait_ge(bank_free(f"gu{k}"), turn(f"gu{k}"))
                                last = mul(bs[tt][:, :], FT[:, k, tt * P:(tt + 1) * P], w[:, k - k0, :], k == 0, k == FF // P - 1)
                            if k1 == FF // P:
                                last.then_inc(bank_ready(f"d{cb}{tt}"), 1)
                        weight_read(f"ffd{cb}{e}", f"d{cb}1")

            @block.scalar
            def _(act):
                act_squares(X, Y, "ffn_sq", D)
                take_turn(A, "xt", XT, [(0, 0), (1, 0)])
                for f in range(FF // P):
                    A.wait_ge(bank_ready(f"gu{f}"), turn(f"gu{f}"))
                    b = result(f"gu{f}")
                    if f >= 2:
                        A.wait_ge(bank_free(f"gu{f - 2}"), turn(f"gu{f - 2}"))
                    A.activation(SG[f % 2][:, :], b[:, 0:T], ACT.Silu).then_inc(*tick("silu_done"))
                    A.wait_ge(*now("silu_done"))

            @block.vector
            def _(dve):
                rows_here(0, 1)
                dve_rms("ffn", rows[0][:, 0, :])
                take_turn(V, "xt", XT, [(0, 1), (1, 1)])
                for f in range(FF // P):
                    V.wait_ge(*nth("silu_done", f + 1))
                    V.wait_ge(bank_ready(f"gu{f}"), turn(f"gu{f}"))
                    b = result(f"gu{f}")
                    V.tensor_tensor(FT[:, f, :], b[:, T:2 * T], SG[f % 2][:, :], ALU.mult).then_inc(bank_free(f"gu{f}"), 1)
                for cb in range(2):
                    for tt in range(TT):
                        s = slice(cb * 512, cb * 512 + 512)
                        V.wait_ge(bank_ready(f"d{cb}{tt}"), turn(f"d{cb}{tt}"))
                        b = result(f"d{cb}{tt}")
                        V.tensor_tensor(X[:, tt, s], X[:, tt, s], b[:, :], ALU.add).then_inc(bank_free(f"d{cb}{tt}"), 1)
                V.wait_ge(bank_free("d00"), turn("d00"))
                V.wait_ge(bank_free("d01"), turn("d01"))
                V.wait_ge(bank_free("d10"), turn("d10"))
                V.wait_ge(bank_free("d11"), turn("d11"))

            @block.gpsimd
            def _(pool):
                pool_rms("ffn")

        def last(block, st):
            @block.gpsimd
            def _(pool):
                pool_rms("ple")

            def dve_before():
                rows_here(1, 2)
                dve_rms("ple", rows[1][:, 0, :])

            embed(block, st, Y, "ple2_gate", "ple2_proj", 2,
                  before=(lambda: act_squares(X, Y, "ple_sq", D), dve_before))

        def final_norm(block, st):
            block.scalar(lambda act: act_squares(X, Y, "fin_sq", D))
            block.gpsimd(lambda pool: pool_rms("fin"))

            @block.vector
            def _(dve):
                dve_mean_square("fin", D, EPS2)
                for tt in range(TT):
                    V.scalar_tensor_tensor(Y[:, tt, :], X[:, tt, :], stat[:, 12 + tt:13 + tt], rows[1][:, 1, :], ALU.mult, ALU.mult).then_inc(*tick("out_ready"))
                    V.wait_ge(*now("out_ready"))

        block = ctx.enter_context(nc.Block())

        def phase(make, *args, with_pool=False, **kw):
            with ExitStack() as st:
                make(block, st, *args, **kw)
                end_phase(block, with_pool)

        def peers():
            issue_gathers(block)
            with ExitStack() as st:
                peer_route(block, st, 0, BOTH, "0")
                end_phase(block, False)
                phase(weigh, 0)
                phase(peer_done, 1, True)
            with ExitStack() as st:
                KNT = sb("KNT", [P, AH, T], F32, st)
                VM = sb("VM", [P, TT, AH * AV], F32, st)
                KRT = sb("KRT", [ROPE, T], F32, st)
                for tt in range(TT):
                    phase(embed, X, f"ple_gate0{tt}_", f"ple_proj0{tt}", 0, tiles=(tt,))
                    phase(mla, tt, KNT, VM, KRT)
                    phase(weigh, 2 + 2 * tt)
                    phase(peer_route, 1, (tt,), f"1{tt}")
                    phase(peer_done, 3 + 2 * tt, True)
            phase(embed, X, "ple_gate10_", "ple_proj10", 1, tiles=(0,))
            phase(weigh, 6)
            phase(peer_done, 7, False)
            phase(embed, X, "ple_gate11_", "ple_proj11", 1, tiles=(1,), with_pool=True)
            peer_mem.close()

        phase(mlstm, with_pool=True)
        peers()
        nsa()
        phase(ffn, with_pool=True)
        phase(last, with_pool=True)
        phase(final_norm, with_pool=True)
        store_and_load(block)


_INS = [
    "x", "p", "positions", "ln_g", "ln_b", "a_w_in", "a_b_if", "a_hn_g", "a_w_out", "kv_w_down", "kv_norm_g", "kv_w_up",
    "b_w_dq", "b_q_norm_g", "b_w_uq", "b_w_out", "peer_w_q", "peer_sub_keys", "peer_u", "peer_v", "ple_w_proj",
    "ple_w_gate", "p_2", "rel_bias_2", "mix_norm_g_2", "w_in_2", "w_out_2", "cmp_pos_k_2", "cmp_w1_k_2",
    "cmp_b1_k_2", "cmp_w2_k_2", "cmp_pos_v_2", "cmp_w1_v_2", "cmp_b1_v_2", "cmp_w2_v_2", "conv_w_2", "conv_b_2",
    "conv_ln_g_2", "conv_ln_b_2", "gla_w_alpha_2", "gla_b_alpha_2", "gla_norm_g_2", "ffn_norm_g_2",
    "ffn_w_gate_2", "ffn_w_up_2", "ffn_w_down_2", "ple_norm_g_2", "ple_w_gate_2", "ple_w_proj_2", "final_norm_g_2",
]


def kernel(**inputs):
    import concourse.bacc as bacc
    from concourse.bass_utils import run_bass_kernel_spmd

    nc = bacc.Bacc("TRN2", target_bir_lowering=False, num_devices=1)
    arrays, aps = {}, {}
    for name in _INS:
        arr = np.ascontiguousarray(inputs[name])
        arrays[f"in_{name}"] = arr
        aps[name] = nc.dram_tensor(f"in_{name}", arr.shape, mybir.dt.from_np(arr.dtype), kind="ExternalInput").ap()
    table, where = constants()
    arrays["in_constants"] = table
    consts = nc.dram_tensor("in_constants", table.shape, F32, kind="ExternalInput").ap()
    scratch = nc.dram_tensor("bias_rows", (NH, P, 384), F32, kind="Internal").ap()
    out = nc.dram_tensor("out_x", (1, T, D), F32, kind="ExternalOutput").ap()
    build(nc, aps, consts, where, scratch, out)
    done = run_bass_kernel_spmd(nc, [arrays], core_ids=[0])
    return done.results[0]["out_x"]
```
